# Optimizing a Trainium2 kernel written in Bass

```python
import math
import jax, jax.numpy as jnp
from jax import lax
import numpy as np

D_MODEL = 1024
BATCH = 1
SEQ = 256
DEPTH = 1

SB_WIDTH = D_MODEL // 2
SB_HEAD_DIM = 64
SB_HEADS = SB_WIDTH // SB_HEAD_DIM
SB_BLOCK = 128
HGRN_WIDTH = D_MODEL // 2
HGRN_HEAD_DIM = 128
HGRN_HEADS = HGRN_WIDTH // HGRN_HEAD_DIM
HGRN_CHUNK = 64
N_EXPERTS = 32
TOP_K = 4
D_FF = D_MODEL
SWIGLU_ALPHA = 1.702
SWIGLU_LIMIT = 7.0
EXPERT_BLOCK = 128
DEEPNORM_ALPHA = (2 * DEPTH) ** 0.25
DEEPNORM_BETA = (8 * DEPTH) ** -0.25
LN_EPS = 1e-5
RMS_EPS = 1e-6
IN_SPLITS = (SB_WIDTH, SB_WIDTH, SB_WIDTH, HGRN_WIDTH, HGRN_WIDTH, HGRN_WIDTH, HGRN_WIDTH, D_MODEL, D_MODEL)
IN_WIDTH = sum(IN_SPLITS)


def layer_norm(x, g, b):
    xf = x.astype(jnp.float32)
    mu = jnp.mean(xf, axis=-1, keepdims=True)
    var = jnp.mean(jnp.square(xf - mu), axis=-1, keepdims=True)
    return ((xf - mu) * lax.rsqrt(var + LN_EPS) * g + b).astype(x.dtype)

def stick_breaking_attention(q, k, v):
    T = q.shape[2]
    scale = SB_HEAD_DIM ** -0.5
    qf, kf, vf = q.astype(jnp.float32), k.astype(jnp.float32), v.astype(jnp.float32)
    outs = []
    for blk in range(T // SB_BLOCK):
        t0 = blk * SB_BLOCK
        t1 = t0 + SB_BLOCK
        z = jnp.einsum('bhtd,bhsd->bhts', qf[:, :, t0:t1], kf[:, :, :t1]) * scale
        mask = jnp.arange(t1)[None, :] < (t0 + jnp.arange(SB_BLOCK))[:, None]
        log_keep = jnp.where(mask, jax.nn.log_sigmoid(-z), 0.0)
        log_after = lax.cumsum(log_keep, axis=3, reverse=True) - log_keep
        weights = jnp.where(mask, jnp.exp(jax.nn.log_sigmoid(z) + log_after), 0.0)
        outs.append(jnp.einsum('bhts,bhsd->bhtd', weights, vf[:, :, :t1]))
    return jnp.concatenate(outs, axis=2).astype(q.dtype)

def hgrn2_recurrence(q, k, logf, v):
    B, T, H, dk = q.shape
    dv = v.shape[-1]
    n_chunks = T // HGRN_CHUNK

    def to_chunks(a):
        return a.reshape(B, n_chunks, HGRN_CHUNK, H, a.shape[-1]).transpose(1, 0, 3, 2, 4)

    causal = jnp.tril(jnp.ones((HGRN_CHUNK, HGRN_CHUNK), dtype=bool))

    def step(S, xs):
        qc, kc, gc, vc = xs
        b = jnp.cumsum(gc, axis=2)
        o_inter = jnp.einsum('bhtk,bhkv->bhtv', qc * jnp.exp(b), S)
        diff = b[:, :, :, None, :] - b[:, :, None, :, :]
        decay = jnp.exp(jnp.where(causal[:, :, None], diff, -jnp.inf))
        scores = jnp.einsum('bhtsk,bhsk->bhts', qc[:, :, :, None, :] * decay, kc)
        o = o_inter + jnp.einsum('bhts,bhsv->bhtv', scores, vc)
        b_last = b[:, :, -1:, :]
        S_new = jnp.exp(b_last[:, :, 0, :])[..., None] * S + jnp.einsum(
            'bhsk,bhsv->bhkv', kc * jnp.exp(b_last - b), vc)
        return S_new, o

    S0 = jnp.zeros((B, H, dk, dv), jnp.float32)
    _, o = lax.scan(step, S0, (to_chunks(q), to_chunks(k), to_chunks(logf), to_chunks(v)))
    return o.transpose(1, 0, 3, 2, 4).reshape(B, T, H, dv)

def hybrid_mixer(x, w_in, lower_bound, hgrn_norm_g, w_branch_sb, w_branch_hgrn, w_out):
    B, T, _ = x.shape
    proj = x @ w_in
    offsets = np.cumsum(IN_SPLITS)[:-1].tolist()
    sq, sk, sv, hq, hf, hi, hg, gate_sb, gate_hg = jnp.split(proj, offsets, axis=-1)

    def heads(a):
        return a.reshape(B, T, SB_HEADS, SB_HEAD_DIM).transpose(0, 2, 1, 3)
    o_sb = stick_breaking_attention(heads(sq), heads(sk), heads(sv))
    o_sb = o_sb.transpose(0, 2, 1, 3).reshape(B, T, SB_WIDTH)

    f = lower_bound + (1.0 - lower_bound) * jax.nn.sigmoid(hf.astype(jnp.float32))
    shp = (B, T, HGRN_HEADS, HGRN_HEAD_DIM)
    o_hg = hgrn2_recurrence(jax.nn.silu(hq.astype(jnp.float32)).reshape(shp),
                            (1.0 - f).reshape(shp),
                            jnp.log(f).reshape(shp),
                            hi.astype(jnp.float32).reshape(shp))
    o_hg = o_hg * lax.rsqrt(jnp.mean(jnp.square(o_hg), axis=-1, keepdims=True) + RMS_EPS)
    o_hg = (o_hg.reshape(B, T, HGRN_WIDTH) * hgrn_norm_g * jax.nn.sigmoid(hg.astype(jnp.float32))).astype(x.dtype)

    merged = jax.nn.sigmoid(gate_sb) * (o_sb @ w_branch_sb) + jax.nn.sigmoid(gate_hg) * (o_hg @ w_branch_hgrn)
    return merged @ w_out

def moe(h, router_w, router_b, w_up, b_up, w_down, b_down):
    B, T, D = h.shape
    N = B * T
    xt = h.reshape(N, D)
    logits = (xt @ router_w + router_b).astype(jnp.float32)
    top_vals, top_idx = lax.top_k(logits, TOP_K)
    gates = jax.nn.softmax(top_vals, axis=-1)

    e_flat = top_idx.reshape(-1)
    tok_flat = jnp.arange(N * TOP_K, dtype=jnp.int32) // TOP_K
    order = jnp.argsort(e_flat)
    e_sorted = e_flat[order]
    tok_sorted = tok_flat[order]
    gate_sorted = gates.reshape(-1)[order].astype(h.dtype)

    counts = jnp.bincount(e_flat, length=N_EXPERTS)
    padded = (counts + EXPERT_BLOCK - 1) // EXPERT_BLOCK * EXPERT_BLOCK
    start = jnp.cumsum(counts) - counts
    pad_end = jnp.cumsum(padded)
    pad_start = pad_end - padded
    dest = pad_start[e_sorted] + (jnp.arange(N * TOP_K) - start[e_sorted])

    cap = N * TOP_K + N_EXPERTS * (EXPERT_BLOCK - 1)
    n_blocks = -(-cap // EXPERT_BLOCK)
    n_slots = n_blocks * EXPERT_BLOCK
    slot_tok = jnp.full((n_slots,), N, dtype=jnp.int32).at[dest].set(tok_sorted)
    x_pad = jnp.concatenate([xt, jnp.zeros((1, D), xt.dtype)], axis=0)
    xb = x_pad[slot_tok].reshape(n_blocks, EXPERT_BLOCK, D)
    block_e = jnp.minimum(jnp.searchsorted(pad_end, jnp.arange(n_blocks) * EXPERT_BLOCK, side='right'),
                          N_EXPERTS - 1)

    def expert_block(args):
        xblk, e = args
        hcat = xblk @ w_up[e] + b_up[e]
        x_glu = jnp.minimum(hcat[:, 0::2], SWIGLU_LIMIT)
        x_lin = jnp.clip(hcat[:, 1::2], -SWIGLU_LIMIT, SWIGLU_LIMIT)
        act = x_glu * jax.nn.sigmoid(SWIGLU_ALPHA * x_glu) * (x_lin + 1.0)
        return act @ w_down[e] + b_down[e]

    y_slots = lax.map(expert_block, (xb, block_e)).reshape(n_slots, D)
    contrib = y_slots[dest] * gate_sorted[:, None]
    out = jax.ops.segment_sum(contrib, tok_sorted, num_segments=N)
    return out.reshape(B, T, D).astype(h.dtype)

def first_inputs(seed: int = 0) -> dict:
    key = jax.random.key(seed)
    ks = jax.random.split(key, 18)
    nrm = jax.random.normal
    beta = DEEPNORM_BETA
    col_scale = jnp.concatenate([jnp.full((w,), s, jnp.float32) for w, s in
                                 zip(IN_SPLITS, (1.0, 1.0, beta, 1.0, 1.0, beta, 1.0, 1.0, 1.0))])
    x = nrm(ks[0], (BATCH, SEQ, D_MODEL), jnp.float32)
    w_in = nrm(ks[1], (DEPTH, D_MODEL, IN_WIDTH), jnp.float32) * D_MODEL ** -0.5 * col_scale
    hgrn_lb_logits = 1.0 + 0.1 * nrm(ks[2], (DEPTH + 1, HGRN_WIDTH), jnp.float32)
    hgrn_norm_g = 1.0 + 0.05 * nrm(ks[3], (DEPTH, HGRN_WIDTH), jnp.float32)
    w_branch_sb = nrm(ks[4], (DEPTH, SB_WIDTH, D_MODEL), jnp.float32) * SB_WIDTH ** -0.5
    w_branch_hgrn = nrm(ks[5], (DEPTH, HGRN_WIDTH, D_MODEL), jnp.float32) * HGRN_WIDTH ** -0.5
    w_out = nrm(ks[6], (DEPTH, D_MODEL, D_MODEL), jnp.float32) * D_MODEL ** -0.5 * beta
    ln1_g = 1.0 + 0.05 * nrm(ks[7], (DEPTH, D_MODEL), jnp.float32)
    ln1_b = 0.02 * nrm(ks[8], (DEPTH, D_MODEL), jnp.float32)
    router_w = nrm(ks[9], (DEPTH, D_MODEL, N_EXPERTS), jnp.float32) * D_MODEL ** -0.5
    router_b = 0.01 * nrm(ks[10], (DEPTH, N_EXPERTS), jnp.float32)
    expert_w_up = nrm(ks[11], (DEPTH, N_EXPERTS, D_MODEL, 2 * D_FF), jnp.float32) * D_MODEL ** -0.5 * beta
    expert_b_up = 0.01 * nrm(ks[12], (DEPTH, N_EXPERTS, 2 * D_FF), jnp.float32)
    expert_w_down = nrm(ks[13], (DEPTH, N_EXPERTS, D_FF, D_MODEL), jnp.float32) * D_FF ** -0.5 * beta
    expert_b_down = 0.01 * nrm(ks[14], (DEPTH, N_EXPERTS, D_MODEL), jnp.float32)
    ln2_g = 1.0 + 0.05 * nrm(ks[15], (DEPTH, D_MODEL), jnp.float32)
    ln2_b = 0.02 * nrm(ks[16], (DEPTH, D_MODEL), jnp.float32)
    return {'x': x, 'w_in': w_in, 'hgrn_lb_logits': hgrn_lb_logits, 'hgrn_norm_g': hgrn_norm_g,
            'w_branch_sb': w_branch_sb, 'w_branch_hgrn': w_branch_hgrn, 'w_out': w_out,
            'ln1_g': ln1_g, 'ln1_b': ln1_b, 'router_w': router_w, 'router_b': router_b,
            'expert_w_up': expert_w_up, 'expert_b_up': expert_b_up,
            'expert_w_down': expert_w_down, 'expert_b_down': expert_b_down,
            'ln2_g': ln2_g, 'ln2_b': ln2_b}

def first_block(x, w_in, hgrn_lb_logits, hgrn_norm_g, w_branch_sb, w_branch_hgrn, w_out,
              ln1_g, ln1_b, router_w, router_b, expert_w_up, expert_b_up,
              expert_w_down, expert_b_down, ln2_g, ln2_b):
    lower_bounds = jnp.cumsum(jax.nn.softmax(hgrn_lb_logits.astype(jnp.float32), axis=0), axis=0)
    h = x
    for l in range(DEPTH):
        mix = hybrid_mixer(h, w_in[l], lower_bounds[l], hgrn_norm_g[l],
                           w_branch_sb[l], w_branch_hgrn[l], w_out[l])
        h = layer_norm(DEEPNORM_ALPHA * h + mix, ln1_g[l], ln1_b[l])
        ffn = moe(h, router_w[l], router_b[l], expert_w_up[l], expert_b_up[l],
                  expert_w_down[l], expert_b_down[l])
        h = layer_norm(DEEPNORM_ALPHA * h + ffn, ln2_g[l], ln2_b[l])
    return h


GRID_W = 64
HEAD_DIM = 64
NA_HEADS = D_MODEL // 256
NA_WIDTH = NA_HEADS * HEAD_DIM
NA_KR_MAX = 8
NA_KC = 16
MLA_HEADS = D_MODEL // 128
MLA_NOPE = 64
MLA_ROPE = 32
MLA_V = 64
MLA_Q_RANK = 384
MLA_KV_RANK = 256
MLA_WIDTH = MLA_HEADS * MLA_V
ROPE_THETA = 10000.0
Q_BLOCK = 128
CONV_WIDTH = D_MODEL // 4
CONV_K = 3
D_MIX = NA_WIDTH + MLA_WIDTH + CONV_WIDTH
D_IN = 3 * NA_WIDTH + MLA_Q_RANK + MLA_KV_RANK + MLA_ROPE + 3 * CONV_WIDTH
OUT_GROUPS = D_MIX // HEAD_DIM
D_FF_2 = -(-8 * D_MODEL // (3 * 256)) * 256
EPS = 1e-6


def rms_norm(x, g):
    xf = x.astype(jnp.float32)
    y = xf * lax.rsqrt(jnp.mean(xf * xf, axis=-1, keepdims=True) + EPS)
    return (y * g.astype(jnp.float32)).astype(x.dtype)

def ada_norm(x, g, shift, scale):
    return rms_norm(x, g) * (1 + scale) + shift

def rope_tables(positions):
    inv = ROPE_THETA ** (-jnp.arange(0, MLA_ROPE, 2, dtype=jnp.float32) / MLA_ROPE)
    ang = positions.astype(jnp.float32)[..., None] * inv
    return jnp.cos(ang), jnp.sin(ang)

def apply_rope(x, cos, sin):
    xf = x.astype(jnp.float32)
    x1, x2 = jnp.split(xf, 2, axis=-1)
    return jnp.concatenate([x1 * cos - x2 * sin, x2 * cos + x1 * sin], axis=-1).astype(x.dtype)

def neighbourhood_attention(q, k, v, rpb):
    b, t, h, dh = q.shape
    rows = t // GRID_W
    kr = min(NA_KR_MAX, rows)
    kc = NA_KC
    qg = q.reshape(b, rows, GRID_W, h, dh)
    kg = k.reshape(b, rows, GRID_W, h, dh)
    vg = v.reshape(b, rows, GRID_W, h, dh)
    r = jnp.arange(rows)
    row_start = jnp.clip(r - kr // 2, 0, rows - kr)
    row_idx = row_start[:, None] + jnp.arange(kr)[None, :]
    k_band = kg[:, row_idx]
    v_band = vg[:, row_idx]
    s = jnp.einsum('brqhd,brjwhd->bhrqjw', qg, k_band).astype(jnp.float32) * (dh ** -0.5)
    cols = jnp.arange(GRID_W)
    col_start = jnp.clip(cols - kc // 2, 0, GRID_W - kc)
    col_ok = (cols[None, :] >= col_start[:, None]) & (cols[None, :] < col_start[:, None] + kc)
    dr_i = row_idx - r[:, None] + NA_KR_MAX - 1
    dc_i = jnp.clip(cols[None, :] - cols[:, None] + kc - 1, 0, 2 * kc - 2)
    bias = rpb[:, dr_i[:, None, :, None], dc_i[None, :, None, :]]
    s = jnp.where(col_ok[:, None, :], s + bias.astype(jnp.float32)[None], -jnp.inf)
    p = jax.nn.softmax(s.reshape(b, h, rows, GRID_W, kr * GRID_W), axis=-1)
    p = p.reshape(s.shape).astype(v.dtype)
    o = jnp.einsum('bhrqjw,brjwhd->brqhd', p, v_band)
    return o.reshape(b, t, h * dh)

def latent_attention(c_q, c_kv, k_rope, q_a_g, kv_a_g, w_uq, w_ukv, qn_g, kn_g, qr_g, kr_g, cos, sin):
    b, t, _ = c_q.shape
    q = (rms_norm(c_q, q_a_g) @ w_uq).reshape(b, t, MLA_HEADS, MLA_NOPE + MLA_ROPE)
    kv = (rms_norm(c_kv, kv_a_g) @ w_ukv).reshape(b, t, MLA_HEADS, MLA_NOPE + MLA_V)
    q_nope = rms_norm(q[..., :MLA_NOPE], qn_g)
    q_rope = apply_rope(rms_norm(q[..., MLA_NOPE:], qr_g), cos[:, :, None], sin[:, :, None])
    k_nope = rms_norm(kv[..., :MLA_NOPE], kn_g)
    v = kv[..., MLA_NOPE:]
    k_r = apply_rope(rms_norm(k_rope, kr_g), cos, sin)
    scale = (MLA_NOPE + MLA_ROPE) ** -0.5
    nb = t // Q_BLOCK

    def to_blocks(a):
        return jnp.moveaxis(a.reshape(b, nb, Q_BLOCK, *a.shape[2:]), 1, 0)

    def block(qs):
        qn, qr = qs
        s = jnp.einsum('bqhd,bkhd->bhqk', qn, k_nope) + jnp.einsum('bqhr,bkr->bhqk', qr, k_r)
        p = jax.nn.softmax(s.astype(jnp.float32) * scale, axis=-1).astype(v.dtype)
        return jnp.einsum('bhqk,bkhd->bqhd', p, v)

    o = lax.map(block, (to_blocks(q_nope), to_blocks(q_rope)))
    return jnp.moveaxis(o, 0, 1).reshape(b, t, MLA_WIDTH)

def short_conv(x_in, gate_b, gate_c, conv_w, conv_b):
    u = gate_c * x_in
    y = lax.conv_general_dilated(u, conv_w[:, None, :], window_strides=(1,),
                                 padding=((CONV_K // 2, CONV_K // 2),),
                                 dimension_numbers=('NWC', 'WIO', 'NWC'),
                                 feature_group_count=CONV_WIDTH) + conv_b
    return gate_b * y

def second_inputs(seed: int = 0) -> dict:
    key = jax.random.key(seed)
    ks = jax.random.split(key, 24)
    f32 = jnp.float32

    def dense(k, shape, fan_in, mult=1.0):
        return jax.random.normal(k, shape, f32) * (mult * fan_in ** -0.5)

    def gain(k, shape):
        return 1.0 + 0.05 * jax.random.normal(k, shape, f32)

    def small(k, shape, s):
        return s * jax.random.normal(k, shape, f32)

    L = DEPTH
    return {
        'x': jax.random.normal(ks[0], (BATCH, SEQ, D_MODEL), f32),
        'c': jax.random.normal(ks[1], (BATCH, D_MODEL), f32),
        'positions': jnp.broadcast_to(jnp.arange(SEQ, dtype=jnp.int32), (BATCH, SEQ)),
        'norm1_g': gain(ks[2], (L, D_MODEL)),
        'norm2_g': gain(ks[3], (L, D_MODEL)),
        'w_ada': dense(ks[4], (L, D_MODEL, 6 * D_MODEL), D_MODEL, 0.5),
        'b_ada': small(ks[5], (L, 6 * D_MODEL), 0.02),
        'w_in': dense(ks[6], (L, D_MODEL, D_IN), D_MODEL),
        'na_q_g': gain(ks[7], (L, HEAD_DIM)),
        'na_k_g': gain(ks[8], (L, HEAD_DIM)),
        'na_rpb': small(ks[9], (L, NA_HEADS, 2 * NA_KR_MAX - 1, 2 * NA_KC - 1), 0.05),
        'mla_q_a_g': gain(ks[10], (L, MLA_Q_RANK)),
        'mla_kv_a_g': gain(ks[11], (L, MLA_KV_RANK)),
        'mla_w_uq': dense(ks[12], (L, MLA_Q_RANK, MLA_HEADS * (MLA_NOPE + MLA_ROPE)), MLA_Q_RANK),
        'mla_w_ukv': dense(ks[13], (L, MLA_KV_RANK, MLA_HEADS * (MLA_NOPE + MLA_V)), MLA_KV_RANK),
        'mla_qn_g': gain(ks[14], (L, MLA_NOPE)),
        'mla_kn_g': gain(ks[15], (L, MLA_NOPE)),
        'mla_qr_g': gain(ks[16], (L, MLA_ROPE)),
        'mla_kr_g': gain(ks[17], (L, MLA_ROPE)),
        'conv_w': dense(ks[18], (L, CONV_K, CONV_WIDTH), CONV_K),
        'conv_b': small(ks[19], (L, CONV_WIDTH), 0.02),
        'out_norm_g': gain(ks[20], (L, D_MIX)),
        'w_out': dense(ks[21], (L, D_MIX, D_MODEL), D_MIX),
        'w_gu': dense(ks[22], (L, D_MODEL, 2 * D_FF_2), D_MODEL),
        'w_down': dense(ks[23], (L, D_FF_2, D_MODEL), D_FF_2),
    }

def second_block(x, c, positions, norm1_g, norm2_g, w_ada, b_ada, w_in, na_q_g, na_k_g, na_rpb,
              mla_q_a_g, mla_kv_a_g, mla_w_uq, mla_w_ukv, mla_qn_g, mla_kn_g, mla_qr_g, mla_kr_g,
              conv_w, conv_b, out_norm_g, w_out, w_gu, w_down):
    b, t, _ = x.shape
    cos, sin = rope_tables(positions)
    c_act = jax.nn.silu(c)
    i0 = 3 * NA_WIDTH
    i1 = i0 + MLA_Q_RANK
    i2 = i1 + MLA_KV_RANK
    i3 = i2 + MLA_ROPE
    for l in range(DEPTH):
        mod = c_act @ w_ada[l] + b_ada[l]
        sh1, sc1, g1, sh2, sc2, g2 = jnp.split(mod[:, None, :], 6, axis=-1)
        h = ada_norm(x, norm1_g[l], sh1, sc1)
        proj = h @ w_in[l]
        na_qkv, c_q, c_kv, k_rope, conv_in = jnp.split(proj, [i0, i1, i2, i3], axis=-1)
        q, k, v = jnp.split(na_qkv, 3, axis=-1)
        q = rms_norm(q.reshape(b, t, NA_HEADS, HEAD_DIM), na_q_g[l])
        k = rms_norm(k.reshape(b, t, NA_HEADS, HEAD_DIM), na_k_g[l])
        v = v.reshape(b, t, NA_HEADS, HEAD_DIM)
        y_na = neighbourhood_attention(q, k, v, na_rpb[l])
        y_mla = latent_attention(c_q, c_kv, k_rope, mla_q_a_g[l], mla_kv_a_g[l], mla_w_uq[l],
                                 mla_w_ukv[l], mla_qn_g[l], mla_kn_g[l], mla_qr_g[l], mla_kr_g[l],
                                 cos, sin)
        x_in, gate_b, gate_c = jnp.split(conv_in, 3, axis=-1)
        y_conv = short_conv(x_in, gate_b, gate_c, conv_w[l], conv_b[l])
        mixed = jnp.concatenate([y_na, y_mla, y_conv], axis=-1)
        mixed = rms_norm(mixed.reshape(b, t, OUT_GROUPS, HEAD_DIM),
                         out_norm_g[l].reshape(OUT_GROUPS, HEAD_DIM)).reshape(b, t, D_MIX)
        x = x + g1 * (mixed @ w_out[l])
        h2 = ada_norm(x, norm2_g[l], sh2, sc2)
        gt, up = jnp.split(h2 @ w_gu[l], 2, axis=-1)
        x = x + g2 * ((jax.nn.silu(gt) * up) @ w_down[l])
    return x


def setup_inputs(seed=0):
    out = dict(first_inputs(seed))
    for name, value in second_inputs(seed + 1).items():
        if name != "x":
            out[name + "_2"] = value
    return out


def reference(
    x, w_in, hgrn_lb_logits, hgrn_norm_g, w_branch_sb, w_branch_hgrn, w_out, ln1_g, ln1_b,
    router_w, router_b, expert_w_up, expert_b_up, expert_w_down, expert_b_down, ln2_g, ln2_b,
    c_2, positions_2, norm1_g_2, norm2_g_2, w_ada_2, b_ada_2, w_in_2, na_q_g_2, na_k_g_2,
    na_rpb_2, mla_q_a_g_2, mla_kv_a_g_2, mla_w_uq_2, mla_w_ukv_2, mla_qn_g_2, mla_kn_g_2,
    mla_qr_g_2, mla_kr_g_2, conv_w_2, conv_b_2, out_norm_g_2, w_out_2, w_gu_2, w_down_2,
):
    x = first_block(
        x, w_in, hgrn_lb_logits, hgrn_norm_g, w_branch_sb, w_branch_hgrn, w_out, ln1_g, ln1_b,
        router_w, router_b, expert_w_up, expert_b_up, expert_w_down, expert_b_down, ln2_g,
        ln2_b,
    )
    return second_block(
        x, c_2, positions_2, norm1_g_2, norm2_g_2, w_ada_2, b_ada_2, w_in_2, na_q_g_2, na_k_g_2,
        na_rpb_2, mla_q_a_g_2, mla_kv_a_g_2, mla_w_uq_2, mla_w_ukv_2, mla_qn_g_2, mla_kn_g_2,
        mla_qr_g_2, mla_kr_g_2, conv_w_2, conv_b_2, out_norm_g_2, w_out_2, w_gu_2, w_down_2,
    )


_drawn_inputs = setup_inputs


def setup_inputs(seed=0):
    import zlib

    import numpy as np

    out = dict(_drawn_inputs(seed))
    spreads = {}
    factors = {'hgrn_lb_logits': 8.0,
     'hgrn_norm_g': 6.514,
     'router_b': 6.779,
     'expert_b_up': 8.0,
     'expert_b_down': 8.0,
     'norm1_g_2': 3.602,
     'norm2_g_2': 3.8,
     'na_q_g_2': 8.0,
     'na_k_g_2': 8.0,
     'na_rpb_2': 8.0,
     'mla_q_a_g_2': 8.0,
     'mla_kv_a_g_2': 4.115,
     'mla_qn_g_2': 8.0,
     'mla_kn_g_2': 8.0,
     'mla_qr_g_2': 8.0,
     'mla_kr_g_2': 8.0,
     'conv_b_2': 64.0,
     'out_norm_g_2': 3.978}
    for name, (base, spread) in spreads.items():
        noise = np.random.default_rng([zlib.crc32(name.encode()), seed]).standard_normal(out[name].shape)
        drawn = base * np.exp(spread * noise) if base else spread * noise
        out[name] = __import__('jax').numpy.asarray(drawn.astype(out[name].dtype))
    for name, factor in factors.items():
        out[name] = (out[name] * factor).astype(out[name].dtype)
    return out
```

```python
from contextlib import ExitStack

import numpy as np

import concourse.bass as bass
from concourse import mybir

F32 = mybir.dt.float32
I32 = mybir.dt.int32
U32 = mybir.dt.uint32
ALU = mybir.AluOpType
ACT = mybir.ActivationFunctionType
AX = mybir.AxisListType

P = 128
T = 256
TT = T // P
D = 1024
KD = D // P
CH = 256
SLOTS = 12
EARLY = 6
LATE = [6, 7, 8, 9, 10, 11, 4, 5]
SLOT = 2048
ALPHA = 2.0 ** 0.25
LN_EPS = 1e-5
RMS_EPS = 1e-6

HEADS = 4
SUB = 8
CHUNK = 64
NSUB = CHUNK // SUB

E = 32
CAP = 64
ROUNDS = T // CAP
F = 1024
KF = F // P
LINKS = 8
PER = 12

NA = 4
NM = 8
KC = 16
GW = 64
F2 = 2816
KF2 = F2 // P
BIG = -1.0e30

ROWS, at = {}, 0
for name, n in (("lb", 8), ("hnorm", 4), ("convw", 6), ("convb", 2), ("onorm", 8), ("n1", 8), ("n2", 8),
                ("bada", 48), ("cqg", 3), ("ckvg", 2), ("naq", 1), ("nak", 1), ("c", 8), ("q96", 1), ("k96", 1)):
    ROWS[name] = at
    at += n
NROWS = at
SHIFT1, SCALE1, GATE1, SHIFT2, SCALE2, GATE2 = range(0, 48, 8)


class Kit:

    def __init__(self):
        self.chains = {}


class Factors:

    def __init__(self, A, B, C, q):
        self.A, self.B, self.C, self.q = A, B, C, q


def chain(k, eng, name):
    if name not in k.chains:
        k.chains[name] = [k.sem(f"chain_{name}"), 0]
    c = k.chains[name]

    def link(ins):
        c[1] += 1
        ins.then_inc(c[0], 1)
        eng.wait_ge(c[0], c[1])
    return link


def loop_chain(eng, sem, base, per):
    c = [0]

    def link(ins):
        c[0] += 1
        assert c[0] <= per
        ins.then_inc(sem, 1)
        eng.wait_ge(sem, base + c[0])

    def end():
        assert c[0] == per, c[0]
    return link, end


def bc(ap, axis, n):
    v = ap.unsqueeze(axis)
    s = list(v.shape)
    s[axis] = n
    return v.to_broadcast(s)


def first_chunks(a):
    out = []
    w = a["w_in"][0].rearrange("(k p) n -> p k n", p=P)
    for c in IN_ORDER:
        out.append((w[:, :, c * CH:(c + 1) * CH], 8, CH))
    w = a["w_ada_2"][0].rearrange("(k p) n -> p k n", p=P)
    for c in range(24):
        out.append((w[:, :, c * CH:(c + 1) * CH], 8, CH))
    for name in ("w_branch_sb", "w_branch_hgrn"):
        w = a[name][0].rearrange("(k p) n -> p k n", p=P)
        for c in range(2):
            out.append((w[:, :, c * 512:(c + 1) * 512], 4, 512))
    w = a["w_out"][0].rearrange("(k p) n -> p k n", p=P)
    for c in range(4):
        out.append((w[:, :, c * CH:(c + 1) * CH], 8, CH))
    return out


IN_ORDER = [8, 9, 6, 7, 0, 1, 2, 3, 4, 5, 10, 11, 12, 13] + list(range(14, 22))
C_ADA = 22
C_BR = 46
C_OUT = 50
N_FIRST = 54


def last_chunks(a):
    out = []
    w = a["w_in_2"][0].rearrange("(k p) n -> p k n", p=P)
    for c0, n in [(c * CH, CH) for c in range(5)] + [(1280, 160)] + [(1440 + c * CH, CH) for c in range(3)]:
        out.append((w[:, :, c0:c0 + n], 8, n))
    w = a["mla_w_uq_2"][0].rearrange("(k p) n -> p k n", p=P)
    for c in range(2):
        out.append((w[:, :, c * 384:(c + 1) * 384], 3, 384))
    out.append((a["mla_w_ukv_2"][0].rearrange("(k p) n -> p k n", p=P), 2, 1024))
    w = a["w_out_2"][0].rearrange("(k p) n -> p k n", p=P)
    for c in range(4):
        out.append((w[:, :, c * CH:(c + 1) * CH], 8, CH))
    w = a["w_gu_2"][0].rearrange("(k p) n -> p k n", p=P)
    for c in range(F2 // CH):
        for half in (0, F2):
            out.append((w[:, :, half + c * CH:half + (c + 1) * CH], 8, CH))
    w = a["w_down_2"][0].rearrange("(j k p) n -> j p k n", p=P, k=2)
    for c in range(KF2 // 2):
        out.append((w[c], 2, 1024))
    return out


L_UQ = 9
L_UKV = 11
L_OUT = 12
L_GU = 16
L_DOWN = 38
N_LAST = 49


def slot_first(k, i, kt, n):
    return k.ring[:, i % EARLY, 0:kt * n].rearrange("p (k n) -> p k n", k=kt)


def slot_last(k, i, kt, n):
    return k.ring[:, LATE[i % len(LATE)], 0:kt * n].rearrange("p (k n) -> p k n", k=kt)


def load_first(k, sp, lo, hi):
    for i in range(lo, min(hi, N_FIRST)):
        src, kt, n = k.first[i]
        if i >= EARLY:
            sp.wait_ge(k.first_used, i - EARLY + 1)
        sp.dma_start(slot_first(k, i, kt, n), src).then_inc(k.first_in[i % EARLY], 16)


def first_arrived(k, pe, i):
    pe.wait_ge(k.first_in[i % EARLY], 16 * (i // EARLY + 1))
    _, kt, n = k.first[i]
    return slot_first(k, i, kt, n)


def load_last(k, sp, lo, hi):
    for i in range(lo, min(hi, N_LAST)):
        src, kt, n = k.last[i]
        if i >= len(LATE):
            sp.wait_ge(k.last_used, i - len(LATE) + 1)
        sp.dma_start(slot_last(k, i, kt, n), src).then_inc(k.last_in[i % len(LATE)], 16)


def last_arrived(k, pe, i):
    pe.wait_ge(k.last_in[i % len(LATE)], 16 * (i // len(LATE) + 1))
    _, kt, n = k.last[i]
    return slot_last(k, i, kt, n)


def feature_major(nc, out, w, xT, kt, m):
    for j in range(m):
        for q in range(kt):
            last = nc.tensor.matmul(out[:, j * T:(j + 1) * T], w[:, q, j * P:(j + 1) * P], xT[:, q, :],
                                    start=(q == 0), stop=(q == kt - 1))
    return last


def token_major(nc, out, w, xT, kt, n):
    for t in range(TT):
        for q in range(kt):
            last = nc.tensor.matmul(out[:, t * n:(t + 1) * n], xT[:, q, t * P:(t + 1) * P], w[:, q, :],
                                    start=(q == 0), stop=(q == kt - 1))
    return last


def transpose_tokens(nc, k, out, x, first, n):
    for j in range(n):
        for t in range(TT):
            last = nc.tensor.transpose(out[:, j * T + t * P:j * T + (t + 1) * P],
                                       x[:, t, (first + j) * P:(first + j + 1) * P], k.ident[:, :])
    return last


def projections(nc, k, a):
    sem = k.sem
    rows_in, x_in, rows_one = sem("rows_in"), sem("x_in"), sem("rows_one")
    consts = sem("consts")
    xT_done, xT_ready = sem("xT_done"), sem("xT_ready")
    col_done, cols_ready = sem("col_done"), sem("cols_ready")
    evac = sem("in_evac")
    lbd, lb_ready, f_ready, lf_ready = sem("lbd"), sem("lb_ready"), sem("f_ready"), sem("lf_ready")
    diff, expd, fac, zeroed, score, st_ready = (sem(n) for n in (
        "hg_diff", "hg_exp", "hg_factors", "hg_zeroed", "hg_score", "hg_weights"))
    bias_done = sem("bias_done")
    k.fbuf, k.kk, k.hq, k.sgq = (k.tmp(n, [P, HEADS, T]) for n in ("fbuf", "kk", "hq", "sgq"))
    k.bb = k.tmp("bb", [P, HEADS, T + 1])
    k.lb = k.tmp("lb", [P, 3 * HEADS])
    lb, om = k.lb[:, 0:4], k.lb[:, 4:8]
    arena = k.ring[:, EARLY:SLOTS, :].rearrange("p s n -> p (s n)")
    k.arena = arena
    k.st = arena[:, 0:HEADS * 384].rearrange("p (h n) -> p h n", h=HEADS)
    size = 2048 + 1792 + 576 + 2 * T
    bufs = []
    for b in range(2):
        o = HEADS * 384 + b * size
        bufs.append(Factors(
            A=arena[:, o:o + 2048].rearrange("p (b s t) -> p b s t", s=SUB, t=SUB),
            B=arena[:, o + 2048:o + 3840].rearrange("p (c i s) -> p c i s", c=4, i=NSUB - 1),
            C=arena[:, o + 3840:o + 4416].rearrange("p (c s) -> p c s", c=3),
            q=arena[:, o + 4416:o + 4416 + 2 * T].rearrange("p (l t) -> p l t", l=2)))
    tmpA = k.tmp("hg_tmpA", [P, 2, P])
    bank = k.ps[:, 7, :]
    jobs = {6: ("E", 0), 8: ("E", 1), 11: ("E", 2), 14: ("E", 3)}
    pe_jobs = {10: 0, 13: 1, 16: 2, 19: 3}

    block = k.ctx_block("projections")
    with block as blk:
        @blk.sync
        def _(sp):
            for t in range(TT):
                sp.dma_start(k.x[:, t, :], a["x"][0, t * P:(t + 1) * P, :]).then_inc(x_in, 16)
            load_first(k, sp, 0, C_ADA + EARLY)
            for dst, src in k.broadcasts:
                sp.dma_start(dst, src).then_inc(k.bcast_in, 16)

        @blk.gpsimd
        def _(pool):
            link = chain(k, pool, "pool")
            link(nc.gpsimd.memset(k.ones[:, :], 1.0))
            link(nc.gpsimd.memset(k.ident[:, :], 0.0))
            link(nc.gpsimd.affine_select(out=k.ident[:, :], in_=k.ident[:, :], compare_op=ALU.not_equal, fill=1.0,
                                         base=0, pattern=[[-1, P]], channel_multiplier=1))
            nc.gpsimd.affine_select(out=k.strict[:, :], in_=k.ones[:, :], compare_op=ALU.is_ge, fill=0.0,
                                    base=-1, pattern=[[1, P]], channel_multiplier=-1)
            nc.gpsimd.affine_select(out=k.tri[:, :], in_=k.ones[:, :], compare_op=ALU.is_ge, fill=0.0,
                                    base=0, pattern=[[-1, P]], channel_multiplier=1)
            nc.gpsimd.affine_select(out=k.later[:, :], in_=k.ones[:, :], compare_op=ALU.is_ge, fill=0.0,
                                    base=-1, pattern=[[SUB, P // SUB], [0, SUB]], channel_multiplier=-1)
            link(nc.gpsimd.affine_select(out=k.same[:, :], in_=k.ones[:, :], compare_op=ALU.is_ge, fill=0.0,
                                         base=0, pattern=[[1, P]], channel_multiplier=-1))
            link(nc.gpsimd.affine_select(out=k.same[:, :], in_=k.same[:, :], compare_op=ALU.is_ge, fill=0.0,
                                         base=0, pattern=[[-SUB, P // SUB], [0, SUB]], channel_multiplier=1))
            for i in range(3):
                nc.gpsimd.tensor_copy(k.keep[:, i * P:(i + 1) * P], (k.ones if i == 1 else k.strict)[:, :])
            link(nc.gpsimd.iota(k.iota_i[:, :], pattern=[[1, CAP]], base=0, channel_multiplier=0))
            nc.gpsimd.tensor_copy(k.iota[:, :], k.iota_i[:, :]).then_inc(consts, 1)

        @blk.tensor
        def _(pe):
            pe.wait_ge(consts, 1)
            pe.wait_ge(x_in, 32)
            transpose_tokens(nc, k, k.flat[:, 0:2048], k.x, 0, KD).then_inc(xT_done, 1)
            pe.wait_ge(rows_in, 16 * k.n_rows)
            nc.tensor.transpose(k.ps[:, 4, 0:NROWS], k.rows[:, :], k.ident[0:NROWS, 0:NROWS]).then_inc(col_done, 1)
            pe.wait_ge(xT_ready, 2)
            pe.wait_ge(cols_ready, 1)

            def head_scores(h):
                b = bufs[h % 2]
                pe.wait_ge(fac, h + 1)
                pe.wait_ge(zeroed, h + 1)
                for tile in range(2):
                    for t in range(SUB):
                        v = b.A[:, tile * 16:(tile + 1) * 16, :, t].rearrange("p b s -> p (b s)")
                        nc.tensor.matmul(bank[:, 384 + tile * SUB + t:385 + tile * SUB + t], v, k.ones[:, 0:1],
                                         start=True, stop=True)
                for c in range(4):
                    row, col = (c % 2) * CHUNK, (0 if c < 2 else 128) + c * CHUNK
                    for i in range(1, NSUB):
                        nc.tensor.matmul(bank[row:row + CHUNK, col + i * SUB:col + (i + 1) * SUB], b.B[:, c, i - 1, :],
                                         b.q[:, 0, c * CHUNK + i * SUB:c * CHUNK + (i + 1) * SUB],
                                         start=True, stop=True)
                for c in range(1, 4):
                    n = min(c * CHUNK, P)
                    nc.tensor.matmul(bank[0:n, c * CHUNK:(c + 1) * CHUNK], b.C[:, c - 1, 0:n],
                                     b.q[:, 1, c * CHUNK:(c + 1) * CHUNK], start=True, stop=True)
                nc.tensor.matmul(bank[0:CHUNK, 320:384], b.C[:, 2, P:P + CHUNK], b.q[:, 1, 3 * CHUNK:4 * CHUNK],
                                 start=True, stop=True).then_inc(score, 1)

            for i in range(C_ADA):
                w = first_arrived(k, pe, i)
                if i >= 7:
                    pe.wait_ge(evac, i - 6)
                out = k.ps[:, i % 7, :]
                form = token_major if IN_ORDER[i] in (4, 5, 10, 11) else None
                last = token_major(nc, out, w, k.xT, KD, CH) if form else feature_major(nc, out, w, k.xT, KD, 2)
                last.then_inc(k.first_used, 1)
                if i in pe_jobs:
                    head_scores(pe_jobs[i])
            pe.wait_ge(evac, C_ADA)
            pe.wait_ge(k.bias_in, 32)
            for par in range(2):
                for m in range(KF):
                    nc.tensor.transpose(k.ps[:, 0, (par * 8 + m) * E:(par * 8 + m + 1) * E],
                                        k.b_up[:, m * 256 + par:(m + 1) * 256:2], k.ident[0:E, 0:E])
            for m in range(KD):
                last = nc.tensor.transpose(k.ps[:, 1, m * E:(m + 1) * E], k.b_dn[:, m * P:(m + 1) * P],
                                           k.ident[0:E, 0:E])
            last.then_inc(bias_done, 1)

        @blk.scalar
        def _(act):
            act.wait_ge(rows_one, 1)
            for dst, src in k.row_loads:
                act.dma_start(dst, src).then_inc(rows_in, 16)
            act.dma_start(k.b_up[:, :], a["expert_b_up"][0]).then_inc(k.bias_in, 16)
            act.dma_start(k.b_dn[:, :], a["expert_b_down"][0]).then_inc(k.bias_in, 16)
            link = chain(k, act, "act")
            act.wait_ge(xT_done, 1)
            nc.scalar.copy(k.xT[:, 4:8, :].rearrange("p k t -> p (k t)"), k.flat[:, 1024:2048]).then_inc(xT_ready, 1)
            act.wait_ge(lbd, 1)
            nc.scalar.activation(lb, k.lb[:, 8:12], ACT.Sigmoid).then_inc(lb_ready, 1)

            def exps(h):
                b = bufs[h % 2]
                act.wait_ge(diff, h + 1)
                for v in (b.A, b.B, b.C):
                    v = v.rearrange("p b s t -> p (b s t)") if len(v.shape) == 4 else v.rearrange("p b s -> p (b s)")
                    nc.scalar.activation(v, v, ACT.Exp)
                nc.scalar.activation(b.q, b.q, ACT.Exp).then_inc(expd, 1)

            for i, c in enumerate(IN_ORDER):
                act.wait_ge(k.first_used, i + 1)
                src = k.ps[:, i % 7, :]
                two = src.rearrange("p (m t) -> p m t", m=2)
                j = 2 * (c % 2)
                if c in (8, 9):
                    ins = nc.scalar.activation(k.fbuf[:, j:j + 2, :], two, ACT.Sigmoid)
                elif c in (6, 7):
                    nc.scalar.copy(k.hq[:, j:j + 2, :], two)
                    ins = nc.scalar.activation(k.sgq[:, j:j + 2, :], two, ACT.Sigmoid)
                elif c in (0, 1):
                    ins = nc.scalar.mul(k.sbq[:, j:j + 2, :], two, 0.125)
                elif c in (2, 3):
                    ins = nc.scalar.copy(k.sbk[:, j:j + 2, :], two)
                elif c in (4, 5):
                    ins = nc.scalar.copy(k.sbv[:, :, (c - 4) * CH:(c - 3) * CH], two)
                elif c in (10, 11):
                    ins = nc.scalar.copy(k.hgv[:, :, (c - 10) * CH:(c - 9) * CH], two)
                elif c in (12, 13):
                    ins = nc.scalar.activation(k.hgs[:, j:j + 2, :], two, ACT.Sigmoid)
                else:
                    ins = nc.scalar.activation(k.gates[:, 2 * (c - 14):2 * (c - 14) + 2, :], two, ACT.Sigmoid)
                ins.then_inc(evac, 1)
                if i == 4:
                    act.wait_ge(f_ready, 1)
                    nc.scalar.activation(k.sgq[:, :, :], k.fbuf[:, :, :], ACT.Ln).then_inc(lf_ready, 1)
                if i in jobs:
                    exps(jobs[i][1])
            act.wait_ge(bias_done, 1)
            nc.scalar.copy(k.bupT[:, :], k.ps[:, 0, :])
            link(nc.scalar.copy(k.bdnT[:, :], k.ps[:, 1, 0:KD * E]))

        @blk.vector
        def _(dve):
            link = chain(k, dve, "dve")
            nc.vector.memset(k.rows[:, :], 1.0).then_inc(rows_one, 1)
            nc.vector.memset(k.bb[:, :, 0:1], 0.0)
            dve.wait_ge(consts, 1)
            nc.vector.tensor_scalar(k.nkeep[:, :], k.keep[:, :], -1.0, None, ALU.mult)
            nc.vector.memset(k.eps[:, 0:1], LN_EPS)
            link(nc.vector.memset(k.eps[:, 1:2], RMS_EPS))
            dve.wait_ge(xT_done, 1)
            nc.vector.tensor_copy(k.xT[:, 0:4, :].rearrange("p k t -> p (k t)"), k.flat[:, 0:1024]).then_inc(xT_ready, 1)
            dve.wait_ge(col_done, 1)
            nc.vector.tensor_copy(k.cols[:, :], k.ps[:, 4, 0:NROWS]).then_inc(cols_ready, 1)
            dve.wait_ge(cols_ready, 1)
            nc.vector.tensor_tensor(k.lb[:, 8:12], k.cols[:, 0:4], k.cols[:, 4:8], ALU.subtract).then_inc(lbd, 1)
            dve.wait_ge(lb_ready, 1)
            link(nc.vector.tensor_scalar(om, lb, -1.0, 1.0, ALU.mult, ALU.add))
            dve.wait_ge(evac, 4)
            for h in range(HEADS):
                ins = nc.vector.tensor_scalar(k.fbuf[:, h, :], k.fbuf[:, h, :], om[:, h:h + 1], lb[:, h:h + 1],
                                              ALU.mult, ALU.add)
            link(ins)
            link(nc.vector.tensor_tensor(k.hq[:, :, :], k.hq[:, :, :], k.sgq[:, :, :], ALU.mult))
            nc.vector.tensor_scalar(k.kk[:, :, :], k.fbuf[:, :, :], -1.0, 1.0, ALU.mult, ALU.add).then_inc(f_ready, 1)
            dve.wait_ge(lf_ready, 1)
            dve.wait_ge(f_ready, 1)
            one = k.ones[:, 0:1].to_broadcast([P, T])
            for h in range(HEADS):
                ins = nc.vector.tensor_tensor_scan(k.bb[:, h, 1:T + 1], one, k.sgq[:, h, :], 0.0, ALU.mult, ALU.add)
            link(ins)

            def diffs(h):
                b = bufs[h % 2]
                after = k.bb[:, h, 1:T + 1]
                before = k.bb[:, h, 0:T]
                small = after.rearrange("p (b s) -> p b s", s=SUB)
                nc.vector.tensor_tensor(b.A, bc(small, 2, SUB), bc(small, 3, SUB), ALU.subtract)
                for c in range(4):
                    keys = after[:, c * CHUNK:(c + 1) * CHUNK]
                    starts = before[:, c * CHUNK + SUB:(c + 1) * CHUNK:SUB]
                    nc.vector.tensor_tensor(b.B[:, c], bc(starts, 2, CHUNK), bc(keys, 1, NSUB - 1), ALU.subtract)
                starts = before[:, CHUNK:T:CHUNK]
                nc.vector.tensor_tensor(b.C, bc(starts, 2, 192), bc(after[:, 0:192], 1, 3), ALU.subtract)
                nc.vector.tensor_tensor(b.q[:, 0, :].rearrange("p (b s) -> p b s", s=SUB), small,
                                        bc(before[:, 0:T:SUB], 2, SUB), ALU.subtract)
                link(nc.vector.tensor_tensor(b.q[:, 1, :].rearrange("p (b s) -> p b s", s=CHUNK),
                                             after.rearrange("p (b s) -> p b s", s=CHUNK),
                                             bc(before[:, 0:T:CHUNK], 2, CHUNK), ALU.subtract))
                whole = arena[:, HEADS * 384 + (h % 2) * size:HEADS * 384 + (h % 2) * size + size]
                nc.vector.tensor_scalar(whole, whole, 0.0, None, ALU.min).then_inc(diff, 1)

            def factors(h):
                b = bufs[h % 2]
                key, query = k.kk[:, h, :], k.hq[:, h, :]
                dve.wait_ge(expd, h + 1)
                nc.vector.tensor_tensor(b.C, b.C, bc(key[:, 0:192], 1, 3), ALU.mult)
                for c in range(4):
                    nc.vector.tensor_tensor(b.B[:, c], b.B[:, c], bc(key[:, c * CHUNK:(c + 1) * CHUNK], 1, NSUB - 1),
                                            ALU.mult)
                link(nc.vector.tensor_tensor(b.A, b.A, bc(key.rearrange("p (b s) -> p b s", s=SUB), 3, SUB), ALU.mult))
                nc.vector.tensor_tensor(b.q, b.q, bc(query, 1, 2), ALU.mult)
                nc.vector.tensor_tensor(b.A, b.A, bc(query.rearrange("p (b s) -> p b s", s=SUB), 2, SUB),
                                        ALU.mult).then_inc(fac, 1)

            def zero():
                nc.vector.memset(bank[:, 0:384], 0.0).then_inc(zeroed, 1)

            def weights(h):
                dve.wait_ge(score, h + 1)
                for tile in range(2):
                    g = bank[:, 384 + tile * SUB:384 + (tile + 1) * SUB]
                    nc.vector.tensor_tensor(tmpA[:, tile, :].rearrange("p (b s) -> p b s", s=SUB),
                                            k.same[:, :].rearrange("p (b s) -> p b s", s=SUB), bc(g, 1, P // SUB),
                                            ALU.mult)
                    nc.vector.tensor_tensor(k.st[:, h, tile * 256:tile * 256 + P], bank[:, tile * 256:tile * 256 + P],
                                            k.later[:, :], ALU.mult)
                link(nc.vector.tensor_copy(k.st[:, h, P:2 * P], bank[:, P:2 * P]))
                for tile in range(2):
                    ins = nc.vector.tensor_tensor(k.st[:, h, tile * 256:tile * 256 + P],
                                                  k.st[:, h, tile * 256:tile * 256 + P], tmpA[:, tile, :], ALU.add)
                link(ins)

            zero()
            diffs(0)
            diffs(1)
            factors(0)
            for h in range(HEADS):
                weights(h)
                if h + 1 < HEADS:
                    zero()
                if h + 2 < HEADS:
                    diffs(h + 2)
                if h + 1 < HEADS:
                    factors(h + 1)


def mixers(nc, k, a):
    sem = k.sem
    cact_r, cact = sem("c_sig"), sem("c_act")
    z_done, l_ready, lk_ready, r_done, arg_ready, e_ready, w_ready, pv_done, o_evac = (sem(n) for n in (
        "sb_z", "sb_log", "sb_keep", "sb_sum", "sb_arg", "sb_exp", "sb_weights", "sb_out", "sb_evac"))
    o_done, sq_ready, ss_ready, root_ready, on_ready = (sem(n) for n in (
        "hg_out", "hg_squares", "hg_sums", "hg_root", "hg_normed"))
    el, lk, wt = (k.arena[:, HEADS * 384 * (1 + n):HEADS * 384 * (2 + n)].rearrange("p (h n) -> p h n", h=4)
                  for n in range(3))
    o = 4 * HEADS * 384
    sq = k.arena[:, o:o + 1024].rearrange("p (a n) -> p a n", n=512)
    on = k.arena[:, o + 1024:o + 2048].rearrange("p (a n) -> p a n", n=512)
    small = k.small
    ss, root, rs = small[:, 0:8], small[:, 8:16], small[:, 16:24]
    ca, csig = small[:, 24:32], small[:, 32:40]

    with k.ctx_block("mixers") as blk:
        @blk.sync
        def _(sp):
            load_first(k, sp, C_ADA + EARLY, C_BR + EARLY)

        @blk.tensor
        def _(pe):
            def z(h):
                b, r = h % 4, 64 * (h % 2)
                if h >= 4:
                    pe.wait_ge(o_evac, h - 3)
                q, key = k.sbq[r:r + 64, h // 2, :], k.sbk[r:r + 64, h // 2, :]
                nc.tensor.matmul(k.ps[:, b, 0:T], key[:, 0:P], q, start=True, stop=False, skip_group_check=True)
                nc.tensor.matmul(k.ps[:, b, T:T + P], key[:, P:T], q[:, P:T], start=False, stop=False,
                                 skip_group_check=True).then_inc(z_done, 1)

            def sums(h):
                b = h % 4
                pe.wait_ge(lk_ready, h + 1)
                nc.tensor.matmul(k.ps[:, b, 0:T], k.tri[:, :], lk[:, b, 0:T], start=False, stop=False,
                                 skip_group_check=True)
                nc.tensor.matmul(k.ps[:, b, P:T], k.ones[:, :], lk[:, b, T:T + P], start=False, stop=False,
                                 skip_group_check=True)
                nc.tensor.matmul(k.ps[:, b, T:T + P], k.tri[:, :], lk[:, b, T:T + P], start=False, stop=True,
                                 skip_group_check=True).then_inc(r_done, 1)

            def values(h):
                b, r = h % 4, 64 * (h % 2)
                pe.wait_ge(w_ready, h + 1)
                nc.tensor.matmul(k.ps[r:r + 64, b, 0:T], k.sbv[:, 0, h * 64:(h + 1) * 64], wt[:, b, 0:T],
                                 start=True, stop=False, skip_group_check=True)
                nc.tensor.matmul(k.ps[r:r + 64, b, P:T], k.sbv[:, 1, h * 64:(h + 1) * 64], wt[:, b, T:T + P],
                                 start=False, stop=True, skip_group_check=True).then_inc(pv_done, 1)

            def ada(lo, hi):
                for c in range(lo, hi):
                    w = first_arrived(k, pe, C_ADA + c)
                    for m in range(2):
                        for q in range(KD):
                            last = nc.tensor.matmul(k.ps[:, 6, 2 * c + m:2 * c + m + 1], w[:, q, m * P:(m + 1) * P],
                                                    ca[:, q:q + 1], start=(q == 0), stop=(q == KD - 1))
                    last.then_inc(k.first_used, 1)

            for h in range(4):
                z(h)
            pe.wait_ge(cact, 1)
            ada(0, 3)
            for h in range(HEADS):
                v = [k.hgv[:, t, h * P:(h + 1) * P] for t in range(TT)]
                nc.tensor.matmul(k.ps[:, 4, h * P:(h + 1) * P], k.st[:, h, 0:P], v[0], start=True, stop=True)
                nc.tensor.matmul(k.ps[:, 5, h * P:(h + 1) * P], k.st[:, h, P:2 * P], v[0], start=True, stop=False)
                last = nc.tensor.matmul(k.ps[:, 5, h * P:(h + 1) * P], k.st[:, h, 2 * P:3 * P], v[1],
                                        start=False, stop=True)
            last.then_inc(o_done, 1)
            ada(3, 6)
            for h in range(4):
                sums(h)
            ada(6, 12)
            for h in range(4):
                values(h)
            for h in range(4, 8):
                z(h)
            ada(12, 18)
            for h in range(4, 8):
                sums(h)
            ada(18, 24)
            for h in range(4, 8):
                values(h)
            pe.wait_ge(on_ready, 1)
            transpose_tokens(nc, k, k.flat[:, 2048:3072], on, 0, HEADS).then_inc(k.hg_turned, 1)

        @blk.scalar
        def _(act):
            act.wait_ge(cact_r, 1)
            nc.scalar.activation(csig, k.cols[:, ROWS["c"]:ROWS["c"] + 8], ACT.Sigmoid).then_inc(cact_r, 1)
            link = chain(k, act, "act")

            def logs(h):
                b = h % 4
                act.wait_ge(z_done, h + 1)
                if h >= 4:
                    act.wait_ge(lk_ready, h - 3)
                link(nc.scalar.activation(el[:, b, :], k.ps[:, b, 0:384], ACT.Abs))
                link(nc.scalar.activation(el[:, b, :], el[:, b, :], ACT.Exp, scale=-1.0))
                nc.scalar.activation(el[:, b, :], el[:, b, :], ACT.Ln, bias=1.0).then_inc(l_ready, 1)

            def exps(h):
                b = h % 4
                act.wait_ge(arg_ready, h + 1)
                nc.scalar.activation(wt[:, b, :], wt[:, b, :], ACT.Exp).then_inc(e_ready, 1)

            for h in range(4):
                logs(h)
            act.wait_ge(o_done, 1)
            nc.scalar.activation(sq, k.ps[:, 4:6, :], ACT.Square).then_inc(sq_ready, 1)
            for h in range(4):
                exps(h)
            for h in range(4, 8):
                logs(h)
            for h in range(4, 8):
                exps(h)
            act.wait_ge(ss_ready, 1)
            nc.scalar.activation(root, ss, ACT.Sqrt, bias=k.eps[:, 1:2], scale=1.0 / P).then_inc(root_ready, 1)

        @blk.vector
        def _(dve):
            link = chain(k, dve, "dve")
            nc.vector.memset(ss, 0.0).then_inc(cact_r, 1)
            dve.wait_ge(cact_r, 2)
            nc.vector.tensor_tensor(ca, csig, k.cols[:, ROWS["c"]:ROWS["c"] + 8], ALU.mult).then_inc(cact, 1)

            def keeps(h):
                b = h % 4
                dve.wait_ge(l_ready, h + 1)
                if h >= 4:
                    dve.wait_ge(r_done, h - 3)
                link(nc.vector.scalar_tensor_tensor(out=lk[:, b, :], in0=k.ps[:, b, 0:384], scalar=0.0,
                                                    in1=el[:, b, :], op0=ALU.max, op1=ALU.add))
                nc.vector.tensor_tensor(lk[:, b, :], lk[:, b, :], k.nkeep[:, :], ALU.mult).then_inc(lk_ready, 1)

            def args(h):
                b = h % 4
                dve.wait_ge(r_done, h + 1)
                if h >= 4:
                    dve.wait_ge(pv_done, h - 3)
                nc.vector.tensor_scalar(wt[:, b, :], k.ps[:, b, 0:384], 0.0, None, ALU.min).then_inc(arg_ready, 1)

            def weights(h):
                b = h % 4
                dve.wait_ge(e_ready, h + 1)
                nc.vector.tensor_tensor(wt[:, b, :], wt[:, b, :], k.keep[:, :], ALU.mult).then_inc(w_ready, 1)

            def out(h):
                r = 64 * (h % 2)
                dve.wait_ge(pv_done, h + 1)
                nc.vector.tensor_copy(k.osbT[r:r + 64, h // 2, :], k.ps[r:r + 64, h % 4, 0:T]).then_inc(o_evac, 1)

            for h in range(4):
                keeps(h)
            for h in range(4):
                args(h)
            for h in range(4):
                weights(h)
            dve.wait_ge(sq_ready, 1)
            nc.vector.tensor_reduce(ss, sq.rearrange("p a (h n) -> p (a h) n", n=P), AX.X, ALU.add)\
                .then_inc(ss_ready, 1)
            for h in range(4):
                out(h)
            for h in range(4, 8):
                keeps(h)
            for h in range(4, 8):
                args(h)
            for h in range(4, 8):
                weights(h)
            for h in range(4, 8):
                out(h)
            dve.wait_ge(k.first_used, C_BR)
            nc.vector.tensor_tensor(k.mod[:, :], k.ps[:, 6, 0:48], k.cols[:, ROWS["bada"]:ROWS["bada"] + 48], ALU.add)
            dve.wait_ge(root_ready, 1)
            link(nc.vector.reciprocal(rs, root))
            nc.vector.tensor_tensor(on.rearrange("p a (h n) -> p (a h) n", n=P),
                                    k.ps[:, 4:6, :].rearrange("p a (h n) -> p (a h) n", n=P), bc(rs, 2, P),
                                    ALU.mult).then_inc(on_ready, 1)


def norm_stats(nc, k, link, x, var_ready):
    for t in range(TT):
        for half in range(2):
            nc.vector.bn_stats(k.stats[:, t, half, :], x[:, t, half * 512:(half + 1) * 512])
    link(nc.vector.memset(k.mv[:, :, :], 0.0))
    for t in range(TT):
        ins = nc.vector.bn_aggr(k.mv[:, t, :], k.stats[:, t, :, :])
    ins.then_inc(var_ready, 1)


def norm_apply(nc, k, dve, link, x, var_ready, n_var, root_ready, n, g, b):
    dve.wait_ge(var_ready, n_var)
    dve.wait_ge(root_ready, n)
    link(nc.vector.reciprocal(k.rstd[:, :], k.root[:, :]))
    for t in range(TT):
        ins = nc.vector.tensor_scalar(x[:, t, :], x[:, t, :], k.mv[:, t, 0:1], k.rstd[:, t:t + 1],
                                      ALU.subtract, ALU.mult)
    link(ins)
    link(nc.vector.tensor_tensor(x[:, :, :], x[:, :, :], bc(g, 1, TT), ALU.mult))
    return nc.vector.tensor_tensor(x[:, :, :], x[:, :, :], bc(b, 1, TT), ALU.add)


def branches(nc, k, a):
    sem = k.sem
    hgT, merged, res, var, root, h_ready = (sem(n) for n in (
        "hgT_ready", "merged", "mix_added", "ln1_var", "ln1_root", "h_ready"))
    hT_done, hT_ready, log_done, negmax, expd, m_ready, pos_done = (sem(n) for n in (
        "hT_done", "hT_ready", "logits_done", "top_negmax", "top_exp", "chosen", "pos_done"))
    ln_in = sem("ln1_in")
    gates, m = k.gates, k.xT
    hT = k.gates[:, 0:8, :]
    lg, m8, ix, ixf, gv, tmp = k.lg, k.m8, k.ix, k.ixf, k.gv, k.rtmp

    with k.ctx_block("branches") as blk:
        @blk.sync
        def _(sp):
            load_first(k, sp, C_BR + EARLY, N_FIRST)
            for q in range(PER):
                if q >= EARLY:
                    sp.wait_ge(k.first_used, N_FIRST - EARLY + (q - EARLY) + 1)
                load_expert(k, sp, a, 0, q)

        @blk.tensor
        def _(pe):
            for c in range(2):
                w = first_arrived(k, pe, C_BR + c)
                feature_major(nc, k.flat[:, c * 1024:(c + 1) * 1024], w, k.osbT, 4, 4).then_inc(k.first_used, 1)
            pe.wait_ge(hgT, HEADS)
            for c in range(2):
                w = first_arrived(k, pe, C_BR + 2 + c)
                feature_major(nc, k.flat[:, 2048 + c * 1024:2048 + (c + 1) * 1024], w, k.hgT, 4, 4)\
                    .then_inc(k.first_used, 1)
            pe.wait_ge(merged, 2)
            for c in range(4):
                w = first_arrived(k, pe, C_OUT + c)
                token_major(nc, k.ps[:, c, :], w, m, KD, CH).then_inc(k.first_used, 1)
            pe.wait_ge(h_ready, 1)
            transpose_tokens(nc, k, k.flat[:, 2048:4096], k.h, 0, KD).then_inc(hT_done, 1)
            pe.wait_ge(hT_ready, 2)
            pe.wait_ge(k.bcast_in, 16 * len(k.broadcasts))
            token_major(nc, k.ps[:, 0, 0:TT * E], k.rw, hT, KD, E).then_inc(log_done, 1)
            pe.wait_ge(m_ready, 1)
            mm = k.chosen
            nc.tensor.matmul(k.ps[:, 1, 0:E], k.strict[:, :], mm[:, 0, :], start=True, stop=True)
            nc.tensor.matmul(k.ps[:, 1, E:2 * E], k.ones[:, :], mm[:, 0, :], start=True, stop=False)
            nc.tensor.matmul(k.ps[:, 1, E:2 * E], k.strict[:, :], mm[:, 1, :], start=False, stop=True)
            nc.tensor.matmul(k.ps[:, 1, 2 * E:3 * E], k.ones[:, :], mm[:, 0, :], start=True, stop=False)
            nc.tensor.matmul(k.ps[:, 1, 2 * E:3 * E], k.ones[:, :], mm[:, 1, :], start=False, stop=True)\
                .then_inc(pos_done, 1)

        @blk.scalar
        def _(act):
            act.dma_start(k.g1, a["ln1_g"][0:1, :].to_broadcast([P, D])).then_inc(ln_in, 16)
            act.dma_start(k.b1, a["ln1_b"][0:1, :].to_broadcast([P, D])).then_inc(ln_in, 16)
            act.wait_ge(var, 1)
            nc.scalar.activation(k.root[:, :], k.mv[:, :, 1], ACT.Sqrt, bias=k.eps[:, 0:1]).then_inc(root, 1)
            act.wait_ge(hT_done, 1)
            nc.scalar.copy(hT[:, 4:8, :].rearrange("p k t -> p (k t)"), k.flat[:, 3072:4096]).then_inc(hT_ready, 1)
            act.wait_ge(negmax, 1)
            for t in range(TT):
                ins = nc.scalar.activation(gv[:, t, :], m8[:, t, 0:4], ACT.Exp, bias=k.small[:, t:t + 1])
            ins.then_inc(expd, 1)

        @blk.vector
        def _(dve):
            link = chain(k, dve, "dve")
            dve.wait_ge(k.hg_turned, 1)
            for h in range(HEADS):
                nc.vector.scalar_tensor_tensor(out=k.hgT[:, h, :], in0=k.flat[:, 2048 + h * T:2048 + (h + 1) * T],
                                               scalar=k.cols[:, ROWS["hnorm"] + h:ROWS["hnorm"] + h + 1],
                                               in1=k.hgs[:, h, :], op0=ALU.mult, op1=ALU.mult).then_inc(hgT, 1)
            for c in range(2):
                f = k.flat[:, c * 1024:(c + 1) * 1024].rearrange("p (m t) -> p m t", t=T)
                g = gates[:, 4 * c:4 * c + 4, :]
                dve.wait_ge(k.first_used, C_BR + c + 1)
                link(nc.vector.tensor_tensor(g, g, f, ALU.mult))
            for c in range(2):
                f = k.flat[:, 2048 + c * 1024:2048 + (c + 1) * 1024].rearrange("p (m t) -> p m t", t=T)
                g = gates[:, 8 + 4 * c:12 + 4 * c, :]
                dve.wait_ge(k.first_used, C_BR + 2 + c + 1)
                link(nc.vector.tensor_tensor(g, g, f, ALU.mult))
                nc.vector.tensor_tensor(m[:, 4 * c:4 * c + 4, :], gates[:, 4 * c:4 * c + 4, :], g, ALU.add)\
                    .then_inc(merged, 1)
            for c in range(4):
                dve.wait_ge(k.first_used, C_OUT + c + 1)
                s = slice(c * CH, (c + 1) * CH)
                ins = nc.vector.scalar_tensor_tensor(out=k.h[:, :, s], in0=k.x[:, :, s], scalar=ALPHA,
                                                     in1=k.ps[:, c, :].rearrange("p (t n) -> p t n", t=TT),
                                                     op0=ALU.mult, op1=ALU.add)
            link(ins)
            dve.wait_ge(k.bcast_in, 16 * len(k.broadcasts))
            dve.wait_ge(ln_in, 32)
            norm_stats(nc, k, link, k.h, var)
            norm_apply(nc, k, dve, link, k.h, var, 1, root, 1, k.g1, k.b1).then_inc(h_ready, 1)
            dve.wait_ge(hT_done, 1)
            nc.vector.tensor_copy(hT[:, 0:4, :].rearrange("p k t -> p (k t)"), k.flat[:, 2048:3072])\
                .then_inc(hT_ready, 1)
            dve.wait_ge(log_done, 1)
            link(nc.vector.tensor_tensor(lg[:, :, :], k.ps[:, 0, 0:TT * E].rearrange("p (t e) -> p t e", t=TT),
                                         bc(k.rb[:, :], 1, TT), ALU.add))
            for t in range(TT):
                ins = nc.vector.max(m8[:, t, :], lg[:, t, :])
            link(ins)
            nc.vector.tensor_scalar(k.small[:, 0:TT], m8[:, :, 0], -1.0, None, ALU.mult).then_inc(negmax, 1)
            for t in range(TT):
                ins = nc.vector.max_index(ix[:, t, :], m8[:, t, :], lg[:, t, :])
            link(ins)
            link(nc.vector.tensor_copy(ixf[:, :, :], ix[:, :, :]))
            dve.wait_ge(expd, 1)
            link(nc.vector.tensor_reduce(k.small[:, 2:4], gv[:, :, :], AX.X, ALU.add))
            link(nc.vector.reciprocal(k.small[:, 4:6], k.small[:, 2:4]))
            link(nc.vector.tensor_tensor(gv[:, :, :], gv[:, :, :], bc(k.small[:, 4:6], 2, 4), ALU.mult))
            for j in range(4):
                for t in range(TT):
                    nc.vector.tensor_scalar(tmp[:, 0, t, :], k.iota[:, 0:E], ixf[:, t, j:j + 1], None, ALU.is_equal)
                    ins = nc.vector.tensor_scalar(tmp[:, 1, t, :], k.iota[:, 0:E], ixf[:, t, j:j + 1],
                                                  gv[:, t, j:j + 1], ALU.is_equal, ALU.mult)
                link(ins)
                for n, dst in ((0, k.chosen), (1, k.gate)):
                    if j == 0:
                        ins = nc.vector.tensor_copy(dst[:, :, :], tmp[:, n])
                    else:
                        ins = nc.vector.tensor_tensor(dst[:, :, :], dst[:, :, :], tmp[:, n], ALU.add)
                if j < 3:
                    link(ins)
                else:
                    ins.then_inc(m_ready, 1)
            dve.wait_ge(pos_done, 1)
            dve.wait_ge(m_ready, 1)
            link(nc.vector.tensor_scalar(k.place[:, :, :], k.ps[:, 1, 0:2 * E].rearrange("p (t e) -> p t e", t=TT),
                                         1.0, None, ALU.add))
            link(nc.vector.tensor_tensor(k.place[:, :, :], k.place[:, :, :], k.chosen[:, :, :], ALU.mult))
            link(nc.vector.tensor_scalar(k.place[:, :, :], k.place[:, :, :], -1.0, None, ALU.add))
            link(nc.vector.tensor_reduce(k.small[:, 0:1], k.ps[:, 1, 2 * E:3 * E], AX.X, ALU.max))
            for j in range(1, ROUNDS):
                ins = nc.vector.tensor_scalar(k.small[:, j:j + 1], k.small[:, 0:1], float(j * CAP), None, ALU.is_gt)
            link(ins)
            link(nc.vector.tensor_reduce(k.small[:, 4:5], k.small[:, 1:ROUNDS], AX.X, ALU.add))
            link(nc.vector.tensor_copy(k.rounds[:, :], k.small[:, 4:5]))


def load_expert(k, sp, a, e, q):
    slot = (EARLY + q) % SLOTS
    if q < 8:
        src = a["expert_w_up"][0, bass.ds(e, 1), q * P:(q + 1) * P, :].rearrange("e p n -> p (e n)")
        dst = k.ring[:, slot, :]
    else:
        j = q - 8
        src = a["expert_w_down"][0, bass.ds(e, 1), j * 256:(j + 1) * 256, :].rearrange("e (k p) n -> p (e k) n", p=P)
        dst = k.ring[:, slot, :].rearrange("p (k n) -> p k n", k=2)
    sp.dma_start(dst, src).then_inc(k.expert_in[q], 16)


def experts(nc, k, a):
    sem = k.sem
    sel_ready, xg_done, xg_ready, selT_done, selT_ready = (sem(n) for n in (
        "sel_ready", "gathered", "xg_ready", "selT_done", "selT_ready"))
    glu_ready, sig_ready, act_ready, y_ready, yt_done, yt_ready, sc_done, acc_done = (sem(n) for n in (
        "glu_ready", "sig_ready", "act_ready", "y_ready", "y_turned", "y_rows", "scattered", "acc_done"))
    used = k.expert_used
    dchain = sem("moe_dve")
    pairs = E // 2
    up, down, selps, xps, yps = k.ps[:, 0:2, :], k.ps[:, 2, :], k.ps[:, 3, 0:T], k.flat[:, 2048:3072], k.flat[:, 3072:4096]

    def extra_rounds(eng):
        return eng.value_load(k.rounds[0:1, 0:1], min_val=0, max_val=ROUNDS - 1)

    with k.ctx_block("experts") as blk:
        @blk.sync
        def _(sp):
            extra = extra_rounds(sp)

            def refill(e, done):
                for q in range(PER):
                    sp.wait_ge(used, done + q + 1)
                    load_expert(k, sp, a, e, q)

            with sp.Fori(0, E - 1) as e:
                refill(e + 1, e * PER)
            with sp.If(extra > 0):
                with sp.Fori(0, extra) as r:
                    refill(0, r * (E * PER) + (E - 1) * PER)
                    with sp.Fori(0, E - 1) as e:
                        refill(e + 1, r * (E * PER) + e * PER + E * PER)
            done = extra * (E * PER)
            for i, slot in enumerate(LATE):
                src, kt, cols = k.last[i]
                q = (slot - EARLY) % SLOTS
                sp.wait_ge(used, done + (E * PER + q + 1 - PER))
                sp.dma_start(slot_last(k, i, kt, cols), src).then_inc(k.last_in[i], 16)

        @blk.tensor
        def _(pe):
            extra = extra_rounds(pe)
            with pe.Fori(0, extra + 1) as r, pe.Fori(0, pairs) as p:
                n = r * pairs + p
                pe.wait_ge(sel_ready, n + 1)
                pe.wait_ge(acc_done, n * 2 + 1)
                for q in range(KD):
                    for t in range(TT):
                        last = nc.tensor.matmul(xps[:, q * P:(q + 1) * P], k.h[:, t, q * P:(q + 1) * P], k.sel[:, 0, t, :],
                                                start=(t == 0), stop=(t == TT - 1))
                last.then_inc(xg_done, 1)
                for t in range(TT):
                    last = nc.tensor.transpose(selps[:, t * P:(t + 1) * P], k.sel[:, 1, t, :], k.ident[:, :])
                last.then_inc(selT_done, 1)
                pe.wait_ge(xg_ready, n + 1)
                pe.wait_ge(acc_done, n * 2 + 2)
                for h in range(2):
                    if h == 1:
                        pe.wait_ge(act_ready, n * 2 + 1)
                    for q in range(KD):
                        pe.wait_ge(k.expert_in[q], n * 32 + 16 * (h + 1))
                        w = k.ring[:, (EARLY + q) % SLOTS, :]
                        for par in range(2):
                            for m in range(KF):
                                last = nc.tensor.matmul(up[:, par, m * CAP:(m + 1) * CAP], w[:, m * 256 + par:(m + 1) * 256:2],
                                                        k.xg[:, q, h * CAP:(h + 1) * CAP], start=(q == 0 and m == 0),
                                                        stop=(q == KD - 1), skip_group_check=True)
                        last.then_inc(used, 1)
                    pe.wait_ge(act_ready, n * 2 + h + 1)
                    for j in range(4):
                        pe.wait_ge(k.expert_in[8 + j], n * 32 + 16 * (h + 1))
                        w = k.ring[:, (EARLY + 8 + j) % SLOTS, :]
                        for kk in range(2):
                            for m in range(KD):
                                last = nc.tensor.matmul(down[:, m * CAP:(m + 1) * CAP], w[:, kk * D + m * P:kk * D + (m + 1) * P],
                                                        k.act[:, 2 * j + kk, :], start=(j == 0 and kk == 0 and m == 0),
                                                        stop=(j == 3 and kk == 1), skip_group_check=True)
                        last.then_inc(used, 1)
                pe.wait_ge(y_ready, n * 2 + 2)
                for m in range(KD):
                    last = nc.tensor.transpose(yps[:, m * P:(m + 1) * P], k.yT[:, m, :], k.ident[:, :])
                last.then_inc(yt_done, 1)
                pe.wait_ge(yt_ready, n + 1)
                pe.wait_ge(selT_ready, n + 1)
                for t, out in enumerate((k.ps[:, 4:6, :], k.ps[:, 0:2, :])):
                    for half in range(2):
                        last = nc.tensor.matmul(out[:, half, :], k.selT[:, t * P:(t + 1) * P],
                                                k.y[:, half * 512:(half + 1) * 512], start=True, stop=True)
                    last.then_inc(sc_done, 1)

        @blk.scalar
        def _(act):
            for dst, src in k.late_loads:
                act.dma_start(dst, src).then_inc(k.late_in, 16)
            extra = extra_rounds(act)
            with act.Fori(0, extra + 1) as r, act.Fori(0, pairs) as p:
                n = r * pairs + p
                act.wait_ge(xg_done, n + 1)
                nc.scalar.copy(k.xg[:, :, :].rearrange("p k n -> p (k n)"), xps).then_inc(xg_ready, 1)
                act.wait_ge(selT_done, n + 1)
                nc.scalar.copy(k.selT[:, :], selps).then_inc(selT_ready, 1)
                for h in range(2):
                    act.wait_ge(glu_ready, n * 2 + h + 1)
                    nc.scalar.activation(k.sig[:, :, :], k.glu[:, :, :], ACT.Sigmoid, scale=1.702).then_inc(sig_ready, 1)
                act.wait_ge(yt_done, n + 1)
                nc.scalar.copy(k.y[:, :], yps).then_inc(yt_ready, 1)

        @blk.vector
        def _(dve):
            extra = extra_rounds(dve)
            for t in range(TT):
                nc.vector.memset(k.acc[:, t, :], 0.0).then_inc(acc_done, 1)
            with dve.Fori(0, extra + 1) as r:
                with dve.Fori(0, pairs) as p:
                    n = r * pairs + p
                    link, end = loop_chain(dve, dchain, n * LINKS + r, LINKS)
                    for h in range(2):
                        for t in range(TT):
                            place = k.place[:, t, bass.ds(p * 2 + h, 1)]
                            g = k.gate[:, t, bass.ds(p * 2 + h, 1)]
                            nc.vector.tensor_scalar(k.sel[:, 0, t, h * CAP:(h + 1) * CAP], k.slots[:, :], place, None,
                                                    ALU.is_equal)
                            last = nc.vector.tensor_scalar(k.sel[:, 1, t, h * CAP:(h + 1) * CAP], k.slots[:, :], place, g,
                                                           ALU.is_equal, ALU.mult)
                    last.then_inc(sel_ready, 1)
                    for h in range(2):
                        e = p * 2 + h
                        bg = k.bupT[:, 0:KF * E].rearrange("p (m e) -> p m e", e=E)[:, :, bass.ds(e, 1)]
                        bl = k.bupT[:, KF * E:2 * KF * E].rearrange("p (m e) -> p m e", e=E)[:, :, bass.ds(e, 1)]
                        bd = k.bdnT[:, :].rearrange("p (m e) -> p m e", e=E)[:, :, bass.ds(e, 1)]
                        wide = [P, KF, CAP]
                        dve.wait_ge(used, n * 24 + h * 12 + 8)
                        link(nc.vector.tensor_tensor(k.glu[:, :, :], up[:, 0, :].rearrange("p (m s) -> p m s", m=KF),
                                                     bg.to_broadcast(wide), ALU.add))
                        nc.vector.tensor_scalar(k.glu[:, :, :], k.glu[:, :, :], 7.0, None, ALU.min).then_inc(glu_ready, 1)
                        link(nc.vector.tensor_tensor(k.lin[:, :, :], up[:, 1, :].rearrange("p (m s) -> p m s", m=KF),
                                                     bl.to_broadcast(wide), ALU.add))
                        link(nc.vector.tensor_scalar(k.lin[:, :, :], k.lin[:, :, :], 7.0, -7.0, ALU.min, ALU.max))
                        dve.wait_ge(sig_ready, n * 2 + h + 1)
                        link(nc.vector.scalar_tensor_tensor(out=k.lin[:, :, :], in0=k.lin[:, :, :], scalar=1.0,
                                                            in1=k.sig[:, :, :], op0=ALU.add, op1=ALU.mult))
                        nc.vector.tensor_tensor(k.act[:, :, :], k.lin[:, :, :], k.glu[:, :, :], ALU.mult)\
                            .then_inc(act_ready, 1)
                        dve.wait_ge(used, n * 24 + h * 12 + 12)
                        nc.vector.tensor_tensor(k.yT[:, :, h * CAP:(h + 1) * CAP],
                                                down.rearrange("p (m s) -> p m s", m=KD), bd.to_broadcast(wide),
                                                ALU.add).then_inc(y_ready, 1)
                    for t, src in enumerate((k.ps[:, 4:6, :], k.ps[:, 0:2, :])):
                        dve.wait_ge(sc_done, n * 2 + t + 1)
                        dve.wait_ge(acc_done, n * 2 + t + 1)
                        nc.vector.tensor_tensor(k.acc[:, t, :], k.acc[:, t, :], src.rearrange("p a n -> p (a n)"),
                                                ALU.add).then_inc(acc_done, 1)
                    end()
                nc.vector.tensor_scalar(k.slots[:, :], k.slots[:, :], float(CAP), None, ALU.add).then_inc(dchain, 1)
                dve.wait_ge(dchain, (r + 1) * (pairs * LINKS + 1))


def rms_root(nc, act, src, junk, ss, root, eps, width, sums_ready, n_in, root_ready):
    act.wait_ge(sums_ready, n_in)
    nc.scalar.activation(root, ss, ACT.Sqrt, bias=eps, scale=1.0 / width).then_inc(root_ready, 1)


def second_in(nc, k, a):
    sem = k.sem
    var, root, x_ready, sq_done, rroot, xn_ready, xnT_done = (sem(n) for n in (
        "ln2_var", "ln2_root", "x2_ready", "x2_squared", "x2_root", "x2_normed", "x2_turned"))
    hT_ready, evac = sem("h2T_ready"), sem("in2_evac")
    gd, gb_done = sem("gate_diag"), sem("gate_rows")
    gb_out, flip_ready, bm_done, bm_out = (sem(n) for n in ("gate_rows_out", "flip_ready", "bias_turned", "bias_out"))
    x2, xn, hT = k.h, k.xn, k.hT2
    rs = k.small[:, 0:2]
    with k.ctx_block("second_in") as blk:
        @blk.sync
        def _(sp):
            load_last(k, sp, len(LATE), L_UQ + len(LATE))

        @blk.tensor
        def _(pe):
            for n in range(2):
                pe.wait_ge(gd, n + 1)
                for m in range(KD):
                    last = nc.tensor.matmul(k.flat[:, n * D + m * P:n * D + (m + 1) * P], k.ones[:, :],
                                            k.diag[:, n, m * P:(m + 1) * P], start=True, stop=True)
                last.then_inc(gb_done, 1)
            pe.wait_ge(gb_out, 1)
            pe.wait_ge(flip_ready, 1)
            pe.wait_ge(k.late_in, 16 * len(k.late_loads))
            bias = k.bm[:, :, :, :].rearrange("p t h n -> p (t h n)")
            for b in range(4):
                last = nc.tensor.matmul(k.ps[:, b, :], k.flip[:, :], bias[:, b * 512:(b + 1) * 512], start=True, stop=True)
            last.then_inc(bm_done, 1)
            pe.wait_ge(xn_ready, 1)
            transpose_tokens(nc, k, k.flat[:, 2048:4096], xn, 0, KD).then_inc(xnT_done, 1)
            pe.wait_ge(bm_out, 1)
            pe.wait_ge(hT_ready, 2)
            for i in range(L_UQ):
                w = last_arrived(k, pe, i)
                if i >= 8:
                    pe.wait_ge(evac, i - 7)
                n = k.last[i][2]
                out = k.ps[:, i % 8, :]
                last = token_major(nc, out, w, hT, KD, n) if i < 6 else feature_major(nc, out, w, hT, KD, 2)
                last.then_inc(k.last_used, 1)

        @blk.scalar
        def _(act):
            link = chain(k, act, "act")
            act.wait_ge(gb_done, 2)
            nc.scalar.copy(k.gB[:, :, :].rearrange("p n d -> p (n d)"), k.flat[:, 0:2048]).then_inc(gb_out, 1)
            act.wait_ge(bm_done, 1)
            nc.scalar.copy(k.bm[:, :, :, :].rearrange("p t h n -> p (t h n)"), k.flat[:, 0:2048]).then_inc(bm_out, 1)
            act.wait_ge(var, 1)
            nc.scalar.activation(k.root[:, :], k.mv[:, :, 1], ACT.Sqrt, bias=k.eps[:, 0:1]).then_inc(root, 1)
            act.wait_ge(sq_done, 1)
            nc.scalar.activation(k.root[:, :], k.small[:, 2:4], ACT.Sqrt, bias=k.eps[:, 1:2], scale=1.0 / D)\
                .then_inc(rroot, 1)
            act.wait_ge(xnT_done, 1)
            for m in range(4, KD):
                ins = nc.scalar.activation(hT[:, m, :], k.flat[:, 2048 + m * T:2048 + (m + 1) * T], ACT.Identity,
                                           bias=k.mod[:, SHIFT1 + m:SHIFT1 + m + 1], scale=k.ada[:, m:m + 1])
            ins.then_inc(hT_ready, 1)
            for i in range(L_UQ):
                act.wait_ge(k.last_used, i + 1)
                n = k.last[i][2]
                src = k.ps[:, i % 8, :]
                if i < 6:
                    ins = nc.scalar.copy(k.proj[:, :, i * CH:i * CH + n],
                                         src[:, 0:TT * n].rearrange("p (t n) -> p t n", t=TT))
                else:
                    ins = nc.scalar.copy(k.conv[:, 2 * (i - 6):2 * (i - 5), :], src.rearrange("p (m t) -> p m t", m=2))
                ins.then_inc(evac, 1)

        @blk.gpsimd
        def _(pool):
            link = chain(k, pool, "pool")
            link(nc.gpsimd.memset(k.flip[:, :], 0.0))
            for half in range(2):
                v = k.flip[half * GW:(half + 1) * GW, half * GW:(half + 1) * GW]
                ins = nc.gpsimd.affine_select(out=v, in_=v, compare_op=ALU.not_equal, fill=1.0, base=-(GW - 1),
                                              pattern=[[1, GW]], channel_multiplier=1)
            ins.then_inc(flip_ready, 1)
            pool.wait_ge(bm_out, 1)
            for half in range(2):
                v = k.bm[half * GW:(half + 1) * GW, :, :, :].rearrange("p t h (j w) -> p (t h j) w", w=GW)
                left, right = v[:, :, 0:GW - KC], v[:, :, KC:GW]
                link(nc.gpsimd.affine_select(out=left, in_=left, compare_op=ALU.is_ge, fill=BIG, base=KC // 2,
                                             pattern=[[0, TT * NA * 4], [1, GW - KC]], channel_multiplier=-1))
                link(nc.gpsimd.affine_select(out=right, in_=right, compare_op=ALU.is_ge, fill=BIG,
                                             base=KC // 2 - 1 - KC, pattern=[[0, TT * NA * 4], [-1, GW - KC]],
                                             channel_multiplier=1))

        @blk.vector
        def _(dve):
            link = chain(k, dve, "dve")
            for n, row in enumerate((GATE1, GATE2)):
                for m in range(KD):
                    ins = nc.vector.tensor_scalar(k.diag[:, n, m * P:(m + 1) * P], k.ident[:, :],
                                                  k.mod[:, row + m:row + m + 1], None, ALU.mult)
                ins.then_inc(gd, 1)
            for n, (row, gain) in enumerate(((SCALE1, "n1"), (SCALE2, "n2"))):
                nc.vector.scalar_tensor_tensor(out=k.ada[:, n * KD:(n + 1) * KD], in0=k.mod[:, row:row + KD], scalar=1.0,
                                               in1=k.cols[:, ROWS[gain]:ROWS[gain] + KD], op0=ALU.add, op1=ALU.mult)
            link(nc.vector.scalar_tensor_tensor(out=x2[:, :, :], in0=k.h[:, :, :], scalar=ALPHA, in1=k.acc[:, :, :],
                                                op0=ALU.mult, op1=ALU.add))
            dve.wait_ge(k.late_in, 16 * len(k.late_loads))
            norm_stats(nc, k, link, x2, var)
            link(norm_apply(nc, k, dve, link, x2, var, 1, root, 1, k.g2[:, :], k.b2[:, :]))
            link(nc.vector.tensor_tensor(xn[:, :, :], x2[:, :, :], x2[:, :, :], ALU.mult))
            nc.vector.tensor_reduce(k.small[:, 2:4], xn[:, :, :], AX.X, ALU.add).then_inc(sq_done, 1)
            dve.wait_ge(rroot, 1)
            link(nc.vector.reciprocal(rs, k.root[:, :]))
            for t in range(TT):
                ins = nc.vector.tensor_scalar(xn[:, t, :], x2[:, t, :], rs[:, t:t + 1], None, ALU.mult)
            ins.then_inc(xn_ready, 1)
            dve.wait_ge(xnT_done, 1)
            for m in range(4):
                ins = nc.vector.tensor_scalar(hT[:, m, :], k.flat[:, 2048 + m * T:2048 + (m + 1) * T],
                                              k.ada[:, m:m + 1], k.mod[:, SHIFT1 + m:SHIFT1 + m + 1], ALU.mult, ALU.add)
            ins.then_inc(hT_ready, 1)


def group_norm(nc, link, x, sq, ss, n):
    link(nc.vector.tensor_tensor(sq, x, x, ALU.mult))
    return nc.vector.tensor_reduce(ss, sq, AX.X, ALU.add)


def heads_in(nc, k, a):
    sem = k.sem
    sums, roots, na_n, na_t, ck_n, ck_t, ck_ready = (sem(n) for n in (
        "proj_sums", "proj_roots", "na_normed", "na_turned", "lat_normed", "lat_turned", "latT_ready"))
    q_evac, msums, mroots, ang, trig, q_ready, k_ready, qt_done, qt_ready, kt_done = (sem(n) for n in (
        "mla_evac", "mla_sums", "mla_roots", "angles", "trig", "q96_ready", "k96_ready", "q96_turned", "q96_out",
        "k96_turned"))
    cv, cv_t = sem("conv_ready"), sem("conv_turned")
    proj = k.proj
    nav = proj[:, :, 0:512].rearrange("p t (g n) -> p t g n", n=64)
    ss, root, rs = k.ss, k.sroot, k.srs
    sq = k.sq
    qm, kv = k.qm, k.kv
    kr = proj[:, :, 1408:1440]
    with k.ctx_block("heads_in") as blk:
        @blk.sync
        def _(sp):
            load_last(k, sp, L_UQ + len(LATE), L_OUT + len(LATE))

        @blk.tensor
        def _(pe):
            pe.wait_ge(na_n, 1)
            transpose_tokens(nc, k, k.flat[:, 0:1024], proj[:, :, 0:512], 0, 4).then_inc(na_t, 1)
            pe.wait_ge(ck_n, 1)
            transpose_tokens(nc, k, k.flat[:, 1024:2304], proj[:, :, 768:1408], 0, 5).then_inc(ck_t, 1)
            pe.wait_ge(ck_ready, 1)
            pe.wait_ge(k.naT_ready, 1)
            for c in range(2):
                w = last_arrived(k, pe, L_UQ + c)
                for t in range(TT):
                    b = (5 + 2 * c + t) % 8
                    for q in range(3):
                        last = nc.tensor.matmul(k.ps[:, b, 0:384], k.ckT[:, q, t * P:(t + 1) * P], w[:, q, :],
                                                start=(q == 0), stop=(q == 2))
                last.then_inc(k.last_used, 1)
            w = last_arrived(k, pe, L_UKV)
            for t in range(TT):
                for half in range(2):
                    for q in range(2):
                        last = nc.tensor.matmul(k.ps[:, 1 + 2 * t + half, :], k.ckT[:, 3 + q, t * P:(t + 1) * P],
                                                w[:, q, half * 512:(half + 1) * 512], start=(q == 0), stop=(q == 1))
            last.then_inc(k.last_used, 1)
            pe.wait_ge(cv, 1)
            pe.wait_ge(q_evac, 3)
            for m in range(2):
                for t in range(TT):
                    last = nc.tensor.transpose(k.ps[:, 7, t * 256 + m * P:t * 256 + (m + 1) * P],
                                               k.cy[:, m, t * P:(t + 1) * P], k.ident[:, :])
            last.then_inc(cv_t, 1)
            pe.wait_ge(q_ready, 1)
            for h in range(NM):
                for t in range(TT):
                    last = nc.tensor.transpose(k.flat[0:96, h * T + t * P:h * T + (t + 1) * P],
                                               qm[:, t, h * 96:(h + 1) * 96], k.ident[:, :])
            last.then_inc(qt_done, 1)
            pe.wait_ge(k_ready, 1)
            pe.wait_ge(qt_ready, 1)
            for h in range(NM):
                for t in range(TT):
                    last = nc.tensor.transpose(k.flat[0:96, h * T + t * P:h * T + (t + 1) * P],
                                               k.k96[:, t, h * 96:(h + 1) * 96], k.ident[:, :])
            last.then_inc(kt_done, 1)

        @blk.scalar
        def _(act):
            act.wait_ge(ang, 1)
            nc.scalar.activation(k.trig[:, :, :], k.ang[:, :, :], ACT.Sin).then_inc(trig, 1)
            act.wait_ge(sums, 1)
            nc.scalar.activation(root[:, 0:16], ss[:, 0:16], ACT.Sqrt, bias=k.eps[:, 1:2], scale=1.0 / 64)
            nc.scalar.activation(root[:, 16:18], ss[:, 16:18], ACT.Sqrt, bias=k.eps[:, 1:2], scale=1.0 / 384)
            nc.scalar.activation(root[:, 18:20], ss[:, 18:20], ACT.Sqrt, bias=k.eps[:, 1:2], scale=1.0 / 256)
            nc.scalar.activation(root[:, 20:22], ss[:, 20:22], ACT.Sqrt, bias=k.eps[:, 1:2], scale=1.0 / 32)\
                .then_inc(roots, 1)
            for c in range(2):
                act.wait_ge(k.last_used, L_UQ + c + 1)
                for t in range(TT):
                    ins = nc.scalar.copy(qm[:, t, c * 384:(c + 1) * 384], k.ps[:, (5 + 2 * c + t) % 8, 0:384])
                ins.then_inc(q_evac, 1)
            act.wait_ge(k.last_used, L_OUT)
            nc.scalar.copy(kv[:, :, :].rearrange("p t n -> p (t n)"), k.flat[:, 512:512 + 2048]).then_inc(q_evac, 1)
            act.wait_ge(msums, 1)
            nc.scalar.activation(root[:, 0:16], ss[:, 0:16], ACT.Sqrt, bias=k.eps[:, 1:2], scale=1.0 / 64)
            nc.scalar.activation(root[:, 16:32], ss[:, 16:32], ACT.Sqrt, bias=k.eps[:, 1:2], scale=1.0 / 32)
            nc.scalar.activation(root[:, 32:48], ss[:, 32:48], ACT.Sqrt, bias=k.eps[:, 1:2], scale=1.0 / 64)\
                .then_inc(mroots, 1)
            act.wait_ge(cv_t, 1)
            nc.scalar.copy(k.mixed[:, :, 768:1024], k.ps[:, 7, :].rearrange("p (t n) -> p t n", t=TT))
            act.wait_ge(qt_done, 1)
            nc.scalar.activation(k.q96T[0:96, :, :].rearrange("p h t -> p (h t)"), k.flat[0:96, 0:2048], ACT.Copy,
                                 scale=k.cols[0:96, ROWS["q96"]:ROWS["q96"] + 1]).then_inc(qt_ready, 1)
            act.wait_ge(kt_done, 1)
            link = chain(k, act, "act")
            link(nc.scalar.activation(k.k96T[0:96, :, :].rearrange("p h t -> p (h t)"), k.flat[0:96, 0:2048], ACT.Copy,
                                      scale=k.cols[0:96, ROWS["k96"]:ROWS["k96"] + 1]))

        @blk.gpsimd
        def _(pool):
            link = chain(k, pool, "pool")
            u, y = k.cu, k.cy
            nc.gpsimd.memset(u[:, :, 0:1], 0.0)
            nc.gpsimd.memset(u[:, :, T + 1:T + 2], 0.0)
            link(nc.gpsimd.tensor_tensor(u[:, :, 1:T + 1], k.conv[:, 4:6, :], k.conv[:, 0:2, :], ALU.mult))
            r = ROWS["convw"]
            for m in range(2):
                ins = nc.gpsimd.tensor_scalar(y[:, m, :], u[:, m, 1:T + 1], k.cols[:, r + 2 + m:r + 3 + m],
                                              k.cols[:, ROWS["convb"] + m:ROWS["convb"] + m + 1], ALU.mult, ALU.add)
            link(ins)
            for tap in (0, 2):
                for m in range(2):
                    ins = nc.gpsimd.tensor_scalar(k.ctmp[:, m, :], u[:, m, tap:tap + T],
                                                  k.cols[:, r + 2 * tap + m:r + 2 * tap + m + 1], None, ALU.mult)
                link(ins)
                link(nc.gpsimd.tensor_tensor(y[:, :, :], y[:, :, :], k.ctmp[:, :, :], ALU.add))
            nc.gpsimd.tensor_tensor(y[:, :, :], y[:, :, :], k.conv[:, 2:4, :], ALU.mult).then_inc(cv, 1)

        @blk.vector
        def _(dve):
            link = chain(k, dve, "dve")
            link(nc.vector.tensor_copy(k.posf[:, :], k.pos[:, :]))
            for i, f in enumerate(k.inv):
                ins = nc.vector.tensor_scalar(k.ang[:, :, i], k.posf[:, :], float(f), None, ALU.mult)
            link(ins)
            sn, cs, turn = k.ang[:, :, 0:16], k.ang[:, :, 16:32], k.turn[:, :, :]
            magic, c1 = 1.5 * 2.0 ** 23, 6.28125
            c2 = float(np.float32(2 * np.pi - c1))
            link(nc.vector.tensor_scalar(turn, sn, float(1 / (2 * np.pi)), magic, ALU.mult, ALU.add))
            link(nc.vector.tensor_scalar(turn, turn, magic, None, ALU.subtract))
            link(nc.vector.scalar_tensor_tensor(out=sn, in0=turn, scalar=-c1, in1=sn, op0=ALU.mult, op1=ALU.add))
            link(nc.vector.scalar_tensor_tensor(out=sn, in0=turn, scalar=-c2, in1=sn, op0=ALU.mult, op1=ALU.add))
            link(nc.vector.tensor_scalar(turn, sn, float(np.pi / 2), float(-2 * np.pi), ALU.is_gt, ALU.mult))
            link(nc.vector.scalar_tensor_tensor(out=cs, in0=sn, scalar=float(np.pi / 2), in1=turn, op0=ALU.add,
                                                op1=ALU.add))
            lim = float(np.nextafter(np.float32(np.pi), np.float32(0)))
            nc.vector.tensor_scalar(k.ang[:, :, :], k.ang[:, :, :], lim, -lim, ALU.min, ALU.max).then_inc(ang, 1)
            link(nc.vector.tensor_tensor(sq[:, :, 0:1440], proj[:, :, :], proj[:, :, :], ALU.mult))
            for t in range(TT):
                nc.vector.tensor_reduce(ss[:, t * 8:(t + 1) * 8], sq[:, t, 0:512].rearrange("p (g n) -> p g n", n=64),
                                        AX.X, ALU.add)
            nc.vector.tensor_reduce(ss[:, 16:18], sq[:, :, 768:1152], AX.X, ALU.add)
            nc.vector.tensor_reduce(ss[:, 18:20], sq[:, :, 1152:1408], AX.X, ALU.add)
            nc.vector.tensor_reduce(ss[:, 20:22], sq[:, :, 1408:1440], AX.X, ALU.add).then_inc(sums, 1)
            dve.wait_ge(roots, 1)
            link(nc.vector.reciprocal(rs[:, 0:22], root[:, 0:22]))
            for t in range(TT):
                ins = nc.vector.tensor_tensor(nav[:, t], nav[:, t], bc(rs[:, t * 8:(t + 1) * 8], 2, 64), ALU.mult)
            ins.then_inc(na_n, 1)
            nc.vector.tensor_tensor(proj[:, :, 768:1152], proj[:, :, 768:1152], bc(rs[:, 16:18], 2, 384), ALU.mult)
            nc.vector.tensor_tensor(proj[:, :, 1152:1408], proj[:, :, 1152:1408], bc(rs[:, 18:20], 2, 256), ALU.mult)\
                .then_inc(ck_n, 1)
            link(nc.vector.tensor_tensor(kr, kr, bc(rs[:, 20:22], 2, 32), ALU.mult))
            dve.wait_ge(ck_t, 1)
            for m in range(5):
                ins = nc.vector.tensor_scalar(k.ckT[:, m, :], k.flat[:, 1024 + m * T:1024 + (m + 1) * T],
                                              k.cols[:, ROWS["cqg"] + m:ROWS["cqg"] + m + 1], None, ALU.mult)
            ins.then_inc(ck_ready, 1)
            nc.vector.tensor_scalar(k.naT[:, 0:2, :], k.flat[:, 0:512].rearrange("p (m t) -> p m t", t=T),
                                    k.cols[:, ROWS["naq"]:ROWS["naq"] + 1], 0.125, ALU.mult, ALU.mult)
            nc.vector.tensor_scalar(k.naT[:, 2:4, :], k.flat[:, 512:1024].rearrange("p (m t) -> p m t", t=T),
                                    k.cols[:, ROWS["nak"]:ROWS["nak"] + 1], None, ALU.mult).then_inc(k.naT_ready, 1)
            dve.wait_ge(trig, 1)
            sin, cos = k.trig[:, :, 0:16], k.trig[:, :, 16:32]
            ro, rt = k.rope, k.rope_t
            link(nc.vector.tensor_tensor(kr, kr, bc(k.krg[:, :], 1, TT), ALU.mult))
            nc.vector.tensor_tensor(ro[:, :, 0:16], kr[:, :, 0:16], cos, ALU.mult)
            nc.vector.tensor_tensor(rt[:, :, 0:16], kr[:, :, 16:32], sin, ALU.mult)
            nc.vector.tensor_tensor(ro[:, :, 16:32], kr[:, :, 16:32], cos, ALU.mult)
            link(nc.vector.tensor_tensor(rt[:, :, 16:32], kr[:, :, 0:16], sin, ALU.mult))
            nc.vector.tensor_tensor(ro[:, :, 0:16], ro[:, :, 0:16], rt[:, :, 0:16], ALU.subtract)
            link(nc.vector.tensor_tensor(ro[:, :, 16:32], ro[:, :, 16:32], rt[:, :, 16:32], ALU.add))
            dve.wait_ge(q_evac, 2)
            link(nc.vector.tensor_tensor(sq[:, :, 0:768], qm[:, :, :], qm[:, :, :], ALU.mult))
            for t in range(TT):
                v = sq[:, t, 0:768].rearrange("p (h n) -> p h n", n=96)
                nc.vector.tensor_reduce(ss[:, t * 8:(t + 1) * 8], v[:, :, 0:64], AX.X, ALU.add)
                ins = nc.vector.tensor_reduce(ss[:, 16 + t * 8:16 + (t + 1) * 8], v[:, :, 64:96], AX.X, ALU.add)
            dve.wait_ge(q_evac, 3)
            keys = [kv[:, t, :].rearrange("p (h n) -> p h n", n=128) for t in range(TT)]
            for t in range(TT):
                ins = nc.vector.tensor_tensor(sq[:, t, 768:1280].rearrange("p (h n) -> p h n", n=64),
                                              keys[t][:, :, 0:64], keys[t][:, :, 0:64], ALU.mult)
            link(ins)
            for t in range(TT):
                ins = nc.vector.tensor_reduce(ss[:, 32 + t * 8:32 + (t + 1) * 8],
                                              sq[:, t, 768:1280].rearrange("p (h n) -> p h n", n=64), AX.X, ALU.add)
            ins.then_inc(msums, 1)
            dve.wait_ge(mroots, 1)
            link(nc.vector.reciprocal(rs[:, 0:48], root[:, 0:48]))
            for t in range(TT):
                v = qm[:, t, :].rearrange("p (h n) -> p h n", n=96)
                nc.vector.tensor_tensor(v[:, :, 0:64], v[:, :, 0:64], bc(rs[:, t * 8:(t + 1) * 8], 2, 64), ALU.mult)
                nc.vector.tensor_tensor(v[:, :, 64:96], v[:, :, 64:96], bc(rs[:, 16 + t * 8:24 + t * 8], 2, 32), ALU.mult)
                kd = k.k96[:, t, :].rearrange("p (h n) -> p h n", n=96)
                nc.vector.tensor_tensor(kd[:, :, 0:64], keys[t][:, :, 0:64], bc(rs[:, 32 + t * 8:40 + t * 8], 2, 64),
                                        ALU.mult)
                ins = nc.vector.tensor_copy(kd[:, :, 64:96], bc(ro[:, t, :], 1, NM))
            ins.then_inc(k_ready, 1)
            dve.wait_ge(k_ready, 1)
            vs = [qm[:, t, :].rearrange("p (h n) -> p h n", n=96)[:, :, 64:96] for t in range(TT)]
            for t in range(TT):
                ins = nc.vector.tensor_tensor(vs[t], vs[t], bc(k.qrg[:, :], 1, NM), ALU.mult)
            link(ins)
            for t in range(TT):
                c, s = bc(cos[:, t, :], 1, NM), bc(sin[:, t, :], 1, NM)
                x1, x2 = vs[t][:, :, 0:16], vs[t][:, :, 16:32]
                r1, r2 = (sq[:, t, n:n + 128].rearrange("p (h n) -> p h n", n=16) for n in (0, 128))
                nc.vector.tensor_tensor(r1, x2, s, ALU.mult)
                link(nc.vector.tensor_tensor(r2, x1, s, ALU.mult))
                nc.vector.tensor_tensor(x1, x1, c, ALU.mult)
                link(nc.vector.tensor_tensor(x2, x2, c, ALU.mult))
                nc.vector.tensor_tensor(x1, x1, r1, ALU.subtract)
                ins = nc.vector.tensor_tensor(x2, x2, r2, ALU.add)
                if t == 0:
                    link(ins)
            ins.then_inc(q_ready, 1)


def attention(nc, k, a):
    sem = k.sem
    s_done, m_ready, e_ready, pt_done, pt_ready, o_done, o_out = (sem(n) for n in (
        "att_scores", "att_max", "att_exp", "att_turned", "att_weights", "att_values", "att_out"))
    heads = NA + NM
    mscale = float(MLA_SCALE)
    with k.ctx_block("attention") as blk:
        @blk.tensor
        def _(pe):
            def scores(i):
                if i >= 3:
                    pe.wait_ge(e_ready, i - 2)
                for t in range(TT):
                    if i < NA:
                        r = 64 * (i % 2)
                        q, key = k.naT[r:r + 64, i // 2, :], k.naT[r:r + 64, 2 + i // 2, :]
                    else:
                        q, key = k.q96T[0:96, i - NA, :], k.k96T[0:96, i - NA, :]
                    last = nc.tensor.matmul(k.ps[:, i % 3, t * T:(t + 1) * T], q[:, t * P:(t + 1) * P], key,
                                            start=True, stop=True)
                last.then_inc(s_done, 1)

            def turn(i):
                pe.wait_ge(e_ready, i + 1)
                if i >= 2:
                    pe.wait_ge(pt_ready, i - 1)
                for s in range(TT):
                    for t in range(TT):
                        last = nc.tensor.transpose(k.ps[:, 3 + i % 2, s * T + t * P:s * T + (t + 1) * P],
                                                   k.e[:, i % 2, t, s * P:(s + 1) * P], k.ident[:, :])
                last.then_inc(pt_done, 1)

            def values(i):
                pe.wait_ge(pt_ready, i + 1)
                if i >= 2:
                    pe.wait_ge(o_out, i - 1)
                for t in range(TT):
                    for s in range(TT):
                        v = k.proj[:, s, 512 + 64 * i:576 + 64 * i] if i < NA else \
                            k.kv[:, s, (i - NA) * 128 + 64:(i - NA) * 128 + 128]
                        last = nc.tensor.matmul(k.ps[:, 5 + i % 2, t * 64:(t + 1) * 64], k.pt[:, i % 2, s, t * P:(t + 1) * P],
                                                v, start=(s == 0), stop=(s == 1))
                last.then_inc(o_done, 1)

            scores(0)
            scores(1)
            for i in range(heads):
                if i + 2 < heads:
                    scores(i + 2)
                turn(i)
                if i >= 1:
                    values(i - 1)
            values(heads - 1)

        @blk.scalar
        def _(act):
            def exps(i):
                act.wait_ge(m_ready, i + 1)
                if i >= 2:
                    act.wait_ge(pt_done, i - 1)
                for t in range(TT):
                    src = k.sB[:, i % 2, t, :] if i < NA else k.ps[:, i % 3, t * T:(t + 1) * T]
                    ins = nc.scalar.activation(k.e[:, i % 2, t, :], src, ACT.Exp, bias=k.nmax[:, i, t:t + 1],
                                               scale=1.0 if i < NA else mscale, accum_out=k.den[:, i, t:t + 1])
                ins.then_inc(e_ready, 1)

            def copy(i):
                act.wait_ge(pt_done, i + 1)
                if i >= 2:
                    act.wait_ge(o_done, i - 1)
                nc.scalar.copy(k.pt[:, i % 2, :, :].rearrange("p s t -> p (s t)"), k.ps[:, 3 + i % 2, :])\
                    .then_inc(pt_ready, 1)

            for i in range(heads):
                exps(i)
                if i >= 1:
                    copy(i - 1)
            copy(heads - 1)

        @blk.vector
        def _(dve):
            link = chain(k, dve, "dve")

            def maxima(i):
                dve.wait_ge(s_done, i + 1)
                src = k.ps[:, i % 3, :].rearrange("p (t n) -> p t n", t=TT)
                if i < NA:
                    if i >= 2:
                        dve.wait_ge(e_ready, i - 1)
                    link(nc.vector.tensor_tensor(k.sB[:, i % 2, :, :], src, k.bm[:, :, i, :], ALU.add))
                    src = k.sB[:, i % 2, :, :]
                link(nc.vector.tensor_reduce(k.small[:, 0:TT], src, AX.X, ALU.max))
                nc.vector.tensor_scalar(k.nmax[:, i, :], k.small[:, 0:TT], -1.0 if i < NA else -mscale, None, ALU.mult)\
                    .then_inc(m_ready, 1)

            def out(i):
                dve.wait_ge(o_done, i + 1)
                link(nc.vector.reciprocal(k.rden[:, i, :], k.den[:, i, :]))
                nc.vector.tensor_tensor(k.mixed[:, :, i * 64:(i + 1) * 64],
                                        k.ps[:, 5 + i % 2, 0:TT * 64].rearrange("p (t n) -> p t n", t=TT),
                                        bc(k.rden[:, i, :], 2, 64), ALU.mult).then_inc(o_out, 1)

            maxima(0)
            for i in range(heads):
                if i + 1 < heads:
                    maxima(i + 1)
                if i >= 1:
                    out(i - 1)
            out(heads - 1)


MLA_SCALE = 96 ** -0.5


def output(nc, k, a, y):
    sem = k.sem
    ssum, sroot, mn, mt, mT_ready, xs, rroot, xn_ready, xt, hT_ready = (sem(n) for n in (
        "mix_sums", "mix_roots", "mix_normed", "mix_turned", "mixT_ready", "x3_sums", "x3_root", "x3_normed",
        "x3_turned", "h3T_ready"))
    sig, a_ready, stored, y_ready = sem("gate_sigmoid"), sem("mlp_ready"), sem("stored"), sem("y_out")
    x, xn, mixed, hT = k.h, k.xn, k.mixed, k.hT2
    g = mixed[:, :, :].rearrange("p t (g n) -> p (t g) n", n=64)
    with k.ctx_block("output") as blk:
        @blk.sync
        def _(sp):
            load_last(k, sp, L_OUT + len(LATE), N_LAST)
            for half in range(2):
                for t in range(TT):
                    sp.wait_ge(y_ready, half * 2 + t + 1)
                    sp.dma_start(y[0, t * P:(t + 1) * P, half * 512:(half + 1) * 512],
                                 xn[:, t, half * 512:(half + 1) * 512]).then_inc(stored, 16)
            sp.wait_ge(stored, 64)

        @blk.tensor
        def _(pe):
            pe.wait_ge(mn, 1)
            transpose_tokens(nc, k, k.flat[:, 0:2048], mixed, 0, KD).then_inc(mt, 1)
            pe.wait_ge(mT_ready, 2)
            for c in range(4):
                w = last_arrived(k, pe, L_OUT + c)
                token_major(nc, k.ps[:, 4 + c, :], w, hT, KD, CH).then_inc(k.last_used, 1)
            pe.wait_ge(xn_ready, 1)
            transpose_tokens(nc, k, k.flat[:, 0:2048], xn, 0, KD).then_inc(xt, 1)
            pe.wait_ge(hT_ready, 2)
            for c in range(F2 // CH):
                for half in range(2):
                    i = L_GU + 2 * c + half
                    w = last_arrived(k, pe, i)
                    if half == 0 and c >= 2:
                        pe.wait_ge(a_ready, c - 1)
                    feature_major(nc, k.ps[:, 2 * (c % 2) + half, :], w, hT, KD, 2).then_inc(k.last_used, 1)
            for c in range(KF2 // 2):
                w = last_arrived(k, pe, L_DOWN + c)
                if c < F2 // CH:
                    pe.wait_ge(a_ready, c + 1)
                for kk in range(2):
                    for half in range(2):
                        for t in range(TT):
                            last = nc.tensor.matmul(k.ps[:, 4 + 2 * half + t, :], k.mlp[:, 2 * c + kk, t * P:(t + 1) * P],
                                                    w[:, kk, half * 512:(half + 1) * 512],
                                                    start=(c == 0 and kk == 0), stop=(c == KF2 // 2 - 1 and kk == 1))
                last.then_inc(k.last_used, 1)

        @blk.scalar
        def _(act):
            act.wait_ge(ssum, 1)
            nc.scalar.activation(k.sroot[:, 0:32], k.ss[:, 0:32], ACT.Sqrt, bias=k.eps[:, 1:2], scale=1.0 / 64)\
                .then_inc(sroot, 1)
            act.wait_ge(mt, 1)
            for m in range(4, KD):
                ins = nc.scalar.activation(hT[:, m, :], k.flat[:, m * T:(m + 1) * T], ACT.Copy,
                                           scale=k.cols[:, ROWS["onorm"] + m:ROWS["onorm"] + m + 1])
            ins.then_inc(mT_ready, 1)
            act.wait_ge(xs, 1)
            nc.scalar.activation(k.root[:, :], k.small[:, 2:4], ACT.Sqrt, bias=k.eps[:, 1:2], scale=1.0 / D)\
                .then_inc(rroot, 1)
            act.wait_ge(xt, 1)
            for m in range(4, KD):
                ins = nc.scalar.activation(hT[:, m, :], k.flat[:, m * T:(m + 1) * T], ACT.Identity,
                                           bias=k.mod[:, SHIFT2 + m:SHIFT2 + m + 1], scale=k.ada[:, KD + m:KD + m + 1])
            ins.then_inc(hT_ready, 1)
            for c in range(F2 // CH):
                act.wait_ge(k.last_used, L_GU + 2 * c + 1)
                if c >= 2:
                    act.wait_ge(a_ready, c - 1)
                nc.scalar.activation(k.sB[:, c % 2, :, :].rearrange("p t n -> p (t n)"), k.ps[:, 2 * (c % 2), :],
                                     ACT.Sigmoid).then_inc(sig, 1)

        @blk.vector
        def _(dve):
            link = chain(k, dve, "dve")
            sq = k.mixsq.rearrange("p t (g n) -> p (t g) n", n=64)
            link(nc.vector.tensor_tensor(sq, g, g, ALU.mult))
            nc.vector.tensor_reduce(k.ss[:, 0:32], sq, AX.X, ALU.add).then_inc(ssum, 1)
            dve.wait_ge(sroot, 1)
            link(nc.vector.reciprocal(k.srs[:, 0:32], k.sroot[:, 0:32]))
            nc.vector.tensor_tensor(g, g, bc(k.srs[:, 0:32], 2, 64), ALU.mult).then_inc(mn, 1)
            dve.wait_ge(mt, 1)
            for m in range(4):
                ins = nc.vector.tensor_scalar(hT[:, m, :], k.flat[:, m * T:(m + 1) * T],
                                              k.cols[:, ROWS["onorm"] + m:ROWS["onorm"] + m + 1], None, ALU.mult)
            ins.then_inc(mT_ready, 1)
            for c in range(4):
                dve.wait_ge(k.last_used, L_OUT + c + 1)
                s = slice(c * CH, (c + 1) * CH)
                ins = nc.vector.tensor_tensor(xn[:, :, s], k.ps[:, 4 + c, :].rearrange("p (t n) -> p t n", t=TT),
                                              bc(k.gB[:, 0, s], 1, TT), ALU.mult)
            link(ins)
            link(nc.vector.tensor_tensor(x[:, :, :], x[:, :, :], xn[:, :, :], ALU.add))
            link(nc.vector.tensor_tensor(xn[:, :, :], x[:, :, :], x[:, :, :], ALU.mult))
            nc.vector.tensor_reduce(k.small[:, 2:4], xn[:, :, :], AX.X, ALU.add).then_inc(xs, 1)
            dve.wait_ge(rroot, 1)
            link(nc.vector.reciprocal(k.small[:, 0:2], k.root[:, :]))
            for t in range(TT):
                ins = nc.vector.tensor_scalar(xn[:, t, :], x[:, t, :], k.small[:, t:t + 1], None, ALU.mult)
            ins.then_inc(xn_ready, 1)
            dve.wait_ge(xt, 1)
            for m in range(4):
                ins = nc.vector.tensor_scalar(hT[:, m, :], k.flat[:, m * T:(m + 1) * T], k.ada[:, KD + m:KD + m + 1],
                                              k.mod[:, SHIFT2 + m:SHIFT2 + m + 1], ALU.mult, ALU.add)
            ins.then_inc(hT_ready, 1)
            for c in range(F2 // CH):
                s = k.sB[:, c % 2, :, :].rearrange("p t n -> p (t n)")
                dve.wait_ge(sig, c + 1)
                link(nc.vector.tensor_tensor(s, s, k.ps[:, 2 * (c % 2), :], ALU.mult))
                dve.wait_ge(k.last_used, L_GU + 2 * c + 2)
                nc.vector.tensor_tensor(k.mlp[:, 2 * c:2 * c + 2, :].rearrange("p k t -> p (k t)"), s,
                                        k.ps[:, 2 * (c % 2) + 1, :], ALU.mult).then_inc(a_ready, 1)
            dve.wait_ge(k.last_used, N_LAST)
            for half in range(2):
                s = slice(half * 512, (half + 1) * 512)
                for t in range(TT):
                    link(nc.vector.tensor_tensor(xn[:, t, s], k.ps[:, 4 + 2 * half + t, :], k.gB[:, 1, s], ALU.mult))
                    nc.vector.tensor_tensor(xn[:, t, s], xn[:, t, s], x[:, t, s], ALU.add).then_inc(y_ready, 1)


def program(nc, a, y):
    with ExitStack() as whole:
        k = Kit()
        k.sem = lambda name: whole.enter_context(nc.semaphore(name))
        k.ctx_block = lambda name: nc.Block(name=name)

        def sb(name, shape, dt=F32):
            return whole.enter_context(nc.sbuf_tensor(name, shape, dt))

        k.ps = whole.enter_context(nc.psum_tensor("ps", [P, 8, 512], F32))
        k.flat = k.ps[:, :, :].rearrange("p b n -> p (b n)")
        k.ring = sb("ring", [P, SLOTS, SLOT])
        k.ident, k.ones, k.strict, k.tri, k.later, k.same = (sb(n, [P, P]) for n in (
            "ident", "ones", "strict", "tri", "later", "same"))
        k.keep, k.nkeep = sb("keep", [P, 3 * P]), sb("nkeep", [P, 3 * P])
        k.iota_i, k.iota = sb("iota_i", [P, CAP], I32), sb("iota", [P, CAP])
        k.eps = sb("eps", [P, 2])
        k.cols = sb("cols", [P, NROWS])
        k.bupT, k.bdnT = sb("bupT", [P, 2 * KF * E]), sb("bdnT", [P, KD * E])
        k.mod = sb("mod", [P, 48])
        k.small = sb("small", [P, 64])
        k.h = sb("h", [P, TT, D])
        k.krg, k.qrg = sb("krg", [P, 32]), sb("qrg", [P, 32])
        k.pos = sb("pos", [P, TT], I32)
        k.stats, k.mv = sb("stats", [P, TT, 2, 6]), sb("mv", [P, TT, 2])
        k.root, k.rstd = sb("root", [P, TT]), sb("rstd", [P, TT])
        k.chosen, k.gate, k.place = (sb(n, [P, TT, E]) for n in ("chosen", "gate", "place"))
        k.rounds = sb("rounds", [P, 1], I32)
        k.slots = k.iota

        k.first_in = [k.sem(f"first_in{i}") for i in range(EARLY)]
        k.first_used = k.sem("first_used")
        k.last_in = [k.sem(f"last_in{i}") for i in range(len(LATE))]
        k.last_used = k.sem("last_used")
        k.expert_in = [k.sem(f"expert_in{i}") for i in range(PER)]
        k.expert_used = k.sem("expert_used")
        k.bcast_in, k.late_in, k.bias_in, k.hg_turned, k.naT_ready = (k.sem(n) for n in (
            "bcast_in", "late_in", "bias_in", "hg_turned", "naT_ready"))
        k.inv = [np.float32(10000.0) ** np.float32(-i / 32) for i in range(0, 32, 2)]
        k.first, k.last = first_chunks(a), last_chunks(a)

        with ExitStack() as early:
            k.tmp = lambda name, shape, dt=F32: early.enter_context(nc.sbuf_tensor(name, shape, dt))
            k.x = k.tmp("x", [P, TT, D])
            k.xT = k.tmp("xT", [P, KD, T])
            k.rows = k.tmp("rows", [NROWS, P])
            k.sbq, k.sbk, k.osbT, k.hgs = (k.tmp(n, [P, 4, T]) for n in ("sbq", "sbk", "osbT", "hgs"))
            k.sbv, k.hgv = (k.tmp(n, [P, TT, 512]) for n in ("sbv", "hgv"))
            k.gates = k.tmp("gates", [P, 16, T])
            k.rw, k.rb = k.tmp("rw", [P, KD, E]), k.tmp("rb", [P, E])
            k.lg = k.tmp("lg", [P, TT, E])
            k.m8, k.ixf = k.tmp("m8", [P, TT, 8]), k.tmp("ixf", [P, TT, 8])
            k.ix = k.tmp("ix", [P, TT, 8], U32)
            k.gv = k.tmp("gv", [P, TT, 4])
            k.rtmp = k.tmp("rtmp", [P, 2, TT, E])
            k.b_up = k.h[0:E, :, :].rearrange("p t n -> p (t n)")
            k.b_dn = k.osbT[0:E, :, :].rearrange("p k t -> p (k t)")

            def rows_of(name, ap, extra=0):
                r = ROWS[name] + extra
                return (k.rows[r:r + ap.shape[0], 0:ap.shape[1]], ap)

            def as_rows(ap):
                return ap.rearrange("(r p) -> r p", p=P)

            k.row_loads = [
                rows_of("lb", as_rows(a["hgrn_lb_logits"][0])), rows_of("lb", as_rows(a["hgrn_lb_logits"][1]), 4),
                rows_of("hnorm", as_rows(a["hgrn_norm_g"][0])),
                rows_of("convw", a["conv_w_2"][0].rearrange("k (c p) -> (k c) p", p=P)),
                rows_of("convb", as_rows(a["conv_b_2"][0])), rows_of("onorm", as_rows(a["out_norm_g_2"][0])),
                rows_of("n1", as_rows(a["norm1_g_2"][0])), rows_of("n2", as_rows(a["norm2_g_2"][0])),
                rows_of("bada", as_rows(a["b_ada_2"][0])), rows_of("cqg", as_rows(a["mla_q_a_g_2"][0])),
                rows_of("ckvg", as_rows(a["mla_kv_a_g_2"][0])), rows_of("c", as_rows(a["c_2"][0])),
                rows_of("q96", a["mla_qn_g_2"]), rows_of("k96", a["mla_kn_g_2"]),
            ]
            for name, src in (("naq", a["na_q_g_2"]), ("nak", a["na_k_g_2"])):
                r = ROWS[name]
                k.row_loads += [(k.rows[r:r + 1, 0:64], src), (k.rows[r:r + 1, 64:128], src)]
            k.n_rows = len(k.row_loads)
            k.broadcasts = [(k.rw[:, :, :], a["router_w"][0].rearrange("(k p) e -> p k e", p=P)),
                            (k.rb[:, :], a["router_b"][0:1, :].to_broadcast([P, E])),
                            (k.krg[:, :], a["mla_kr_g_2"][0:1, :].to_broadcast([P, 32])),
                            (k.qrg[:, :], a["mla_qr_g_2"][0:1, :].to_broadcast([P, 32])),
                            ] + [(k.pos[:, t:t + 1], a["positions_2"][0, t * P:(t + 1) * P].rearrange("(p o) -> p o", o=1))
                                 for t in range(TT)]
            projections(nc, k, a)
            k.hgT = k.fbuf
            k.g1, k.b1 = (v[:, :, :].rearrange("p h t -> p (h t)") for v in (k.kk, k.hq))
            mixers(nc, k, a)
            branches(nc, k, a)
        with ExitStack() as late:
            def lt(name, shape, dt=F32):
                return late.enter_context(nc.sbuf_tensor(name, shape, dt))

            k.acc = lt("acc", [P, TT, D])
            k.g2, k.b2, k.bm = lt("g2", [P, D]), lt("b2", [P, D]), lt("bm", [P, TT, NA, T])
            k.late_loads = [(k.g2[:, :], a["ln2_g"][0:1, :].to_broadcast([P, D])),
                            (k.b2[:, :], a["ln2_b"][0:1, :].to_broadcast([P, D]))]
            rpb = a["na_rpb_2"]
            for t in range(TT):
                for half in range(2):
                    for h in range(NA):
                        r = 2 * t + half
                        off = (h * 15 + 7 - r) * 31 + 15 - (GW - 1)
                        src = bass.AP(rpb.tensor, off, [[1, GW], [31, 4], [1, GW]])
                        k.late_loads.append((k.bm[half * GW:(half + 1) * GW, t, h, :].rearrange("p (j w) -> p j w", j=4), src))
            with ExitStack() as middle:
                def md(name, shape):
                    return middle.enter_context(nc.sbuf_tensor(name, shape, F32))

                k.sel, k.selT = md("sel", [P, 2, TT, 2 * CAP]), md("selT", [P, T])
                k.xg, k.yT, k.y = md("xg", [P, KD, 2 * CAP]), md("yT", [P, KD, 2 * CAP]), md("y", [P, D])
                k.glu, k.lin, k.sig, k.act = (md(n, [P, KF, CAP]) for n in ("glu", "lin", "sigm", "act"))
                experts(nc, k, a)
            k.gB, k.ada, k.hT2 = lt("gB", [P, 2, D]), lt("ada", [P, 2 * KD]), lt("hT2", [P, KD, T])
            k.proj, k.conv, k.xn = lt("proj", [P, TT, 1440]), lt("conv", [P, 6, T]), lt("xn", [P, TT, D])
            k.flip = lt("flip", [P, P])
            k.naT, k.k96T = lt("naT", [P, 4, T]), lt("k96T", [P, NM, T])
            k.cu, k.cy, k.ctmp = lt("cu", [P, 2, T + 2]), lt("cy", [P, 2, T]), lt("ctmp", [P, 2, T])
            k.posf, k.ang, k.trig, k.turn = (lt(n, [P, TT] + s) for n, s in (
                ("posf", []), ("ang", [32]), ("trig", [32]), ("turn", [16])))
            k.ss, k.sroot, k.srs = (lt(n, [P, 48]) for n in ("ss", "sroot", "srs"))
            k.rope, k.rope_t = lt("rope", [P, TT, 32]), lt("rope_t", [P, TT, 32])
            k.nmax, k.den, k.rden = (lt(n, [P, NA + NM, TT]) for n in ("nmax", "den", "rden"))
            free = k.ring[:, 0:4, :].rearrange("p s n -> p (s n)")

            def view(at, n, t=None):
                v = free[:, at:at + n]
                return v if t is None else v.rearrange("p (t n) -> p t n", t=t)

            k.diag = view(0, 2 * D, 2)
            second_in(nc, k, a)
            k.kv, k.mixed, k.q96T = k.acc, k.xn, k.hT2
            k.ckT, k.qm, k.k96 = view(0, 1280, 5), view(1280, 1536, TT), view(2816, 1536, TT)
            k.sq = view(4352, 2880, TT)
            heads_in(nc, k, a)
            k.sB, k.e, k.pt = (view(n * 1024, 1024).rearrange("p (b t n) -> p b t n", b=2, t=TT) for n in range(3))
            attention(nc, k, a)
            k.mlp, k.mixsq = view(1024, KF2 * T, KF2), view(1024, 2 * D, TT)
            output(nc, k, a, y)


def kernel(**inputs):
    import concourse.bacc as bacc
    from concourse.bass_utils import run_bass_kernel_spmd

    nc = bacc.Bacc("TRN2", target_bir_lowering=False, num_devices=1)
    arrays, aps = {}, {}
    for name, value in inputs.items():
        v = np.ascontiguousarray(value)
        arrays[f"in_{name}"] = v
        aps[name] = nc.dram_tensor(f"in_{name}", v.shape, mybir.dt.from_np(v.dtype), kind="ExternalInput").ap()
    y = nc.dram_tensor("out_y", (1, T, D), F32, kind="ExternalOutput").ap()
    program(nc, aps, y)
    return run_bass_kernel_spmd(nc, [arrays], core_ids=[0]).results[0]["out_y"]
```

```python
from contextlib import ExitStack

import numpy as np

import concourse.bass as bass
from concourse import mybir

F32 = mybir.dt.float32
I32 = mybir.dt.int32
U32 = mybir.dt.uint32
ALU = mybir.AluOpType
ACT = mybir.ActivationFunctionType
AX = mybir.AxisListType

P = 128
T = 256
TT = T // P
D = 1024
KD = D // P
CH = 256
SLOTS = 12
EARLY = 6
LATE = [6, 7, 8, 9, 10, 11, 4, 5]
SLOT = 2048
ALPHA = 2.0 ** 0.25
LN_EPS = 1e-5
RMS_EPS = 1e-6

HEADS = 4
SUB = 8
CHUNK = 64
NSUB = CHUNK // SUB

E = 32
CAP = 64
ROUNDS = T // CAP
F = 1024
KF = F // P
LINKS = 8
PER = 12

NA = 4
NM = 8
KC = 16
GW = 64
F2 = 2816
KF2 = F2 // P
BIG = -1.0e30

ROWS, at = {}, 0
for name, n in (("lb", 8), ("hnorm", 4), ("convw", 6), ("convb", 2), ("onorm", 8), ("n1", 8), ("n2", 8),
                ("bada", 48), ("cqg", 3), ("ckvg", 2), ("naq", 1), ("nak", 1), ("c", 8), ("q96", 1), ("k96", 1)):
    ROWS[name] = at
    at += n
NROWS = at
ADA_COL = 0
SHIFT1, SCALE1, GATE1, SHIFT2, SCALE2, GATE2 = range(0, 48, 8)


class Kit:

    def __init__(self):
        self.chains = {}


class Factors:

    def __init__(self, A, B, C, q):
        self.A, self.B, self.C, self.q = A, B, C, q


def chain(k, eng, name):
    if name not in k.chains:
        k.chains[name] = [k.sem(f"chain_{name}"), 0]
    c = k.chains[name]

    def link(ins):
        c[1] += 1
        ins.then_inc(c[0], 1)
        eng.wait_ge(c[0], c[1])
    return link


def loop_chain(eng, sem, base, per):
    c = [0]

    def link(ins):
        c[0] += 1
        assert c[0] <= per
        ins.then_inc(sem, 1)
        eng.wait_ge(sem, base + c[0])

    def end():
        assert c[0] == per, c[0]
    return link, end


def bc(ap, axis, n):
    v = ap.unsqueeze(axis)
    s = list(v.shape)
    s[axis] = n
    return v.to_broadcast(s)


IN_ORDER = [8, 9, 6, 7, 0, 1, 2, 3, 4, 5, 10, 11, 12, 13] + list(range(14, 22))
N_IN = len(IN_ORDER)
N_ADA = 12
ADA_AFTER = {9: 1, 11: 1, 13: 1, 15: 1, 19: 1, 21: N_ADA - 5}
ADA_EARLY = 6


def first_order():
    out, pair = [], 0
    for i in range(N_IN):
        out.append(("in", i))
        for _ in range(ADA_AFTER.get(i, 0)):
            out += [("ada", 2 * pair), ("ada", 2 * pair + 1)]
            pair += 1
    assert pair == N_ADA
    return out + [("branch", c) for c in range(4)] + [("out", c) for c in range(4)]


FIRST = first_order()
N_FIRST = len(FIRST)
assert N_FIRST % EARLY == 0
PE_BRANCH = N_IN
PE_OUT = N_IN + 4
N_PE = N_IN + 8


def first_chunks(a):
    tiled = {n: a[n][0].rearrange("(k p) n -> p k n", p=P) for n in (
        "w_in", "w_ada_2", "w_branch_sb", "w_branch_hgrn", "w_out")}
    out = []
    for kind, c in FIRST:
        if kind == "branch":
            w = tiled[("w_branch_sb", "w_branch_hgrn")[c // 2]]
            out.append((w[:, :, (c % 2) * 512:(c % 2 + 1) * 512], 4, 512))
        else:
            w = tiled[{"in": "w_in", "ada": "w_ada_2", "out": "w_out"}[kind]]
            c = IN_ORDER[c] if kind == "in" else c
            out.append((w[:, :, c * CH:(c + 1) * CH], 8, CH))
    return out


def last_chunks(a):
    out = []
    w = a["w_in_2"][0].rearrange("(k p) n -> p k n", p=P)
    for c0, n in [(c * CH, CH) for c in range(5)] + [(1280, 160)] + [(1440 + c * CH, CH) for c in range(3)]:
        out.append((w[:, :, c0:c0 + n], 8, n))
    w = a["mla_w_uq_2"][0].rearrange("(k p) n -> p k n", p=P)
    for c in range(2):
        out.append((w[:, :, c * 384:(c + 1) * 384], 3, 384))
    out.append((a["mla_w_ukv_2"][0].rearrange("(k p) n -> p k n", p=P), 2, 1024))
    w = a["w_out_2"][0].rearrange("(k p) n -> p k n", p=P)
    for c in range(4):
        out.append((w[:, :, c * CH:(c + 1) * CH], 8, CH))
    w = a["w_gu_2"][0].rearrange("(k p) n -> p k n", p=P)
    for c in range(F2 // CH):
        for half in (0, F2):
            out.append((w[:, :, half + c * CH:half + (c + 1) * CH], 8, CH))
    w = a["w_down_2"][0].rearrange("(j k p) n -> j p k n", p=P, k=2)
    for c in range(KF2 // 2):
        out.append((w[c], 2, 1024))
    return out


L_UQ = 9
L_UKV = 11
L_OUT = 12
L_GU = 16
L_DOWN = 38
N_LAST = 49


def slot_first(k, i, kt, n):
    return k.ring[:, i % EARLY, 0:kt * n].rearrange("p (k n) -> p k n", k=kt)


def slot_last(k, i, kt, n):
    return k.ring[:, LATE[i % len(LATE)], 0:kt * n].rearrange("p (k n) -> p k n", k=kt)


def load_first(k, sp, lo, hi):
    for i in range(lo, min(hi, N_FIRST)):
        src, kt, n = k.first[i]
        if i >= EARLY:
            kind, c = FIRST[i - EARLY]
            if kind == "ada":
                sp.wait_ge(k.ada_step, KD * (c // 2 + 1))
            else:
                sp.wait_ge(k.first_used, {"in": 0, "branch": PE_BRANCH, "out": PE_OUT}[kind] + c + 1)
        sp.dma_start(slot_first(k, i, kt, n), src).then_inc(k.first_in[i % EARLY], 16)


def first_arrived(k, eng, kind, c):
    i = FIRST.index((kind, c))
    eng.wait_ge(k.first_in[i % EARLY], 16 * (i // EARLY + 1))
    _, kt, n = k.first[i]
    return slot_first(k, i, kt, n)


def ada_products(nc, k, dve, pair):
    slot = FIRST.index(("ada", 2 * pair)) % EARLY
    for c in range(2):
        first_arrived(k, dve, "ada", 2 * pair + c)
    w = k.ring[:, slot:slot + 2, :].rearrange("p s (k n) -> p s k n", k=KD)
    if pair >= 2:
        dve.wait_ge(k.ada_summed, pair - 1)
    for q in range(KD):
        acc = k.ada_acc[:, pair % 2, q % 2, :, :]
        if q < 2:
            ins = nc.vector.tensor_scalar(acc, w[:, :, q, :], k.cact[:, q:q + 1], None, ALU.mult)
        else:
            dve.wait_ge(k.ada_step, KD * pair + q - 1)
            ins = nc.vector.scalar_tensor_tensor(out=acc, in0=w[:, :, q, :], scalar=k.cact[:, q:q + 1], in1=acc,
                                                 op0=ALU.mult, op1=ALU.add)
        ins.then_inc(k.ada_step, 1)


def ada_sums(nc, k, pe, pair):
    pe.wait_ge(k.ada_step, KD * (pair + 1))
    for m in range(4):
        for odd in range(2):
            last = nc.tensor.matmul(k.ps[:, 6, ADA_COL + 4 * pair + m:ADA_COL + 4 * pair + m + 1],
                                    k.ada_acc[:, pair % 2, odd, m // 2, (m % 2) * P:(m % 2 + 1) * P],
                                    k.ones[:, 0:1], start=(odd == 0), stop=(odd == 1))
    last.then_inc(k.ada_summed, 1)


def load_last(k, sp, lo, hi):
    for i in range(lo, min(hi, N_LAST)):
        src, kt, n = k.last[i]
        if i >= len(LATE):
            sp.wait_ge(k.last_used, i - len(LATE) + 1)
        sp.dma_start(slot_last(k, i, kt, n), src).then_inc(k.last_in[i % len(LATE)], 16)


def last_arrived(k, pe, i):
    pe.wait_ge(k.last_in[i % len(LATE)], 16 * (i // len(LATE) + 1))
    _, kt, n = k.last[i]
    return slot_last(k, i, kt, n)


def feature_major(nc, out, w, xT, kt, m):
    for j in range(m):
        for q in range(kt):
            last = nc.tensor.matmul(out[:, j * T:(j + 1) * T], w[:, q, j * P:(j + 1) * P], xT[:, q, :],
                                    start=(q == 0), stop=(q == kt - 1))
    return last


def token_major(nc, out, w, xT, kt, n):
    for t in range(TT):
        for q in range(kt):
            last = nc.tensor.matmul(out[:, t * n:(t + 1) * n], xT[:, q, t * P:(t + 1) * P], w[:, q, :],
                                    start=(q == 0), stop=(q == kt - 1))
    return last


def transpose_tokens(nc, k, out, x, first, n):
    for j in range(n):
        for t in range(TT):
            last = nc.tensor.transpose(out[:, j * T + t * P:j * T + (t + 1) * P],
                                       x[:, t, (first + j) * P:(first + j + 1) * P], k.ident[:, :])
    return last


def projections(nc, k, a):
    sem = k.sem
    rows_in, x_in, rows_one = sem("rows_in"), sem("x_in"), sem("rows_one")
    consts = sem("consts")
    xT_done, xT_ready = sem("xT_done"), sem("xT_ready")
    col_done, cols_ready = sem("col_done"), sem("cols_ready")
    evac = sem("in_evac")
    lbd, lb_ready, f_ready, lf_ready = sem("lbd"), sem("lb_ready"), sem("f_ready"), sem("lf_ready")
    diff, expd, fac, zeroed, score = (sem(n) for n in ("hg_diff", "hg_exp", "hg_factors", "hg_zeroed", "hg_score"))
    bias_done = sem("bias_done")
    k.fbuf, k.kk, k.hq, k.sgq = (k.tmp(n, [P, HEADS, T]) for n in ("fbuf", "kk", "hq", "sgq"))
    k.bb = k.tmp("bb", [P, HEADS, T + 1])
    k.lb = k.tmp("lb", [P, 3 * HEADS])
    lb, om = k.lb[:, 0:4], k.lb[:, 4:8]
    arena = k.ring[:, EARLY:SLOTS, :].rearrange("p s n -> p (s n)")
    k.arena = arena
    k.st = arena[:, 0:HEADS * 384].rearrange("p (h n) -> p h n", h=HEADS)
    size = 2048 + 1792 + 576 + 2 * T
    bufs = []
    for b in range(2):
        o = HEADS * 384 + b * size
        bufs.append(Factors(
            A=arena[:, o:o + 2048].rearrange("p (b s t) -> p b s t", s=SUB, t=SUB),
            B=arena[:, o + 2048:o + 3840].rearrange("p (c i s) -> p c i s", c=4, i=NSUB - 1),
            C=arena[:, o + 3840:o + 4416].rearrange("p (c s) -> p c s", c=3),
            q=arena[:, o + 4416:o + 4416 + 2 * T].rearrange("p (l t) -> p l t", l=2)))
    tmpA = k.tmp("hg_tmpA", [P, 2, P])
    bank = k.ps[:, 7, :]
    jobs = {6: ("E", 0), 8: ("E", 1), 11: ("E", 2), 14: ("E", 3)}
    pe_jobs = {10: 0, 13: 1, 16: 2, 19: 3}
    ada_jobs = {8: 0, 11: 1, 14: 2, 17: 3, 20: 4}

    block = k.ctx_block("projections")
    with block as blk:
        @blk.sync
        def _(sp):
            for t in range(TT):
                sp.dma_start(k.x[:, t, :], a["x"][0, t * P:(t + 1) * P, :]).then_inc(x_in, 16)
            load_first(k, sp, 0, FIRST.index(("ada", 2 * ADA_EARLY)) + EARLY)
            for dst, src in k.broadcasts:
                sp.dma_start(dst, src).then_inc(k.bcast_in, 16)

        @blk.gpsimd
        def _(pool):
            link = chain(k, pool, "pool")
            link(nc.gpsimd.memset(k.ones[:, :], 1.0))
            link(nc.gpsimd.memset(k.ident[:, :], 0.0))
            link(nc.gpsimd.affine_select(out=k.ident[:, :], in_=k.ident[:, :], compare_op=ALU.not_equal, fill=1.0,
                                         base=0, pattern=[[-1, P]], channel_multiplier=1))
            nc.gpsimd.affine_select(out=k.strict[:, :], in_=k.ones[:, :], compare_op=ALU.is_ge, fill=0.0,
                                    base=-1, pattern=[[1, P]], channel_multiplier=-1)
            nc.gpsimd.affine_select(out=k.tri[:, :], in_=k.ones[:, :], compare_op=ALU.is_ge, fill=0.0,
                                    base=0, pattern=[[-1, P]], channel_multiplier=1)
            nc.gpsimd.affine_select(out=k.later[:, :], in_=k.ones[:, :], compare_op=ALU.is_ge, fill=0.0,
                                    base=-1, pattern=[[SUB, P // SUB], [0, SUB]], channel_multiplier=-1)
            link(nc.gpsimd.affine_select(out=k.same[:, :], in_=k.ones[:, :], compare_op=ALU.is_ge, fill=0.0,
                                         base=0, pattern=[[1, P]], channel_multiplier=-1))
            link(nc.gpsimd.affine_select(out=k.same[:, :], in_=k.same[:, :], compare_op=ALU.is_ge, fill=0.0,
                                         base=0, pattern=[[-SUB, P // SUB], [0, SUB]], channel_multiplier=1))
            for i in range(3):
                nc.gpsimd.tensor_copy(k.keep[:, i * P:(i + 1) * P], (k.ones if i == 1 else k.strict)[:, :])
            link(nc.gpsimd.iota(k.iota_i[:, :], pattern=[[1, CAP]], base=0, channel_multiplier=0))
            nc.gpsimd.tensor_copy(k.iota[:, :], k.iota_i[:, :]).then_inc(consts, 1)

        @blk.tensor
        def _(pe):
            pe.wait_ge(consts, 1)
            pe.wait_ge(x_in, 32)
            transpose_tokens(nc, k, k.flat[:, 0:2048], k.x, 0, KD).then_inc(xT_done, 1)
            pe.wait_ge(xT_ready, 2)

            def head_scores(h):
                b = bufs[h % 2]
                pe.wait_ge(fac, h + 1)
                pe.wait_ge(zeroed, h + 1)
                for tile in range(2):
                    for t in range(SUB):
                        v = b.A[:, tile * 16:(tile + 1) * 16, :, t].rearrange("p b s -> p (b s)")
                        nc.tensor.matmul(bank[:, 384 + tile * SUB + t:385 + tile * SUB + t], v, k.ones[:, 0:1],
                                         start=True, stop=True)
                for c in range(4):
                    row, col = (c % 2) * CHUNK, (0 if c < 2 else 128) + c * CHUNK
                    for i in range(1, NSUB):
                        nc.tensor.matmul(bank[row:row + CHUNK, col + i * SUB:col + (i + 1) * SUB], b.B[:, c, i - 1, :],
                                         b.q[:, 0, c * CHUNK + i * SUB:c * CHUNK + (i + 1) * SUB],
                                         start=True, stop=True)
                for c in range(1, 4):
                    n = min(c * CHUNK, P)
                    nc.tensor.matmul(bank[0:n, c * CHUNK:(c + 1) * CHUNK], b.C[:, c - 1, 0:n],
                                     b.q[:, 1, c * CHUNK:(c + 1) * CHUNK], start=True, stop=True)
                nc.tensor.matmul(bank[0:CHUNK, 320:384], b.C[:, 2, P:P + CHUNK], b.q[:, 1, 3 * CHUNK:4 * CHUNK],
                                 start=True, stop=True).then_inc(score, 1)

            for i in range(N_IN):
                w = first_arrived(k, pe, "in", i)
                if i >= 6:
                    pe.wait_ge(evac, i - 5)
                out = k.ps[:, i % 6, :]
                form = token_major if IN_ORDER[i] in (4, 5, 10, 11) else None
                last = token_major(nc, out, w, k.xT, KD, CH) if form else feature_major(nc, out, w, k.xT, KD, 2)
                last.then_inc(k.first_used, 1)
                if i == 0:
                    pe.wait_ge(rows_in, 16 * k.n_rows)
                    nc.tensor.transpose(bank[:, 0:NROWS], k.rows[:, :], k.ident[0:NROWS, 0:NROWS]).then_inc(col_done, 1)
                if i in pe_jobs:
                    head_scores(pe_jobs[i])
                if i in ada_jobs:
                    ada_sums(nc, k, pe, ada_jobs[i])
            ada_sums(nc, k, pe, ADA_EARLY - 1)
            pe.wait_ge(evac, N_IN)
            pe.wait_ge(k.bias_in, 16)
            for par in range(2):
                for m in range(KF):
                    last = nc.tensor.transpose(k.ps[:, 0, (par * 8 + m) * E:(par * 8 + m + 1) * E],
                                               k.b_up[:, m * 256 + par:(m + 1) * 256:2], k.ident[0:E, 0:E])
            last.then_inc(bias_done, 1)

        @blk.scalar
        def _(act):
            act.wait_ge(rows_one, 1)
            for dst, src in k.row_loads:
                act.dma_start(dst, src).then_inc(rows_in, 16)
            act.dma_start(k.b_up[:, :], a["expert_b_up"][0]).then_inc(k.bias_in, 16)
            link = chain(k, act, "act")
            act.wait_ge(xT_done, 1)
            nc.scalar.copy(k.xT[:, 4:8, :].rearrange("p k t -> p (k t)"), k.flat[:, 1024:2048]).then_inc(xT_ready, 1)
            act.wait_ge(lbd, 1)
            nc.scalar.activation(k.cact[:, :], k.cols[:, ROWS["c"]:ROWS["c"] + KD], ACT.Sigmoid)
            nc.scalar.activation(lb, k.lb[:, 8:12], ACT.Sigmoid).then_inc(lb_ready, 1)

            def exps(h):
                b = bufs[h % 2]
                act.wait_ge(diff, h + 1)
                for v in (b.A, b.B, b.C):
                    v = v.rearrange("p b s t -> p (b s t)") if len(v.shape) == 4 else v.rearrange("p b s -> p (b s)")
                    nc.scalar.activation(v, v, ACT.Exp)
                nc.scalar.activation(b.q, b.q, ACT.Exp).then_inc(expd, 1)

            for i, c in enumerate(IN_ORDER):
                act.wait_ge(k.first_used, i + 1)
                src = k.ps[:, i % 6, :]
                two = src.rearrange("p (m t) -> p m t", m=2)
                j = 2 * (c % 2)
                if c in (8, 9):
                    ins = nc.scalar.activation(k.fbuf[:, j:j + 2, :], two, ACT.Sigmoid)
                elif c in (6, 7):
                    nc.scalar.copy(k.hq[:, j:j + 2, :], two)
                    ins = nc.scalar.activation(k.sgq[:, j:j + 2, :], two, ACT.Sigmoid)
                elif c in (0, 1):
                    ins = nc.scalar.mul(k.sbq[:, j:j + 2, :], two, 0.125)
                elif c in (2, 3):
                    ins = nc.scalar.copy(k.sbk[:, j:j + 2, :], two)
                elif c in (4, 5):
                    ins = nc.scalar.copy(k.sbv[:, :, (c - 4) * CH:(c - 3) * CH], two)
                elif c in (10, 11):
                    ins = nc.scalar.copy(k.hgv[:, :, (c - 10) * CH:(c - 9) * CH], two)
                elif c in (12, 13):
                    ins = nc.scalar.activation(k.hgs[:, j:j + 2, :], two, ACT.Sigmoid)
                else:
                    ins = nc.scalar.activation(k.gates[:, 2 * (c - 14):2 * (c - 14) + 2, :], two, ACT.Sigmoid)
                ins.then_inc(evac, 1)
                if i == 4:
                    act.wait_ge(f_ready, 1)
                    nc.scalar.activation(k.sgq[:, :, :], k.fbuf[:, :, :], ACT.Ln).then_inc(lf_ready, 1)
                if i in jobs:
                    exps(jobs[i][1])
            act.wait_ge(bias_done, 1)
            link(nc.scalar.copy(k.bupT[:, :], k.ps[:, 0, :]))

        @blk.vector
        def _(dve):
            link = chain(k, dve, "dve")
            nc.vector.memset(k.rows[:, :], 1.0).then_inc(rows_one, 1)
            nc.vector.memset(k.bb[:, :, 0:1], 0.0)
            dve.wait_ge(consts, 1)
            nc.vector.tensor_scalar(k.nkeep[:, :], k.keep[:, :], -1.0, None, ALU.mult)
            nc.vector.memset(k.eps[:, 0:1], LN_EPS)
            link(nc.vector.memset(k.eps[:, 1:2], RMS_EPS))
            dve.wait_ge(xT_done, 1)
            nc.vector.tensor_copy(k.xT[:, 0:4, :].rearrange("p k t -> p (k t)"), k.flat[:, 0:1024]).then_inc(xT_ready, 1)
            dve.wait_ge(col_done, 1)
            nc.vector.tensor_copy(k.cols[:, :], bank[:, 0:NROWS]).then_inc(cols_ready, 1)
            dve.wait_ge(cols_ready, 1)
            nc.vector.tensor_tensor(k.lb[:, 8:12], k.cols[:, 0:4], k.cols[:, 4:8], ALU.subtract).then_inc(lbd, 1)
            dve.wait_ge(lb_ready, 1)
            nc.vector.tensor_tensor(k.cact[:, :], k.cact[:, :], k.cols[:, ROWS["c"]:ROWS["c"] + KD], ALU.mult)
            link(nc.vector.tensor_scalar(om, lb, -1.0, 1.0, ALU.mult, ALU.add))
            dve.wait_ge(evac, 4)
            for h in range(HEADS):
                ins = nc.vector.tensor_scalar(k.fbuf[:, h, :], k.fbuf[:, h, :], om[:, h:h + 1], lb[:, h:h + 1],
                                              ALU.mult, ALU.add)
            link(ins)
            link(nc.vector.tensor_tensor(k.hq[:, :, :], k.hq[:, :, :], k.sgq[:, :, :], ALU.mult))
            nc.vector.tensor_scalar(k.kk[:, :, :], k.fbuf[:, :, :], -1.0, 1.0, ALU.mult, ALU.add).then_inc(f_ready, 1)
            dve.wait_ge(lf_ready, 1)
            dve.wait_ge(f_ready, 1)
            one = k.ones[:, 0:1].to_broadcast([P, T])
            for h in range(HEADS):
                ins = nc.vector.tensor_tensor_scan(k.bb[:, h, 1:T + 1], one, k.sgq[:, h, :], 0.0, ALU.mult, ALU.add)
            link(ins)

            def diffs(h):
                b = bufs[h % 2]
                after = k.bb[:, h, 1:T + 1]
                before = k.bb[:, h, 0:T]
                small = after.rearrange("p (b s) -> p b s", s=SUB)
                nc.vector.tensor_tensor(b.A, bc(small, 2, SUB), bc(small, 3, SUB), ALU.subtract)
                for c in range(4):
                    keys = after[:, c * CHUNK:(c + 1) * CHUNK]
                    starts = before[:, c * CHUNK + SUB:(c + 1) * CHUNK:SUB]
                    nc.vector.tensor_tensor(b.B[:, c], bc(starts, 2, CHUNK), bc(keys, 1, NSUB - 1), ALU.subtract)
                starts = before[:, CHUNK:T:CHUNK]
                nc.vector.tensor_tensor(b.C, bc(starts, 2, 192), bc(after[:, 0:192], 1, 3), ALU.subtract)
                nc.vector.tensor_tensor(b.q[:, 0, :].rearrange("p (b s) -> p b s", s=SUB), small,
                                        bc(before[:, 0:T:SUB], 2, SUB), ALU.subtract)
                link(nc.vector.tensor_tensor(b.q[:, 1, :].rearrange("p (b s) -> p b s", s=CHUNK),
                                             after.rearrange("p (b s) -> p b s", s=CHUNK),
                                             bc(before[:, 0:T:CHUNK], 2, CHUNK), ALU.subtract))
                whole = arena[:, HEADS * 384 + (h % 2) * size:HEADS * 384 + (h % 2) * size + size]
                nc.vector.tensor_scalar(whole, whole, 0.0, None, ALU.min).then_inc(diff, 1)

            def factors(h):
                b = bufs[h % 2]
                key, query = k.kk[:, h, :], k.hq[:, h, :]
                dve.wait_ge(expd, h + 1)
                nc.vector.tensor_tensor(b.C, b.C, bc(key[:, 0:192], 1, 3), ALU.mult)
                for c in range(4):
                    nc.vector.tensor_tensor(b.B[:, c], b.B[:, c], bc(key[:, c * CHUNK:(c + 1) * CHUNK], 1, NSUB - 1),
                                            ALU.mult)
                link(nc.vector.tensor_tensor(b.A, b.A, bc(key.rearrange("p (b s) -> p b s", s=SUB), 3, SUB), ALU.mult))
                nc.vector.tensor_tensor(b.q, b.q, bc(query, 1, 2), ALU.mult)
                nc.vector.tensor_tensor(b.A, b.A, bc(query.rearrange("p (b s) -> p b s", s=SUB), 2, SUB),
                                        ALU.mult).then_inc(fac, 1)

            def zero():
                nc.vector.memset(bank[:, 0:384], 0.0).then_inc(zeroed, 1)

            def weights(h):
                dve.wait_ge(score, h + 1)
                for tile in range(2):
                    g = bank[:, 384 + tile * SUB:384 + (tile + 1) * SUB]
                    nc.vector.tensor_tensor(tmpA[:, tile, :].rearrange("p (b s) -> p b s", s=SUB),
                                            k.same[:, :].rearrange("p (b s) -> p b s", s=SUB), bc(g, 1, P // SUB),
                                            ALU.mult)
                    nc.vector.tensor_tensor(k.st[:, h, tile * 256:tile * 256 + P], bank[:, tile * 256:tile * 256 + P],
                                            k.later[:, :], ALU.mult)
                link(nc.vector.tensor_copy(k.st[:, h, P:2 * P], bank[:, P:2 * P]))
                for tile in range(2):
                    ins = nc.vector.tensor_tensor(k.st[:, h, tile * 256:tile * 256 + P],
                                                  k.st[:, h, tile * 256:tile * 256 + P], tmpA[:, tile, :], ALU.add)
                link(ins)

            zero()
            diffs(0)
            diffs(1)
            factors(0)
            ada_products(nc, k, dve, 0)
            ada_products(nc, k, dve, 1)
            for h in range(HEADS):
                weights(h)
                if h + 1 < HEADS:
                    zero()
                if h + 2 < HEADS:
                    diffs(h + 2)
                if h + 1 < HEADS:
                    factors(h + 1)
                ada_products(nc, k, dve, h + 2)


def mixers(nc, k, a):
    sem = k.sem
    z_done, l_ready, lk_ready, r_done, arg_ready, e_ready, w_ready, pv_done, o_evac = (sem(n) for n in (
        "sb_z", "sb_log", "sb_keep", "sb_sum", "sb_arg", "sb_exp", "sb_weights", "sb_out", "sb_evac"))
    o_done, sq_ready, ss_ready, root_ready, on_ready = (sem(n) for n in (
        "hg_out", "hg_squares", "hg_sums", "hg_root", "hg_normed"))
    el, lk, wt = (k.arena[:, HEADS * 384 * (1 + n):HEADS * 384 * (2 + n)].rearrange("p (h n) -> p h n", h=4)
                  for n in range(3))
    o = 4 * HEADS * 384
    sq = k.arena[:, o:o + 1024].rearrange("p (a n) -> p a n", n=512)
    on = k.arena[:, o + 1024:o + 2048].rearrange("p (a n) -> p a n", n=512)
    small = k.small
    ss, root, rs = small[:, 0:8], small[:, 8:16], small[:, 16:24]

    with k.ctx_block("mixers") as blk:
        @blk.sync
        def _(sp):
            load_first(k, sp, FIRST.index(("ada", 2 * ADA_EARLY)) + EARLY, FIRST.index(("branch", 0)) + EARLY)

        @blk.tensor
        def _(pe):
            def z(g):
                if g:
                    pe.wait_ge(o_evac, g)
                for b in range(4):
                    h = 4 * g + b
                    r = 64 * (h % 2)
                    q, key = k.sbq[r:r + 64, h // 2, :], k.sbk[r:r + 64, h // 2, :]
                    nc.tensor.matmul(k.ps[:, b, 0:T], key[:, 0:P], q, start=True, stop=False, skip_group_check=True)
                    last = nc.tensor.matmul(k.ps[:, b, T:T + P], key[:, P:T], q[:, P:T], start=False, stop=False,
                                            skip_group_check=True)
                last.then_inc(z_done, 1)

            def sums(g):
                pe.wait_ge(lk_ready, g + 1)
                for b in range(4):
                    nc.tensor.matmul(k.ps[:, b, 0:T], k.tri[:, :], lk[:, b, 0:T], start=False, stop=False,
                                     skip_group_check=True)
                    nc.tensor.matmul(k.ps[:, b, P:T], k.ones[:, :], lk[:, b, T:T + P], start=False, stop=False,
                                     skip_group_check=True)
                    last = nc.tensor.matmul(k.ps[:, b, T:T + P], k.tri[:, :], lk[:, b, T:T + P], start=False, stop=True,
                                            skip_group_check=True)
                last.then_inc(r_done, 1)

            def values(g):
                pe.wait_ge(w_ready, g + 1)
                for b in range(4):
                    h = 4 * g + b
                    r = 64 * (h % 2)
                    nc.tensor.matmul(k.ps[r:r + 64, b, 0:T], k.sbv[:, 0, h * 64:(h + 1) * 64], wt[:, b, 0:T],
                                     start=True, stop=False, skip_group_check=True)
                    last = nc.tensor.matmul(k.ps[r:r + 64, b, P:T], k.sbv[:, 1, h * 64:(h + 1) * 64], wt[:, b, T:T + P],
                                            start=False, stop=True, skip_group_check=True)
                last.then_inc(pv_done, 1)

            z(0)
            for h in range(HEADS):
                v = [k.hgv[:, t, h * P:(h + 1) * P] for t in range(TT)]
                nc.tensor.matmul(k.ps[:, 4, h * P:(h + 1) * P], k.st[:, h, 0:P], v[0], start=True, stop=True)
                nc.tensor.matmul(k.ps[:, 5, h * P:(h + 1) * P], k.st[:, h, P:2 * P], v[0], start=True, stop=False)
                last = nc.tensor.matmul(k.ps[:, 5, h * P:(h + 1) * P], k.st[:, h, 2 * P:3 * P], v[1],
                                        start=False, stop=True)
            last.then_inc(o_done, 1)
            ada_sums(nc, k, pe, 6)
            sums(0)
            ada_sums(nc, k, pe, 7)
            values(0)
            z(1)
            pe.wait_ge(on_ready, 1)
            transpose_tokens(nc, k, k.flat[:, 2048:3072], on, 0, HEADS).then_inc(k.hg_turned, 1)
            ada_sums(nc, k, pe, 8)
            ada_sums(nc, k, pe, 9)
            sums(1)
            ada_sums(nc, k, pe, 10)
            values(1)
            ada_sums(nc, k, pe, 11)

        @blk.scalar
        def _(act):
            link = chain(k, act, "act")

            def logs(g):
                act.wait_ge(z_done, g + 1)
                if g:
                    act.wait_ge(lk_ready, g)
                link(nc.scalar.activation(el, k.ps[:, 0:4, 0:384], ACT.Abs))
                link(nc.scalar.activation(el, el, ACT.Exp, scale=-1.0))
                nc.scalar.activation(el, el, ACT.Ln, bias=1.0).then_inc(l_ready, 1)

            def exps(g):
                act.wait_ge(arg_ready, g + 1)
                nc.scalar.activation(wt, wt, ACT.Exp).then_inc(e_ready, 1)

            logs(0)
            act.wait_ge(o_done, 1)
            nc.scalar.activation(sq, k.ps[:, 4:6, :], ACT.Square).then_inc(sq_ready, 1)
            act.wait_ge(ss_ready, 1)
            nc.scalar.activation(root, ss, ACT.Sqrt, bias=k.eps[:, 1:2], scale=1.0 / P).then_inc(root_ready, 1)
            exps(0)
            logs(1)
            exps(1)

        @blk.vector
        def _(dve):
            link = chain(k, dve, "dve")

            def keeps(g):
                dve.wait_ge(l_ready, g + 1)
                if g:
                    dve.wait_ge(r_done, g)
                link(nc.vector.scalar_tensor_tensor(out=lk, in0=k.ps[:, 0:4, 0:384], scalar=0.0, in1=el,
                                                    op0=ALU.max, op1=ALU.add))
                nc.vector.tensor_tensor(lk, lk, bc(k.nkeep[:, :], 1, 4), ALU.mult).then_inc(lk_ready, 1)

            def args(g):
                dve.wait_ge(r_done, g + 1)
                if g:
                    dve.wait_ge(pv_done, g)
                nc.vector.tensor_scalar(wt, k.ps[:, 0:4, 0:384], 0.0, None, ALU.min).then_inc(arg_ready, 1)

            def weights(g):
                dve.wait_ge(e_ready, g + 1)
                nc.vector.tensor_tensor(wt, wt, bc(k.keep[:, :], 1, 4), ALU.mult).then_inc(w_ready, 1)

            def out(g):
                dve.wait_ge(pv_done, g + 1)
                for odd in range(2):
                    r = slice(64 * odd, 64 * odd + 64)
                    ins = nc.vector.tensor_copy(k.osbT[r, 2 * g:2 * g + 2, :], k.ps[r, odd:4:2, 0:T])
                ins.then_inc(o_evac, 1)

            ada_products(nc, k, dve, 6)
            ada_products(nc, k, dve, 7)
            keeps(0)
            dve.wait_ge(sq_ready, 1)
            nc.vector.tensor_reduce(ss, sq.rearrange("p a (h n) -> p (a h) n", n=P), AX.X, ALU.add)\
                .then_inc(ss_ready, 1)
            args(0)
            dve.wait_ge(root_ready, 1)
            link(nc.vector.reciprocal(rs, root))
            nc.vector.tensor_tensor(on.rearrange("p a (h n) -> p (a h) n", n=P),
                                    k.ps[:, 4:6, :].rearrange("p a (h n) -> p (a h) n", n=P), bc(rs, 2, P),
                                    ALU.mult).then_inc(on_ready, 1)
            weights(0)
            ada_products(nc, k, dve, 8)
            out(0)
            ada_products(nc, k, dve, 9)
            ada_products(nc, k, dve, 10)
            keeps(1)
            args(1)
            ada_products(nc, k, dve, 11)
            weights(1)
            out(1)
            dve.wait_ge(k.ada_summed, N_ADA)
            link(nc.vector.tensor_tensor(k.mod[:, :], k.ps[:, 6, ADA_COL:ADA_COL + 48],
                                         k.cols[:, ROWS["bada"]:ROWS["bada"] + 48], ALU.add))


def norm_stats(nc, k, link, x, var_ready):
    for t in range(TT):
        for half in range(2):
            nc.vector.bn_stats(k.stats[:, t, half, :], x[:, t, half * 512:(half + 1) * 512])
    link(nc.vector.memset(k.mv[:, :, :], 0.0))
    for t in range(TT):
        ins = nc.vector.bn_aggr(k.mv[:, t, :], k.stats[:, t, :, :])
    ins.then_inc(var_ready, 1)


def norm_apply(nc, k, dve, link, x, var_ready, n_var, root_ready, n, g, b):
    dve.wait_ge(var_ready, n_var)
    dve.wait_ge(root_ready, n)
    link(nc.vector.reciprocal(k.rstd[:, :], k.root[:, :]))
    for t in range(TT):
        ins = nc.vector.tensor_scalar(x[:, t, :], x[:, t, :], k.mv[:, t, 0:1], k.rstd[:, t:t + 1],
                                      ALU.subtract, ALU.mult)
    link(ins)
    link(nc.vector.tensor_tensor(x[:, :, :], x[:, :, :], bc(g, 1, TT), ALU.mult))
    return nc.vector.tensor_tensor(x[:, :, :], x[:, :, :], bc(b, 1, TT), ALU.add)


def branches(nc, k, a):
    sem = k.sem
    hgT, merged, var, root, h_ready = (sem(n) for n in ("hgT_ready", "merged", "ln1_var", "ln1_root", "h_ready"))
    hT_done, hT_ready, log_done, negmax, expd, m_ready, pos_done = (sem(n) for n in (
        "hT_done", "hT_ready", "logits_done", "top_negmax", "top_exp", "chosen", "pos_done"))
    ln_in = sem("ln1_in")
    gates, m = k.gates, k.xT
    hT = k.gates[:, 0:8, :]
    lg, m8, ix, ixf, gv, tmp = k.lg, k.m8, k.ix, k.ixf, k.gv, k.rtmp

    with k.ctx_block("branches") as blk:
        @blk.sync
        def _(sp):
            load_first(k, sp, FIRST.index(("branch", 0)) + EARLY, N_FIRST)
            for q in range(PER):
                if q >= EARLY:
                    sp.wait_ge(k.first_used, N_PE - EARLY + (q - EARLY) + 1)
                load_expert(k, sp, a, 0, q)

        @blk.tensor
        def _(pe):
            for c in range(2):
                w = first_arrived(k, pe, "branch", c)
                feature_major(nc, k.flat[:, c * 1024:(c + 1) * 1024], w, k.osbT, 4, 4).then_inc(k.first_used, 1)
            pe.wait_ge(hgT, HEADS)
            for c in range(2):
                w = first_arrived(k, pe, "branch", 2 + c)
                feature_major(nc, k.flat[:, 2048 + c * 1024:2048 + (c + 1) * 1024], w, k.hgT, 4, 4)\
                    .then_inc(k.first_used, 1)
            pe.wait_ge(merged, 2)
            for c in range(4):
                w = first_arrived(k, pe, "out", c)
                token_major(nc, k.ps[:, c, :], w, m, KD, CH).then_inc(k.first_used, 1)
            pe.wait_ge(h_ready, 1)
            transpose_tokens(nc, k, k.flat[:, 2048:4096], k.h, 0, KD).then_inc(hT_done, 1)
            pe.wait_ge(hT_ready, 2)
            pe.wait_ge(k.bcast_in, 16 * len(k.broadcasts))
            token_major(nc, k.ps[:, 0, 0:TT * E], k.rw, hT, KD, E).then_inc(log_done, 1)
            pe.wait_ge(m_ready, 1)
            mm = k.chosen
            nc.tensor.matmul(k.ps[:, 1, 0:E], k.strict[:, :], mm[:, 0, :], start=True, stop=True)
            nc.tensor.matmul(k.ps[:, 1, E:2 * E], k.ones[:, :], mm[:, 0, :], start=True, stop=False)
            nc.tensor.matmul(k.ps[:, 1, E:2 * E], k.strict[:, :], mm[:, 1, :], start=False, stop=True)
            nc.tensor.matmul(k.ps[:, 1, 2 * E:3 * E], k.ones[:, :], mm[:, 0, :], start=True, stop=False)
            nc.tensor.matmul(k.ps[:, 1, 2 * E:3 * E], k.ones[:, :], mm[:, 1, :], start=False, stop=True)\
                .then_inc(pos_done, 1)

        @blk.scalar
        def _(act):
            act.dma_start(k.g1, a["ln1_g"][0:1, :].to_broadcast([P, D])).then_inc(ln_in, 16)
            act.dma_start(k.b1, a["ln1_b"][0:1, :].to_broadcast([P, D])).then_inc(ln_in, 16)
            act.wait_ge(var, 1)
            nc.scalar.activation(k.root[:, :], k.mv[:, :, 1], ACT.Sqrt, bias=k.eps[:, 0:1]).then_inc(root, 1)
            act.wait_ge(hT_done, 1)
            nc.scalar.copy(hT[:, 4:8, :].rearrange("p k t -> p (k t)"), k.flat[:, 3072:4096]).then_inc(hT_ready, 1)
            act.wait_ge(negmax, 1)
            for t in range(TT):
                ins = nc.scalar.activation(gv[:, t, :], m8[:, t, 0:4], ACT.Exp, bias=k.small[:, t:t + 1])
            ins.then_inc(expd, 1)

        @blk.vector
        def _(dve):
            link = chain(k, dve, "dve")
            dve.wait_ge(k.hg_turned, 1)
            for h in range(HEADS):
                nc.vector.scalar_tensor_tensor(out=k.hgT[:, h, :], in0=k.flat[:, 2048 + h * T:2048 + (h + 1) * T],
                                               scalar=k.cols[:, ROWS["hnorm"] + h:ROWS["hnorm"] + h + 1],
                                               in1=k.hgs[:, h, :], op0=ALU.mult, op1=ALU.mult).then_inc(hgT, 1)
            for c in range(2):
                f = k.flat[:, c * 1024:(c + 1) * 1024].rearrange("p (m t) -> p m t", t=T)
                g = gates[:, 4 * c:4 * c + 4, :]
                dve.wait_ge(k.first_used, PE_BRANCH + c + 1)
                link(nc.vector.tensor_tensor(g, g, f, ALU.mult))
            for c in range(2):
                f = k.flat[:, 2048 + c * 1024:2048 + (c + 1) * 1024].rearrange("p (m t) -> p m t", t=T)
                g = gates[:, 8 + 4 * c:12 + 4 * c, :]
                dve.wait_ge(k.first_used, PE_BRANCH + 2 + c + 1)
                link(nc.vector.tensor_tensor(g, g, f, ALU.mult))
                nc.vector.tensor_tensor(m[:, 4 * c:4 * c + 4, :], gates[:, 4 * c:4 * c + 4, :], g, ALU.add)\
                    .then_inc(merged, 1)
            for c in range(4):
                dve.wait_ge(k.first_used, PE_OUT + c + 1)
                s = slice(c * CH, (c + 1) * CH)
                ins = nc.vector.scalar_tensor_tensor(out=k.h[:, :, s], in0=k.x[:, :, s], scalar=ALPHA,
                                                     in1=k.ps[:, c, :].rearrange("p (t n) -> p t n", t=TT),
                                                     op0=ALU.mult, op1=ALU.add)
            link(ins)
            dve.wait_ge(k.bcast_in, 16 * len(k.broadcasts))
            dve.wait_ge(ln_in, 32)
            norm_stats(nc, k, link, k.h, var)
            norm_apply(nc, k, dve, link, k.h, var, 1, root, 1, k.g1, k.b1).then_inc(h_ready, 1)
            dve.wait_ge(hT_done, 1)
            nc.vector.tensor_copy(hT[:, 0:4, :].rearrange("p k t -> p (k t)"), k.flat[:, 2048:3072])\
                .then_inc(hT_ready, 1)
            dve.wait_ge(log_done, 1)
            link(nc.vector.tensor_tensor(lg[:, :, :], k.ps[:, 0, 0:TT * E].rearrange("p (t e) -> p t e", t=TT),
                                         bc(k.rb[:, :], 1, TT), ALU.add))
            for t in range(TT):
                ins = nc.vector.max(m8[:, t, :], lg[:, t, :])
            link(ins)
            nc.vector.tensor_scalar(k.small[:, 0:TT], m8[:, :, 0], -1.0, None, ALU.mult).then_inc(negmax, 1)
            for t in range(TT):
                ins = nc.vector.max_index(ix[:, t, :], m8[:, t, :], lg[:, t, :])
            link(ins)
            link(nc.vector.tensor_copy(ixf[:, :, :], ix[:, :, :]))
            dve.wait_ge(expd, 1)
            link(nc.vector.tensor_reduce(k.small[:, 2:4], gv[:, :, :], AX.X, ALU.add))
            link(nc.vector.reciprocal(k.small[:, 4:6], k.small[:, 2:4]))
            link(nc.vector.tensor_tensor(gv[:, :, :], gv[:, :, :], bc(k.small[:, 4:6], 2, 4), ALU.mult))
            for j in range(4):
                for t in range(TT):
                    nc.vector.tensor_scalar(tmp[:, 0, t, :], k.iota[:, 0:E], ixf[:, t, j:j + 1], None, ALU.is_equal)
                    ins = nc.vector.tensor_scalar(tmp[:, 1, t, :], k.iota[:, 0:E], ixf[:, t, j:j + 1],
                                                  gv[:, t, j:j + 1], ALU.is_equal, ALU.mult)
                link(ins)
                for n, dst in ((0, k.chosen), (1, k.gate)):
                    if j == 0:
                        ins = nc.vector.tensor_copy(dst[:, :, :], tmp[:, n])
                    else:
                        ins = nc.vector.tensor_tensor(dst[:, :, :], dst[:, :, :], tmp[:, n], ALU.add)
                if j < 3:
                    link(ins)
                else:
                    ins.then_inc(m_ready, 1)
            dve.wait_ge(pos_done, 1)
            dve.wait_ge(m_ready, 1)
            pl = k.place[:, :, 0:E]
            link(nc.vector.tensor_scalar(pl, k.ps[:, 1, 0:2 * E].rearrange("p (t e) -> p t e", t=TT), 1.0, None, ALU.add))
            link(nc.vector.tensor_tensor(pl, pl, k.chosen[:, :, :], ALU.mult))
            link(nc.vector.tensor_scalar(pl, pl, -1.0, None, ALU.add))
            nc.vector.tensor_scalar(k.place[:, :, E:E + 2], k.place[:, :, 0:2], float(-CAP), None, ALU.add)
            link(nc.vector.tensor_reduce(k.small[:, 0:1], k.ps[:, 1, 2 * E:3 * E], AX.X, ALU.max))
            for j in range(1, ROUNDS):
                ins = nc.vector.tensor_scalar(k.small[:, j:j + 1], k.small[:, 0:1], float(j * CAP), None, ALU.is_gt)
            link(ins)
            link(nc.vector.tensor_reduce(k.small[:, 4:5], k.small[:, 1:ROUNDS], AX.X, ALU.add))
            link(nc.vector.tensor_copy(k.rounds[:, :], k.small[:, 4:5]))


def load_expert(k, sp, a, e, q):
    slot = (EARLY + q) % SLOTS
    if q < 8:
        src = a["expert_w_up"][0, bass.ds(e, 1), q * P:(q + 1) * P, :].rearrange("e p n -> p (e n)")
        dst = k.ring[:, slot, :]
    else:
        j = q - 8
        src = a["expert_w_down"][0, bass.ds(e, 1), j * 256:(j + 1) * 256, :].rearrange("e (k p) n -> p (e k) n", p=P)
        dst = k.ring[:, slot, :].rearrange("p (k n) -> p k n", k=2)
    sp.dma_start(dst, src).then_inc(k.expert_in[q], 16)


def experts(nc, k, a):
    sem = k.sem
    hot_ready, gated_ready, g_done, row_ready, xt_done, xg_ready, selps_done, selT_ready = (sem(n) for n in (
        "hot_ready", "gated_ready", "gathered", "xrow_ready", "x_turned", "xg_ready", "sel_turned", "selT_ready"))
    hrow_ready, hT_done, glu_ready, sig_ready, act_ready, y_ready, sc_done, acc_done = (sem(n) for n in (
        "hrow_ready", "up_turned", "glu_ready", "sig_ready", "act_ready", "y_ready", "scattered", "acc_done"))
    gT_done, gT_ready, base_done = sem("gate_turned"), sem("gateT_ready"), sem("bias_sum_done")
    used = k.expert_used
    dchain = sem("moe_dve")
    pairs = E // 2
    up, down, turned, rows, seT = k.ps[:, 0:2, :], k.ps[:, 2, :], k.ps[:, 3:5, :], k.ps[:, 5:7, :], k.ps[:, 7, 0:T]
    scat = (up, rows)

    def extra_rounds(eng):
        return eng.value_load(k.rounds[0:1, 0:1], min_val=0, max_val=ROUNDS - 1)

    def flat(ap):
        return ap.rearrange("p a n -> p (a n)")

    with k.ctx_block("experts") as blk:
        @blk.sync
        def _(sp):
            extra = extra_rounds(sp)

            def refill(e, done):
                for q in range(PER):
                    sp.wait_ge(used, done + q + 1)
                    load_expert(k, sp, a, e, q)

            with sp.Fori(0, E - 1) as e:
                refill(e + 1, e * PER)
            with sp.If(extra > 0):
                with sp.Fori(0, extra) as r:
                    refill(0, r * (E * PER) + (E - 1) * PER)
                    with sp.Fori(0, E - 1) as e:
                        refill(e + 1, r * (E * PER) + e * PER + E * PER)
            done = extra * (E * PER)
            for i, slot in enumerate(LATE):
                src, kt, cols = k.last[i]
                q = (slot - EARLY) % SLOTS
                sp.wait_ge(used, done + (E * PER + q + 1 - PER))
                sp.dma_start(slot_last(k, i, kt, cols), src).then_inc(k.last_in[i], 16)

        @blk.tensor
        def _(pe):
            extra = extra_rounds(pe)

            def gather():
                for half in range(2):
                    for t in range(TT):
                        last = nc.tensor.matmul(rows[:, half, :], k.sel[:, 0, t, :],
                                                k.h[:, t, half * 512:(half + 1) * 512], start=(t == 0), stop=(t == TT - 1))
                last.then_inc(g_done, 1)

            def turn_rows():
                for q in range(KD):
                    last = nc.tensor.transpose(flat(rows)[:, q * P:(q + 1) * P], k.xrow[:, q * P:(q + 1) * P],
                                               k.ident[:, :])
                last.then_inc(xt_done, 1)

            def scatter():
                for t, out in enumerate(scat):
                    for half in range(2):
                        last = nc.tensor.matmul(out[:, half, :], k.selT[:, t * P:(t + 1) * P],
                                                k.y[:, half * 512:(half + 1) * 512], start=True, stop=True)
                    last.then_inc(sc_done, 1)

            def arrivals(q, h):
                return 16 * (h + 1) + (0 if q < SLOTS - EARLY else 16 * (N_FIRST // EARLY))

            for t in range(TT):
                last = nc.tensor.transpose(k.ps[0:E, 7, t * P:(t + 1) * P], k.gate[:, t, :], k.ident[:, :])
            last.then_inc(gT_done, 1)
            pe.wait_ge(hot_ready, 1)
            gather()
            pe.wait_ge(gT_ready, 1)
            pe.wait_ge(k.late_in, 16 * len(k.late_loads))
            for t, out in enumerate((up, turned)):
                for half in range(2):
                    last = nc.tensor.matmul(out[:, half, :], k.gateT[0:E, t * P:(t + 1) * P],
                                            k.b_dn[:, half * 512:(half + 1) * 512], start=True, stop=True)
            last.then_inc(base_done, 1)
            pe.wait_ge(row_ready, 1)
            turn_rows()
            pe.wait_ge(acc_done, 2)
            with pe.Fori(0, extra + 1) as r, pe.Fori(0, pairs) as p:
                n = r * pairs + p
                pe.wait_ge(xg_ready, n + 1)
                for h in range(2):
                    if h == 1:
                        pe.wait_ge(acc_done, n * 2 + 3)
                    for q in range(KD):
                        pe.wait_ge(k.expert_in[q], n * 32 + arrivals(q, h))
                        w = k.ring[:, (EARLY + q) % SLOTS, :]
                        for u in range(2):
                            for a2 in range(2):
                                c = a2 * 1024 + u * 512
                                last = nc.tensor.matmul(up[a2 * CAP:(a2 + 1) * CAP, u, :], k.xg[:, q, h * CAP:(h + 1) * CAP],
                                                        w[:, c:c + 512], start=(q == 0), stop=(q == KD - 1),
                                                        skip_group_check=True)
                        last.then_inc(used, 1)
                    pe.wait_ge(hrow_ready, n * 2 + h + 1)
                    for par in range(2):
                        for j in range(4):
                            last = nc.tensor.transpose(turned[:, par, j * P:(j + 1) * P],
                                                       k.hrow[:, j * 256 + par:(j + 1) * 256:2], k.ident[:, :])
                    last.then_inc(hT_done, 1)
                    if h == 0:
                        pe.wait_ge(selT_ready, n + 1)
                        pe.wait_ge(y_ready, n * 2 + 1)
                        scatter()
                    else:
                        pe.wait_ge(gated_ready, n + 1)
                        for t in range(TT):
                            last = nc.tensor.transpose(seT[:, t * P:(t + 1) * P], k.sel[:, 1, t, :], k.ident[:, :])
                        last.then_inc(selps_done, 1)
                        pe.wait_ge(hot_ready, n + 2)
                        pe.wait_ge(acc_done, n * 2 + 4)
                        gather()
                        pe.wait_ge(row_ready, n + 2)
                        turn_rows()
                    pe.wait_ge(act_ready, n * 2 + h + 1)
                    pe.wait_ge(y_ready, n * 2 + h + 1)
                    for j in range(4):
                        pe.wait_ge(k.expert_in[8 + j], n * 32 + arrivals(8 + j, h))
                        w = k.ring[:, (EARLY + 8 + j) % SLOTS, :]
                        for kk in range(2):
                            m = 2 * j + kk
                            for a2 in range(2):
                                c = kk * D + a2 * 512
                                last = nc.tensor.matmul(down[a2 * CAP:(a2 + 1) * CAP, :], k.act[:, m % 4, m // 4, :],
                                                        w[:, c:c + 512], start=(m == 0), stop=(m == KF - 1),
                                                        skip_group_check=True)
                        last.then_inc(used, 1)
            pe.wait_ge(selT_ready, extra * pairs + pairs + 1)
            pe.wait_ge(y_ready, extra * (2 * pairs) + 2 * pairs + 1)
            scatter()

        @blk.scalar
        def _(act):
            for dst, src in k.late_loads:
                act.dma_start(dst, src).then_inc(k.late_in, 16)
            extra = extra_rounds(act)
            act.wait_ge(gT_done, 1)
            nc.scalar.copy(k.gateT[0:E, :], k.ps[0:E, 7, 0:T]).then_inc(gT_ready, 1)
            act.wait_ge(g_done, 1)
            nc.scalar.copy(k.xrow[:, :], flat(rows)).then_inc(row_ready, 1)
            act.wait_ge(xt_done, 1)
            nc.scalar.copy(k.xg[:, :, :].rearrange("p k n -> p (k n)"), flat(rows)).then_inc(xg_ready, 1)
            with act.Fori(0, extra + 1) as r, act.Fori(0, pairs) as p:
                n = r * pairs + p
                for h in range(2):
                    act.wait_ge(used, n * 24 + h * 12 + 8)
                    nc.scalar.copy(k.hrow[:, :], flat(up)).then_inc(hrow_ready, 1)
                    act.wait_ge(glu_ready, n * 2 + h + 1)
                    nc.scalar.activation(k.sig[:, :, :, :], k.glu[:, :, :, :], ACT.Sigmoid, scale=1.702)\
                        .then_inc(sig_ready, 1)
                    if h == 1:
                        act.wait_ge(selps_done, n + 1)
                        nc.scalar.copy(k.selT[:, :], seT).then_inc(selT_ready, 1)
                        act.wait_ge(g_done, n + 2)
                        nc.scalar.copy(k.xrow[:, :], flat(rows)).then_inc(row_ready, 1)
                        act.wait_ge(xt_done, n + 2)
                        nc.scalar.copy(k.xg[:, :, :].rearrange("p k n -> p (k n)"), flat(rows)).then_inc(xg_ready, 1)
                    act.wait_ge(used, n * 24 + h * 12 + 12)
                    for a2 in range(2):
                        ins = nc.scalar.copy(k.y[h * CAP:(h + 1) * CAP, a2 * 512:(a2 + 1) * 512],
                                             down[a2 * CAP:(a2 + 1) * CAP, :])
                    ins.then_inc(y_ready, 1)

        @blk.vector
        def _(dve):
            extra = extra_rounds(dve)

            def choose(p, gated):
                for h in range(2):
                    for t in range(TT):
                        place = k.place[:, t, bass.ds(p * 2 + h, 1)]
                        g = (k.gate[:, t, bass.ds(p * 2 + h, 1)], ALU.mult) if gated else (None, ALU.bypass)
                        last = nc.vector.tensor_scalar(k.sel[:, int(gated), t, h * CAP:(h + 1) * CAP], k.slots[:, :],
                                                       place, g[0], ALU.is_equal, g[1])
                return last

            def collect(t):
                nc.vector.tensor_tensor(k.acc[:, t, :], k.acc[:, t, :], flat(scat[t]), ALU.add).then_inc(acc_done, 1)

            choose(0, False).then_inc(hot_ready, 1)
            nc.vector.memset(k.selT[:, :], 0.0).then_inc(selT_ready, 1)
            nc.vector.memset(k.y[:, :], 0.0).then_inc(y_ready, 1)
            dve.wait_ge(base_done, 1)
            for t, src in enumerate((up, turned)):
                nc.vector.tensor_copy(k.acc[:, t, :], flat(src)).then_inc(acc_done, 1)
            with dve.Fori(0, extra + 1) as r:
                with dve.Fori(0, pairs) as p:
                    n = r * pairs + p
                    link, end = loop_chain(dve, dchain, n * LINKS + r, LINKS)
                    for h in range(2):
                        e = p * 2 + h
                        b = k.bupT[:, :].rearrange("p (x a j e) -> p x j a e", x=2, a=2, e=E)[:, :, :, :, bass.ds(e, 1)]
                        wide = [P, 4, 2, CAP]
                        g, l = (turned[:, par, :].rearrange("p (j a s) -> p j a s", a=2, s=CAP) for par in range(2))
                        dve.wait_ge(hT_done, n * 2 + h + 1)
                        link(nc.vector.tensor_tensor(k.glu[:, :, :, :], g, b[:, 0].to_broadcast(wide), ALU.add))
                        nc.vector.tensor_scalar(k.glu[:, :, :, :], k.glu[:, :, :, :], 7.0, None, ALU.min)\
                            .then_inc(glu_ready, 1)
                        link(nc.vector.tensor_tensor(k.lin[:, :, :, :], l, b[:, 1].to_broadcast(wide), ALU.add))
                        link(nc.vector.tensor_scalar(k.lin[:, :, :, :], k.lin[:, :, :, :], 7.0, -7.0, ALU.min, ALU.max))
                        dve.wait_ge(glu_ready, n * 2 + h + 1)
                        link(nc.vector.scalar_tensor_tensor(out=k.lin[:, :, :, :], in0=k.lin[:, :, :, :], scalar=1.0,
                                                            in1=k.glu[:, :, :, :], op0=ALU.add, op1=ALU.mult))
                        dve.wait_ge(sig_ready, n * 2 + h + 1)
                        nc.vector.tensor_tensor(k.act[:, :, :, :], k.lin[:, :, :, :], k.sig[:, :, :, :], ALU.mult)\
                            .then_inc(act_ready, 1)
                        if h == 0:
                            for t in range(TT):
                                dve.wait_ge(sc_done, n * 2 + t + 1)
                                dve.wait_ge(acc_done, n * 2 + t + 1)
                                collect(t)
                            choose(p, True).then_inc(gated_ready, 1)
                            choose(p + 1, False).then_inc(hot_ready, 1)
                    end()
                nc.vector.tensor_scalar(k.slots[:, :], k.slots[:, :], float(CAP), None, ALU.add).then_inc(dchain, 1)
                dve.wait_ge(dchain, (r + 1) * (pairs * LINKS + 1))
            for t in range(TT):
                dve.wait_ge(sc_done, extra * (2 * pairs) + (2 * pairs + t + 1))
                dve.wait_ge(acc_done, extra * (2 * pairs) + (2 * pairs + t + 1))
                collect(t)


def second_in(nc, k, a):
    sem = k.sem
    var, root, sq_done, rroot, xn_ready, xnT_done = (sem(n) for n in (
        "ln2_var", "ln2_root", "x2_squared", "x2_root", "x2_normed", "x2_turned"))
    hT_ready, evac = sem("h2T_ready"), sem("in2_evac")
    gd, gb_done = sem("gate_diag"), sem("gate_rows")
    gb_out, flip_ready, bm_done, bm_out = (sem(n) for n in ("gate_rows_out", "flip_ready", "bias_turned", "bias_out"))
    x2, xn, hT = k.h, k.xn, k.hT2
    rs = k.small[:, 0:2]
    with k.ctx_block("second_in") as blk:
        @blk.sync
        def _(sp):
            load_last(k, sp, len(LATE), L_UQ + len(LATE))

        @blk.tensor
        def _(pe):
            for n in range(2):
                pe.wait_ge(gd, n + 1)
                for m in range(KD):
                    last = nc.tensor.matmul(k.flat[:, n * D + m * P:n * D + (m + 1) * P], k.ones[:, :],
                                            k.diag[:, n, m * P:(m + 1) * P], start=True, stop=True)
                last.then_inc(gb_done, 1)
            pe.wait_ge(gb_out, 1)
            pe.wait_ge(flip_ready, 1)
            pe.wait_ge(k.late_in, 16 * len(k.late_loads))
            bias = k.bm[:, :, :, :].rearrange("p t h n -> p (t h n)")
            for b in range(4):
                last = nc.tensor.matmul(k.ps[:, b, :], k.flip[:, :], bias[:, b * 512:(b + 1) * 512], start=True, stop=True)
            last.then_inc(bm_done, 1)
            pe.wait_ge(xn_ready, 1)
            transpose_tokens(nc, k, k.flat[:, 2048:4096], xn, 0, KD).then_inc(xnT_done, 1)
            pe.wait_ge(bm_out, 1)
            pe.wait_ge(hT_ready, 2)
            for i in range(L_UQ):
                w = last_arrived(k, pe, i)
                if i >= 8:
                    pe.wait_ge(evac, i - 7)
                n = k.last[i][2]
                out = k.ps[:, i % 8, :]
                last = token_major(nc, out, w, hT, KD, n) if i < 6 else feature_major(nc, out, w, hT, KD, 2)
                last.then_inc(k.last_used, 1)

        @blk.scalar
        def _(act):
            link = chain(k, act, "act")
            act.wait_ge(gb_done, 2)
            nc.scalar.copy(k.gB[:, :, :].rearrange("p n d -> p (n d)"), k.flat[:, 0:2048]).then_inc(gb_out, 1)
            act.wait_ge(bm_done, 1)
            nc.scalar.copy(k.bm[:, :, :, :].rearrange("p t h n -> p (t h n)"), k.flat[:, 0:2048]).then_inc(bm_out, 1)
            act.wait_ge(var, 1)
            nc.scalar.activation(k.root[:, :], k.mv[:, :, 1], ACT.Sqrt, bias=k.eps[:, 0:1]).then_inc(root, 1)
            act.wait_ge(sq_done, 1)
            nc.scalar.activation(k.root[:, :], k.small[:, 2:4], ACT.Sqrt, bias=k.eps[:, 1:2], scale=1.0 / D)\
                .then_inc(rroot, 1)
            act.wait_ge(xnT_done, 1)
            for m in range(4, KD):
                ins = nc.scalar.activation(hT[:, m, :], k.flat[:, 2048 + m * T:2048 + (m + 1) * T], ACT.Identity,
                                           bias=k.mod[:, SHIFT1 + m:SHIFT1 + m + 1], scale=k.ada[:, m:m + 1])
            ins.then_inc(hT_ready, 1)
            for i in range(L_UQ):
                act.wait_ge(k.last_used, i + 1)
                n = k.last[i][2]
                src = k.ps[:, i % 8, :]
                if i < 6:
                    ins = nc.scalar.copy(k.proj[:, :, i * CH:i * CH + n],
                                         src[:, 0:TT * n].rearrange("p (t n) -> p t n", t=TT))
                else:
                    ins = nc.scalar.copy(k.conv[:, 2 * (i - 6):2 * (i - 5), :], src.rearrange("p (m t) -> p m t", m=2))
                ins.then_inc(evac, 1)

        @blk.gpsimd
        def _(pool):
            link = chain(k, pool, "pool")
            link(nc.gpsimd.memset(k.flip[:, :], 0.0))
            for half in range(2):
                v = k.flip[half * GW:(half + 1) * GW, half * GW:(half + 1) * GW]
                ins = nc.gpsimd.affine_select(out=v, in_=v, compare_op=ALU.not_equal, fill=1.0, base=-(GW - 1),
                                              pattern=[[1, GW]], channel_multiplier=1)
            ins.then_inc(flip_ready, 1)
            pool.wait_ge(bm_out, 1)
            for half in range(2):
                v = k.bm[half * GW:(half + 1) * GW, :, :, :].rearrange("p t h (j w) -> p (t h j) w", w=GW)
                left, right = v[:, :, 0:GW - KC], v[:, :, KC:GW]
                link(nc.gpsimd.affine_select(out=left, in_=left, compare_op=ALU.is_ge, fill=BIG, base=KC // 2,
                                             pattern=[[0, TT * NA * 4], [1, GW - KC]], channel_multiplier=-1))
                link(nc.gpsimd.affine_select(out=right, in_=right, compare_op=ALU.is_ge, fill=BIG,
                                             base=KC // 2 - 1 - KC, pattern=[[0, TT * NA * 4], [-1, GW - KC]],
                                             channel_multiplier=1))

        @blk.vector
        def _(dve):
            link = chain(k, dve, "dve")
            for n, row in enumerate((GATE1, GATE2)):
                for m in range(KD):
                    ins = nc.vector.tensor_scalar(k.diag[:, n, m * P:(m + 1) * P], k.ident[:, :],
                                                  k.mod[:, row + m:row + m + 1], None, ALU.mult)
                ins.then_inc(gd, 1)
            for n, (row, gain) in enumerate(((SCALE1, "n1"), (SCALE2, "n2"))):
                nc.vector.scalar_tensor_tensor(out=k.ada[:, n * KD:(n + 1) * KD], in0=k.mod[:, row:row + KD], scalar=1.0,
                                               in1=k.cols[:, ROWS[gain]:ROWS[gain] + KD], op0=ALU.add, op1=ALU.mult)
            link(nc.vector.scalar_tensor_tensor(out=x2[:, :, :], in0=k.h[:, :, :], scalar=ALPHA, in1=k.acc[:, :, :],
                                                op0=ALU.mult, op1=ALU.add))
            dve.wait_ge(k.late_in, 16 * len(k.late_loads))
            norm_stats(nc, k, link, x2, var)
            link(norm_apply(nc, k, dve, link, x2, var, 1, root, 1, k.g2[:, :], k.b2[:, :]))
            link(nc.vector.tensor_tensor(xn[:, :, :], x2[:, :, :], x2[:, :, :], ALU.mult))
            nc.vector.tensor_reduce(k.small[:, 2:4], xn[:, :, :], AX.X, ALU.add).then_inc(sq_done, 1)
            dve.wait_ge(rroot, 1)
            link(nc.vector.reciprocal(rs, k.root[:, :]))
            for t in range(TT):
                ins = nc.vector.tensor_scalar(xn[:, t, :], x2[:, t, :], rs[:, t:t + 1], None, ALU.mult)
            ins.then_inc(xn_ready, 1)
            dve.wait_ge(xnT_done, 1)
            for m in range(4):
                ins = nc.vector.tensor_scalar(hT[:, m, :], k.flat[:, 2048 + m * T:2048 + (m + 1) * T],
                                              k.ada[:, m:m + 1], k.mod[:, SHIFT1 + m:SHIFT1 + m + 1], ALU.mult, ALU.add)
            ins.then_inc(hT_ready, 1)


def group_norm(nc, link, x, sq, ss, n):
    link(nc.vector.tensor_tensor(sq, x, x, ALU.mult))
    return nc.vector.tensor_reduce(ss, sq, AX.X, ALU.add)


def heads_in(nc, k, a):
    sem = k.sem
    sums, roots, na_n, na_t, ck_n, ck_t, ck_ready = (sem(n) for n in (
        "proj_sums", "proj_roots", "na_normed", "na_turned", "lat_normed", "lat_turned", "latT_ready"))
    q_evac, msums, mroots, ang, trig, q_ready, k_ready, qt_done, qt_ready, kt_done = (sem(n) for n in (
        "mla_evac", "mla_sums", "mla_roots", "angles", "trig", "q96_ready", "k96_ready", "q96_turned", "q96_out",
        "k96_turned"))
    cv, cv_t = sem("conv_ready"), sem("conv_turned")
    proj = k.proj
    nav = proj[:, :, 0:512].rearrange("p t (g n) -> p t g n", n=64)
    ss, root, rs = k.ss, k.sroot, k.srs
    sq = k.sq
    qm, kv = k.qm, k.kv
    kr = proj[:, :, 1408:1440]
    with k.ctx_block("heads_in") as blk:
        @blk.sync
        def _(sp):
            load_last(k, sp, L_UQ + len(LATE), L_OUT + len(LATE))

        @blk.tensor
        def _(pe):
            pe.wait_ge(na_n, 1)
            transpose_tokens(nc, k, k.flat[:, 0:1024], proj[:, :, 0:512], 0, 4).then_inc(na_t, 1)
            pe.wait_ge(ck_n, 1)
            transpose_tokens(nc, k, k.flat[:, 1024:2304], proj[:, :, 768:1408], 0, 5).then_inc(ck_t, 1)
            pe.wait_ge(ck_ready, 1)
            pe.wait_ge(k.naT_ready, 1)
            for c in range(2):
                w = last_arrived(k, pe, L_UQ + c)
                for t in range(TT):
                    b = (5 + 2 * c + t) % 8
                    for q in range(3):
                        last = nc.tensor.matmul(k.ps[:, b, 0:384], k.ckT[:, q, t * P:(t + 1) * P], w[:, q, :],
                                                start=(q == 0), stop=(q == 2))
                last.then_inc(k.last_used, 1)
            w = last_arrived(k, pe, L_UKV)
            for t in range(TT):
                for half in range(2):
                    for q in range(2):
                        last = nc.tensor.matmul(k.ps[:, 1 + 2 * t + half, :], k.ckT[:, 3 + q, t * P:(t + 1) * P],
                                                w[:, q, half * 512:(half + 1) * 512], start=(q == 0), stop=(q == 1))
            last.then_inc(k.last_used, 1)
            pe.wait_ge(cv, 1)
            pe.wait_ge(q_evac, 3)
            for m in range(2):
                for t in range(TT):
                    last = nc.tensor.transpose(k.ps[:, 7, t * 256 + m * P:t * 256 + (m + 1) * P],
                                               k.cy[:, m, t * P:(t + 1) * P], k.ident[:, :])
            last.then_inc(cv_t, 1)
            pe.wait_ge(q_ready, 1)
            for h in range(NM):
                for t in range(TT):
                    last = nc.tensor.transpose(k.flat[0:96, h * T + t * P:h * T + (t + 1) * P],
                                               qm[:, t, h * 96:(h + 1) * 96], k.ident[:, :])
            last.then_inc(qt_done, 1)
            pe.wait_ge(k_ready, 1)
            pe.wait_ge(qt_ready, 1)
            for h in range(NM):
                for t in range(TT):
                    last = nc.tensor.transpose(k.flat[0:96, h * T + t * P:h * T + (t + 1) * P],
                                               k.k96[:, t, h * 96:(h + 1) * 96], k.ident[:, :])
            last.then_inc(kt_done, 1)

        @blk.scalar
        def _(act):
            act.wait_ge(ang, 1)
            nc.scalar.activation(k.trig[:, :, :], k.ang[:, :, :], ACT.Sin).then_inc(trig, 1)
            act.wait_ge(sums, 1)
            nc.scalar.activation(root[:, 0:16], ss[:, 0:16], ACT.Sqrt, bias=k.eps[:, 1:2], scale=1.0 / 64)
            nc.scalar.activation(root[:, 16:18], ss[:, 16:18], ACT.Sqrt, bias=k.eps[:, 1:2], scale=1.0 / 384)
            nc.scalar.activation(root[:, 18:20], ss[:, 18:20], ACT.Sqrt, bias=k.eps[:, 1:2], scale=1.0 / 256)
            nc.scalar.activation(root[:, 20:22], ss[:, 20:22], ACT.Sqrt, bias=k.eps[:, 1:2], scale=1.0 / 32)\
                .then_inc(roots, 1)
            for c in range(2):
                act.wait_ge(k.last_used, L_UQ + c + 1)
                for t in range(TT):
                    ins = nc.scalar.copy(qm[:, t, c * 384:(c + 1) * 384], k.ps[:, (5 + 2 * c + t) % 8, 0:384])
                ins.then_inc(q_evac, 1)
            act.wait_ge(k.last_used, L_OUT)
            nc.scalar.copy(kv[:, :, :].rearrange("p t n -> p (t n)"), k.flat[:, 512:512 + 2048]).then_inc(q_evac, 1)
            act.wait_ge(msums, 1)
            nc.scalar.activation(root[:, 0:16], ss[:, 0:16], ACT.Sqrt, bias=k.eps[:, 1:2], scale=1.0 / 64)
            nc.scalar.activation(root[:, 16:32], ss[:, 16:32], ACT.Sqrt, bias=k.eps[:, 1:2], scale=1.0 / 32)
            nc.scalar.activation(root[:, 32:48], ss[:, 32:48], ACT.Sqrt, bias=k.eps[:, 1:2], scale=1.0 / 64)\
                .then_inc(mroots, 1)
            act.wait_ge(cv_t, 1)
            nc.scalar.copy(k.mixed[:, :, 768:1024], k.ps[:, 7, :].rearrange("p (t n) -> p t n", t=TT))
            act.wait_ge(qt_done, 1)
            nc.scalar.activation(k.q96T[0:96, :, :].rearrange("p h t -> p (h t)"), k.flat[0:96, 0:2048], ACT.Copy,
                                 scale=k.cols[0:96, ROWS["q96"]:ROWS["q96"] + 1]).then_inc(qt_ready, 1)
            act.wait_ge(kt_done, 1)
            link = chain(k, act, "act")
            link(nc.scalar.activation(k.k96T[0:96, :, :].rearrange("p h t -> p (h t)"), k.flat[0:96, 0:2048], ACT.Copy,
                                      scale=k.cols[0:96, ROWS["k96"]:ROWS["k96"] + 1]))

        @blk.gpsimd
        def _(pool):
            link = chain(k, pool, "pool")
            u, y = k.cu, k.cy
            nc.gpsimd.memset(u[:, :, 0:1], 0.0)
            nc.gpsimd.memset(u[:, :, T + 1:T + 2], 0.0)
            link(nc.gpsimd.tensor_tensor(u[:, :, 1:T + 1], k.conv[:, 4:6, :], k.conv[:, 0:2, :], ALU.mult))
            r = ROWS["convw"]
            for m in range(2):
                ins = nc.gpsimd.tensor_scalar(y[:, m, :], u[:, m, 1:T + 1], k.cols[:, r + 2 + m:r + 3 + m],
                                              k.cols[:, ROWS["convb"] + m:ROWS["convb"] + m + 1], ALU.mult, ALU.add)
            link(ins)
            for tap in (0, 2):
                for m in range(2):
                    ins = nc.gpsimd.tensor_scalar(k.ctmp[:, m, :], u[:, m, tap:tap + T],
                                                  k.cols[:, r + 2 * tap + m:r + 2 * tap + m + 1], None, ALU.mult)
                link(ins)
                link(nc.gpsimd.tensor_tensor(y[:, :, :], y[:, :, :], k.ctmp[:, :, :], ALU.add))
            nc.gpsimd.tensor_tensor(y[:, :, :], y[:, :, :], k.conv[:, 2:4, :], ALU.mult).then_inc(cv, 1)

        @blk.vector
        def _(dve):
            link = chain(k, dve, "dve")
            link(nc.vector.tensor_copy(k.posf[:, :], k.pos[:, :]))
            for i, f in enumerate(k.inv):
                ins = nc.vector.tensor_scalar(k.ang[:, :, i], k.posf[:, :], float(f), None, ALU.mult)
            link(ins)
            sn, cs, turn = k.ang[:, :, 0:16], k.ang[:, :, 16:32], k.turn[:, :, :]
            magic, c1 = 1.5 * 2.0 ** 23, 6.28125
            c2 = float(np.float32(2 * np.pi - c1))
            link(nc.vector.tensor_scalar(turn, sn, float(1 / (2 * np.pi)), magic, ALU.mult, ALU.add))
            link(nc.vector.tensor_scalar(turn, turn, magic, None, ALU.subtract))
            link(nc.vector.scalar_tensor_tensor(out=sn, in0=turn, scalar=-c1, in1=sn, op0=ALU.mult, op1=ALU.add))
            link(nc.vector.scalar_tensor_tensor(out=sn, in0=turn, scalar=-c2, in1=sn, op0=ALU.mult, op1=ALU.add))
            link(nc.vector.tensor_scalar(turn, sn, float(np.pi / 2), float(-2 * np.pi), ALU.is_gt, ALU.mult))
            link(nc.vector.scalar_tensor_tensor(out=cs, in0=sn, scalar=float(np.pi / 2), in1=turn, op0=ALU.add,
                                                op1=ALU.add))
            lim = float(np.nextafter(np.float32(np.pi), np.float32(0)))
            nc.vector.tensor_scalar(k.ang[:, :, :], k.ang[:, :, :], lim, -lim, ALU.min, ALU.max).then_inc(ang, 1)
            link(nc.vector.tensor_tensor(sq[:, :, 0:1440], proj[:, :, :], proj[:, :, :], ALU.mult))
            for t in range(TT):
                nc.vector.tensor_reduce(ss[:, t * 8:(t + 1) * 8], sq[:, t, 0:512].rearrange("p (g n) -> p g n", n=64),
                                        AX.X, ALU.add)
            nc.vector.tensor_reduce(ss[:, 16:18], sq[:, :, 768:1152], AX.X, ALU.add)
            nc.vector.tensor_reduce(ss[:, 18:20], sq[:, :, 1152:1408], AX.X, ALU.add)
            nc.vector.tensor_reduce(ss[:, 20:22], sq[:, :, 1408:1440], AX.X, ALU.add).then_inc(sums, 1)
            dve.wait_ge(roots, 1)
            link(nc.vector.reciprocal(rs[:, 0:22], root[:, 0:22]))
            for t in range(TT):
                ins = nc.vector.tensor_tensor(nav[:, t], nav[:, t], bc(rs[:, t * 8:(t + 1) * 8], 2, 64), ALU.mult)
            ins.then_inc(na_n, 1)
            nc.vector.tensor_tensor(proj[:, :, 768:1152], proj[:, :, 768:1152], bc(rs[:, 16:18], 2, 384), ALU.mult)
            nc.vector.tensor_tensor(proj[:, :, 1152:1408], proj[:, :, 1152:1408], bc(rs[:, 18:20], 2, 256), ALU.mult)\
                .then_inc(ck_n, 1)
            link(nc.vector.tensor_tensor(kr, kr, bc(rs[:, 20:22], 2, 32), ALU.mult))
            dve.wait_ge(ck_t, 1)
            for m in range(5):
                ins = nc.vector.tensor_scalar(k.ckT[:, m, :], k.flat[:, 1024 + m * T:1024 + (m + 1) * T],
                                              k.cols[:, ROWS["cqg"] + m:ROWS["cqg"] + m + 1], None, ALU.mult)
            ins.then_inc(ck_ready, 1)
            nc.vector.tensor_scalar(k.naT[:, 0:2, :], k.flat[:, 0:512].rearrange("p (m t) -> p m t", t=T),
                                    k.cols[:, ROWS["naq"]:ROWS["naq"] + 1], 0.125, ALU.mult, ALU.mult)
            nc.vector.tensor_scalar(k.naT[:, 2:4, :], k.flat[:, 512:1024].rearrange("p (m t) -> p m t", t=T),
                                    k.cols[:, ROWS["nak"]:ROWS["nak"] + 1], None, ALU.mult).then_inc(k.naT_ready, 1)
            dve.wait_ge(trig, 1)
            sin, cos = k.trig[:, :, 0:16], k.trig[:, :, 16:32]
            ro, rt = k.rope, k.rope_t
            link(nc.vector.tensor_tensor(kr, kr, bc(k.krg[:, :], 1, TT), ALU.mult))
            nc.vector.tensor_tensor(ro[:, :, 0:16], kr[:, :, 0:16], cos, ALU.mult)
            nc.vector.tensor_tensor(rt[:, :, 0:16], kr[:, :, 16:32], sin, ALU.mult)
            nc.vector.tensor_tensor(ro[:, :, 16:32], kr[:, :, 16:32], cos, ALU.mult)
            link(nc.vector.tensor_tensor(rt[:, :, 16:32], kr[:, :, 0:16], sin, ALU.mult))
            nc.vector.tensor_tensor(ro[:, :, 0:16], ro[:, :, 0:16], rt[:, :, 0:16], ALU.subtract)
            link(nc.vector.tensor_tensor(ro[:, :, 16:32], ro[:, :, 16:32], rt[:, :, 16:32], ALU.add))
            dve.wait_ge(q_evac, 2)
            link(nc.vector.tensor_tensor(sq[:, :, 0:768], qm[:, :, :], qm[:, :, :], ALU.mult))
            for t in range(TT):
                v = sq[:, t, 0:768].rearrange("p (h n) -> p h n", n=96)
                nc.vector.tensor_reduce(ss[:, t * 8:(t + 1) * 8], v[:, :, 0:64], AX.X, ALU.add)
                ins = nc.vector.tensor_reduce(ss[:, 16 + t * 8:16 + (t + 1) * 8], v[:, :, 64:96], AX.X, ALU.add)
            dve.wait_ge(q_evac, 3)
            keys = [kv[:, t, :].rearrange("p (h n) -> p h n", n=128) for t in range(TT)]
            for t in range(TT):
                ins = nc.vector.tensor_tensor(sq[:, t, 768:1280].rearrange("p (h n) -> p h n", n=64),
                                              keys[t][:, :, 0:64], keys[t][:, :, 0:64], ALU.mult)
            link(ins)
            for t in range(TT):
                ins = nc.vector.tensor_reduce(ss[:, 32 + t * 8:32 + (t + 1) * 8],
                                              sq[:, t, 768:1280].rearrange("p (h n) -> p h n", n=64), AX.X, ALU.add)
            ins.then_inc(msums, 1)
            dve.wait_ge(mroots, 1)
            link(nc.vector.reciprocal(rs[:, 0:48], root[:, 0:48]))
            for t in range(TT):
                v = qm[:, t, :].rearrange("p (h n) -> p h n", n=96)
                nc.vector.tensor_tensor(v[:, :, 0:64], v[:, :, 0:64], bc(rs[:, t * 8:(t + 1) * 8], 2, 64), ALU.mult)
                nc.vector.tensor_tensor(v[:, :, 64:96], v[:, :, 64:96], bc(rs[:, 16 + t * 8:24 + t * 8], 2, 32), ALU.mult)
                kd = k.k96[:, t, :].rearrange("p (h n) -> p h n", n=96)
                nc.vector.tensor_tensor(kd[:, :, 0:64], keys[t][:, :, 0:64], bc(rs[:, 32 + t * 8:40 + t * 8], 2, 64),
                                        ALU.mult)
                ins = nc.vector.tensor_copy(kd[:, :, 64:96], bc(ro[:, t, :], 1, NM))
            ins.then_inc(k_ready, 1)
            dve.wait_ge(k_ready, 1)
            vs = [qm[:, t, :].rearrange("p (h n) -> p h n", n=96)[:, :, 64:96] for t in range(TT)]
            for t in range(TT):
                ins = nc.vector.tensor_tensor(vs[t], vs[t], bc(k.qrg[:, :], 1, NM), ALU.mult)
            link(ins)
            for t in range(TT):
                c, s = bc(cos[:, t, :], 1, NM), bc(sin[:, t, :], 1, NM)
                x1, x2 = vs[t][:, :, 0:16], vs[t][:, :, 16:32]
                r1, r2 = (sq[:, t, n:n + 128].rearrange("p (h n) -> p h n", n=16) for n in (0, 128))
                nc.vector.tensor_tensor(r1, x2, s, ALU.mult)
                link(nc.vector.tensor_tensor(r2, x1, s, ALU.mult))
                nc.vector.tensor_tensor(x1, x1, c, ALU.mult)
                link(nc.vector.tensor_tensor(x2, x2, c, ALU.mult))
                nc.vector.tensor_tensor(x1, x1, r1, ALU.subtract)
                ins = nc.vector.tensor_tensor(x2, x2, r2, ALU.add)
                if t == 0:
                    link(ins)
            ins.then_inc(q_ready, 1)


def attention(nc, k, a):
    sem = k.sem
    s_done, m_ready, e_ready, pt_done, pt_ready, o_done, o_out = (sem(n) for n in (
        "att_scores", "att_max", "att_exp", "att_turned", "att_weights", "att_values", "att_out"))
    heads = NA + NM
    mscale = float(MLA_SCALE)
    with k.ctx_block("attention") as blk:
        @blk.tensor
        def _(pe):
            def scores(i):
                if i >= 3:
                    pe.wait_ge(e_ready, i - 2)
                for t in range(TT):
                    if i < NA:
                        r = 64 * (i % 2)
                        q, key = k.naT[r:r + 64, i // 2, :], k.naT[r:r + 64, 2 + i // 2, :]
                    else:
                        q, key = k.q96T[0:96, i - NA, :], k.k96T[0:96, i - NA, :]
                    last = nc.tensor.matmul(k.ps[:, i % 3, t * T:(t + 1) * T], q[:, t * P:(t + 1) * P], key,
                                            start=True, stop=True)
                last.then_inc(s_done, 1)

            def turn(i):
                pe.wait_ge(e_ready, i + 1)
                if i >= 2:
                    pe.wait_ge(pt_ready, i - 1)
                for s in range(TT):
                    for t in range(TT):
                        last = nc.tensor.transpose(k.ps[:, 3 + i % 2, s * T + t * P:s * T + (t + 1) * P],
                                                   k.e[:, i % 2, t, s * P:(s + 1) * P], k.ident[:, :])
                last.then_inc(pt_done, 1)

            def values(i):
                pe.wait_ge(pt_ready, i + 1)
                if i >= 2:
                    pe.wait_ge(o_out, i - 1)
                for t in range(TT):
                    for s in range(TT):
                        v = k.proj[:, s, 512 + 64 * i:576 + 64 * i] if i < NA else \
                            k.kv[:, s, (i - NA) * 128 + 64:(i - NA) * 128 + 128]
                        last = nc.tensor.matmul(k.ps[:, 5 + i % 2, t * 64:(t + 1) * 64], k.pt[:, i % 2, s, t * P:(t + 1) * P],
                                                v, start=(s == 0), stop=(s == 1))
                last.then_inc(o_done, 1)

            scores(0)
            scores(1)
            for i in range(heads):
                if i + 2 < heads:
                    scores(i + 2)
                turn(i)
                if i >= 1:
                    values(i - 1)
            values(heads - 1)

        @blk.scalar
        def _(act):
            def exps(i):
                act.wait_ge(m_ready, i + 1)
                if i >= 2:
                    act.wait_ge(pt_done, i - 1)
                for t in range(TT):
                    src = k.sB[:, i % 2, t, :] if i < NA else k.ps[:, i % 3, t * T:(t + 1) * T]
                    ins = nc.scalar.activation(k.e[:, i % 2, t, :], src, ACT.Exp, bias=k.nmax[:, i, t:t + 1],
                                               scale=1.0 if i < NA else mscale, accum_out=k.den[:, i, t:t + 1])
                ins.then_inc(e_ready, 1)

            def copy(i):
                act.wait_ge(pt_done, i + 1)
                if i >= 2:
                    act.wait_ge(o_done, i - 1)
                nc.scalar.copy(k.pt[:, i % 2, :, :].rearrange("p s t -> p (s t)"), k.ps[:, 3 + i % 2, :])\
                    .then_inc(pt_ready, 1)

            for i in range(heads):
                exps(i)
                if i >= 1:
                    copy(i - 1)
            copy(heads - 1)

        @blk.vector
        def _(dve):
            link = chain(k, dve, "dve")

            def maxima(i):
                dve.wait_ge(s_done, i + 1)
                src = k.ps[:, i % 3, :].rearrange("p (t n) -> p t n", t=TT)
                if i < NA:
                    if i >= 2:
                        dve.wait_ge(e_ready, i - 1)
                    link(nc.vector.tensor_tensor(k.sB[:, i % 2, :, :], src, k.bm[:, :, i, :], ALU.add))
                    src = k.sB[:, i % 2, :, :]
                link(nc.vector.tensor_reduce(k.small[:, 0:TT], src, AX.X, ALU.max))
                nc.vector.tensor_scalar(k.nmax[:, i, :], k.small[:, 0:TT], -1.0 if i < NA else -mscale, None, ALU.mult)\
                    .then_inc(m_ready, 1)

            def out(i):
                dve.wait_ge(o_done, i + 1)
                link(nc.vector.reciprocal(k.rden[:, i, :], k.den[:, i, :]))
                nc.vector.tensor_tensor(k.mixed[:, :, i * 64:(i + 1) * 64],
                                        k.ps[:, 5 + i % 2, 0:TT * 64].rearrange("p (t n) -> p t n", t=TT),
                                        bc(k.rden[:, i, :], 2, 64), ALU.mult).then_inc(o_out, 1)

            maxima(0)
            for i in range(heads):
                if i + 1 < heads:
                    maxima(i + 1)
                if i >= 1:
                    out(i - 1)
            out(heads - 1)


MLA_SCALE = 96 ** -0.5


def output(nc, k, a, y):
    sem = k.sem
    ssum, sroot, mn, mt, mT_ready, xs, rroot, xn_ready, xt, hT_ready = (sem(n) for n in (
        "mix_sums", "mix_roots", "mix_normed", "mix_turned", "mixT_ready", "x3_sums", "x3_root", "x3_normed",
        "x3_turned", "h3T_ready"))
    sig, a_ready, stored, y_ready = sem("gate_sigmoid"), sem("mlp_ready"), sem("stored"), sem("y_out")
    x, xn, mixed, hT = k.h, k.xn, k.mixed, k.hT2
    g = mixed[:, :, :].rearrange("p t (g n) -> p (t g) n", n=64)
    with k.ctx_block("output") as blk:
        @blk.sync
        def _(sp):
            load_last(k, sp, L_OUT + len(LATE), N_LAST)
            for half in range(2):
                for t in range(TT):
                    sp.wait_ge(y_ready, half * 2 + t + 1)
                    sp.dma_start(y[0, t * P:(t + 1) * P, half * 512:(half + 1) * 512],
                                 xn[:, t, half * 512:(half + 1) * 512]).then_inc(stored, 16)
            sp.wait_ge(stored, 64)

        @blk.tensor
        def _(pe):
            pe.wait_ge(mn, 1)
            transpose_tokens(nc, k, k.flat[:, 0:2048], mixed, 0, KD).then_inc(mt, 1)
            pe.wait_ge(mT_ready, 2)
            for c in range(4):
                w = last_arrived(k, pe, L_OUT + c)
                token_major(nc, k.ps[:, 4 + c, :], w, hT, KD, CH).then_inc(k.last_used, 1)
            pe.wait_ge(xn_ready, 1)
            transpose_tokens(nc, k, k.flat[:, 0:2048], xn, 0, KD).then_inc(xt, 1)
            pe.wait_ge(hT_ready, 2)
            for c in range(F2 // CH):
                for half in range(2):
                    i = L_GU + 2 * c + half
                    w = last_arrived(k, pe, i)
                    if half == 0 and c >= 2:
                        pe.wait_ge(a_ready, c - 1)
                    feature_major(nc, k.ps[:, 2 * (c % 2) + half, :], w, hT, KD, 2).then_inc(k.last_used, 1)
            for c in range(KF2 // 2):
                w = last_arrived(k, pe, L_DOWN + c)
                if c < F2 // CH:
                    pe.wait_ge(a_ready, c + 1)
                for kk in range(2):
                    for half in range(2):
                        for t in range(TT):
                            last = nc.tensor.matmul(k.ps[:, 4 + 2 * half + t, :], k.mlp[:, 2 * c + kk, t * P:(t + 1) * P],
                                                    w[:, kk, half * 512:(half + 1) * 512],
                                                    start=(c == 0 and kk == 0), stop=(c == KF2 // 2 - 1 and kk == 1))
                last.then_inc(k.last_used, 1)

        @blk.scalar
        def _(act):
            act.wait_ge(ssum, 1)
            nc.scalar.activation(k.sroot[:, 0:32], k.ss[:, 0:32], ACT.Sqrt, bias=k.eps[:, 1:2], scale=1.0 / 64)\
                .then_inc(sroot, 1)
            act.wait_ge(mt, 1)
            for m in range(4, KD):
                ins = nc.scalar.activation(hT[:, m, :], k.flat[:, m * T:(m + 1) * T], ACT.Copy,
                                           scale=k.cols[:, ROWS["onorm"] + m:ROWS["onorm"] + m + 1])
            ins.then_inc(mT_ready, 1)
            act.wait_ge(xs, 1)
            nc.scalar.activation(k.root[:, :], k.small[:, 2:4], ACT.Sqrt, bias=k.eps[:, 1:2], scale=1.0 / D)\
                .then_inc(rroot, 1)
            act.wait_ge(xt, 1)
            for m in range(4, KD):
                ins = nc.scalar.activation(hT[:, m, :], k.flat[:, m * T:(m + 1) * T], ACT.Identity,
                                           bias=k.mod[:, SHIFT2 + m:SHIFT2 + m + 1], scale=k.ada[:, KD + m:KD + m + 1])
            ins.then_inc(hT_ready, 1)
            for c in range(F2 // CH):
                act.wait_ge(k.last_used, L_GU + 2 * c + 1)
                if c >= 2:
                    act.wait_ge(a_ready, c - 1)
                nc.scalar.activation(k.sB[:, c % 2, :, :].rearrange("p t n -> p (t n)"), k.ps[:, 2 * (c % 2), :],
                                     ACT.Sigmoid).then_inc(sig, 1)

        @blk.vector
        def _(dve):
            link = chain(k, dve, "dve")
            sq = k.mixsq.rearrange("p t (g n) -> p (t g) n", n=64)
            link(nc.vector.tensor_tensor(sq, g, g, ALU.mult))
            nc.vector.tensor_reduce(k.ss[:, 0:32], sq, AX.X, ALU.add).then_inc(ssum, 1)
            dve.wait_ge(sroot, 1)
            link(nc.vector.reciprocal(k.srs[:, 0:32], k.sroot[:, 0:32]))
            nc.vector.tensor_tensor(g, g, bc(k.srs[:, 0:32], 2, 64), ALU.mult).then_inc(mn, 1)
            dve.wait_ge(mt, 1)
            for m in range(4):
                ins = nc.vector.tensor_scalar(hT[:, m, :], k.flat[:, m * T:(m + 1) * T],
                                              k.cols[:, ROWS["onorm"] + m:ROWS["onorm"] + m + 1], None, ALU.mult)
            ins.then_inc(mT_ready, 1)
            for c in range(4):
                dve.wait_ge(k.last_used, L_OUT + c + 1)
                s = slice(c * CH, (c + 1) * CH)
                ins = nc.vector.tensor_tensor(xn[:, :, s], k.ps[:, 4 + c, :].rearrange("p (t n) -> p t n", t=TT),
                                              bc(k.gB[:, 0, s], 1, TT), ALU.mult)
            link(ins)
            link(nc.vector.tensor_tensor(x[:, :, :], x[:, :, :], xn[:, :, :], ALU.add))
            link(nc.vector.tensor_tensor(xn[:, :, :], x[:, :, :], x[:, :, :], ALU.mult))
            nc.vector.tensor_reduce(k.small[:, 2:4], xn[:, :, :], AX.X, ALU.add).then_inc(xs, 1)
            dve.wait_ge(rroot, 1)
            link(nc.vector.reciprocal(k.small[:, 0:2], k.root[:, :]))
            for t in range(TT):
                ins = nc.vector.tensor_scalar(xn[:, t, :], x[:, t, :], k.small[:, t:t + 1], None, ALU.mult)
            ins.then_inc(xn_ready, 1)
            dve.wait_ge(xt, 1)
            for m in range(4):
                ins = nc.vector.tensor_scalar(hT[:, m, :], k.flat[:, m * T:(m + 1) * T], k.ada[:, KD + m:KD + m + 1],
                                              k.mod[:, SHIFT2 + m:SHIFT2 + m + 1], ALU.mult, ALU.add)
            ins.then_inc(hT_ready, 1)
            for c in range(F2 // CH):
                s = k.sB[:, c % 2, :, :].rearrange("p t n -> p (t n)")
                dve.wait_ge(sig, c + 1)
                link(nc.vector.tensor_tensor(s, s, k.ps[:, 2 * (c % 2), :], ALU.mult))
                dve.wait_ge(k.last_used, L_GU + 2 * c + 2)
                nc.vector.tensor_tensor(k.mlp[:, 2 * c:2 * c + 2, :].rearrange("p k t -> p (k t)"), s,
                                        k.ps[:, 2 * (c % 2) + 1, :], ALU.mult).then_inc(a_ready, 1)
            dve.wait_ge(k.last_used, N_LAST)
            for half in range(2):
                s = slice(half * 512, (half + 1) * 512)
                for t in range(TT):
                    link(nc.vector.tensor_tensor(xn[:, t, s], k.ps[:, 4 + 2 * half + t, :], k.gB[:, 1, s], ALU.mult))
                    nc.vector.tensor_tensor(xn[:, t, s], xn[:, t, s], x[:, t, s], ALU.add).then_inc(y_ready, 1)


def program(nc, a, y):
    with ExitStack() as whole:
        k = Kit()
        k.sem = lambda name: whole.enter_context(nc.semaphore(name))
        k.ctx_block = lambda name: nc.Block(name=name)

        def sb(name, shape, dt=F32):
            return whole.enter_context(nc.sbuf_tensor(name, shape, dt))

        k.ps = whole.enter_context(nc.psum_tensor("ps", [P, 8, 512], F32))
        k.flat = k.ps[:, :, :].rearrange("p b n -> p (b n)")
        k.ring = sb("ring", [P, SLOTS, SLOT])
        k.ident, k.ones, k.strict, k.tri, k.later, k.same = (sb(n, [P, P]) for n in (
            "ident", "ones", "strict", "tri", "later", "same"))
        k.keep, k.nkeep = sb("keep", [P, 3 * P]), sb("nkeep", [P, 3 * P])
        k.iota_i, k.iota = sb("iota_i", [P, CAP], I32), sb("iota", [P, CAP])
        k.eps = sb("eps", [P, 2])
        k.cols = sb("cols", [P, NROWS])
        k.bupT = sb("bupT", [P, 2 * KF * E])
        k.mod, k.cact = sb("mod", [P, 48]), sb("cact", [P, KD])
        k.small = sb("small", [P, 64])
        k.h = sb("h", [P, TT, D])
        k.krg, k.qrg = sb("krg", [P, 32]), sb("qrg", [P, 32])
        k.pos = sb("pos", [P, TT], I32)
        k.stats, k.mv = sb("stats", [P, TT, 2, 6]), sb("mv", [P, TT, 2])
        k.root, k.rstd = sb("root", [P, TT]), sb("rstd", [P, TT])
        k.chosen, k.gate = (sb(n, [P, TT, E]) for n in ("chosen", "gate"))
        k.place = sb("place", [P, TT, E + 2])
        k.rounds = sb("rounds", [P, 1], I32)
        k.slots = k.iota

        k.first_in = [k.sem(f"first_in{i}") for i in range(EARLY)]
        k.first_used, k.ada_step, k.ada_summed = (k.sem(n) for n in ("first_used", "ada_step", "ada_summed"))
        k.last_in = [k.sem(f"last_in{i}") for i in range(len(LATE))]
        k.last_used = k.sem("last_used")
        k.expert_in = [k.sem(f"expert_in{i}") for i in range(SLOTS - EARLY)] + k.first_in
        k.expert_used = k.sem("expert_used")
        k.bcast_in, k.late_in, k.bias_in, k.hg_turned, k.naT_ready = (k.sem(n) for n in (
            "bcast_in", "late_in", "bias_in", "hg_turned", "naT_ready"))
        k.inv = [np.float32(10000.0) ** np.float32(-i / 32) for i in range(0, 32, 2)]
        k.first, k.last = first_chunks(a), last_chunks(a)

        with ExitStack() as early:
            k.tmp = lambda name, shape, dt=F32: early.enter_context(nc.sbuf_tensor(name, shape, dt))
            k.x = k.tmp("x", [P, TT, D])
            k.xT = k.tmp("xT", [P, KD, T])
            k.rows = k.tmp("rows", [NROWS, P])
            k.sbq, k.sbk, k.osbT, k.hgs = (k.tmp(n, [P, 4, T]) for n in ("sbq", "sbk", "osbT", "hgs"))
            k.sbv, k.hgv = (k.tmp(n, [P, TT, 512]) for n in ("sbv", "hgv"))
            k.gates = k.tmp("gates", [P, 16, T])
            k.rw, k.rb = k.tmp("rw", [P, KD, E]), k.tmp("rb", [P, E])
            k.lg = k.tmp("lg", [P, TT, E])
            k.m8, k.ixf = k.tmp("m8", [P, TT, 8]), k.tmp("ixf", [P, TT, 8])
            k.ix = k.tmp("ix", [P, TT, 8], U32)
            k.gv = k.tmp("gv", [P, TT, 4])
            k.ada_acc = k.tmp("ada_acc", [P, 2, 2, 2, CH])
            k.rtmp = k.tmp("rtmp", [P, 2, TT, E])
            k.b_up = k.h[0:E, :, :].rearrange("p t n -> p (t n)")

            def rows_of(name, ap, extra=0):
                r = ROWS[name] + extra
                return (k.rows[r:r + ap.shape[0], 0:ap.shape[1]], ap)

            def as_rows(ap):
                return ap.rearrange("(r p) -> r p", p=P)

            k.row_loads = [
                rows_of("lb", as_rows(a["hgrn_lb_logits"][0])), rows_of("lb", as_rows(a["hgrn_lb_logits"][1]), 4),
                rows_of("hnorm", as_rows(a["hgrn_norm_g"][0])),
                rows_of("convw", a["conv_w_2"][0].rearrange("k (c p) -> (k c) p", p=P)),
                rows_of("convb", as_rows(a["conv_b_2"][0])), rows_of("onorm", as_rows(a["out_norm_g_2"][0])),
                rows_of("n1", as_rows(a["norm1_g_2"][0])), rows_of("n2", as_rows(a["norm2_g_2"][0])),
                rows_of("bada", as_rows(a["b_ada_2"][0])), rows_of("cqg", as_rows(a["mla_q_a_g_2"][0])),
                rows_of("ckvg", as_rows(a["mla_kv_a_g_2"][0])), rows_of("c", as_rows(a["c_2"][0])),
                rows_of("q96", a["mla_qn_g_2"]), rows_of("k96", a["mla_kn_g_2"]),
            ]
            for name, src in (("naq", a["na_q_g_2"]), ("nak", a["na_k_g_2"])):
                r = ROWS[name]
                k.row_loads += [(k.rows[r:r + 1, 0:64], src), (k.rows[r:r + 1, 64:128], src)]
            k.n_rows = len(k.row_loads)
            k.broadcasts = [(k.rw[:, :, :], a["router_w"][0].rearrange("(k p) e -> p k e", p=P)),
                            (k.rb[:, :], a["router_b"][0:1, :].to_broadcast([P, E])),
                            (k.krg[:, :], a["mla_kr_g_2"][0:1, :].to_broadcast([P, 32])),
                            (k.qrg[:, :], a["mla_qr_g_2"][0:1, :].to_broadcast([P, 32])),
                            ] + [(k.pos[:, t:t + 1], a["positions_2"][0, t * P:(t + 1) * P].rearrange("(p o) -> p o", o=1))
                                 for t in range(TT)]
            projections(nc, k, a)
            k.hgT = k.fbuf
            k.g1, k.b1 = (v[:, :, :].rearrange("p h t -> p (h t)") for v in (k.kk, k.hq))
            mixers(nc, k, a)
            branches(nc, k, a)
        with ExitStack() as late:
            def lt(name, shape, dt=F32):
                return late.enter_context(nc.sbuf_tensor(name, shape, dt))

            k.acc = lt("acc", [P, TT, D])
            k.g2, k.b2, k.bm = lt("g2", [P, D]), lt("b2", [P, D]), lt("bm", [P, TT, NA, T])
            k.late_loads = [(k.g2[:, :], a["ln2_g"][0:1, :].to_broadcast([P, D])),
                            (k.b2[:, :], a["ln2_b"][0:1, :].to_broadcast([P, D]))]
            rpb = a["na_rpb_2"]
            for t in range(TT):
                for half in range(2):
                    for h in range(NA):
                        r = 2 * t + half
                        off = (h * 15 + 7 - r) * 31 + 15 - (GW - 1)
                        src = bass.AP(rpb.tensor, off, [[1, GW], [31, 4], [1, GW]])
                        k.late_loads.append((k.bm[half * GW:(half + 1) * GW, t, h, :].rearrange("p (j w) -> p j w", j=4), src))
            with ExitStack() as middle:
                def md(name, shape):
                    return middle.enter_context(nc.sbuf_tensor(name, shape, F32))

                k.sel, k.selT = md("sel", [P, 2, TT, 2 * CAP]), md("selT", [P, T])
                k.xg, k.y = md("xg", [P, KD, 2 * CAP]), md("y", [P, D])
                k.xrow, k.hrow = md("xrow", [P, D]), md("hrow", [P, D])
                k.gateT, k.b_dn = md("gateT", [E, T]), md("b_dn", [E, D])
                k.late_loads.append((k.b_dn[:, :], a["expert_b_down"][0]))
                k.glu, k.lin, k.sig, k.act = (md(n, [P, 4, 2, CAP]) for n in ("glu", "lin", "sigm", "act"))
                experts(nc, k, a)
            k.gB, k.ada, k.hT2 = lt("gB", [P, 2, D]), lt("ada", [P, 2 * KD]), lt("hT2", [P, KD, T])
            k.proj, k.conv, k.xn = lt("proj", [P, TT, 1440]), lt("conv", [P, 6, T]), lt("xn", [P, TT, D])
            k.flip = lt("flip", [P, P])
            k.naT, k.k96T = lt("naT", [P, 4, T]), lt("k96T", [P, NM, T])
            k.cu, k.cy, k.ctmp = lt("cu", [P, 2, T + 2]), lt("cy", [P, 2, T]), lt("ctmp", [P, 2, T])
            k.posf, k.ang, k.trig, k.turn = (lt(n, [P, TT] + s) for n, s in (
                ("posf", []), ("ang", [32]), ("trig", [32]), ("turn", [16])))
            k.ss, k.sroot, k.srs = (lt(n, [P, 48]) for n in ("ss", "sroot", "srs"))
            k.rope, k.rope_t = lt("rope", [P, TT, 32]), lt("rope_t", [P, TT, 32])
            k.nmax, k.den, k.rden = (lt(n, [P, NA + NM, TT]) for n in ("nmax", "den", "rden"))
            free = k.ring[:, 0:4, :].rearrange("p s n -> p (s n)")

            def view(at, n, t=None):
                v = free[:, at:at + n]
                return v if t is None else v.rearrange("p (t n) -> p t n", t=t)

            k.diag = view(0, 2 * D, 2)
            second_in(nc, k, a)
            k.kv, k.mixed, k.q96T = k.acc, k.xn, k.hT2
            k.ckT, k.qm, k.k96 = view(0, 1280, 5), view(1280, 1536, TT), view(2816, 1536, TT)
            k.sq = view(4352, 2880, TT)
            heads_in(nc, k, a)
            k.sB, k.e, k.pt = (view(n * 1024, 1024).rearrange("p (b t n) -> p b t n", b=2, t=TT) for n in range(3))
            attention(nc, k, a)
            k.mlp, k.mixsq = view(1024, KF2 * T, KF2), view(1024, 2 * D, TT)
            output(nc, k, a, y)


def kernel(**inputs):
    import concourse.bacc as bacc
    from concourse.bass_utils import run_bass_kernel_spmd

    nc = bacc.Bacc("TRN2", target_bir_lowering=False, num_devices=1)
    arrays, aps = {}, {}
    for name, value in inputs.items():
        v = np.ascontiguousarray(value)
        arrays[f"in_{name}"] = v
        aps[name] = nc.dram_tensor(f"in_{name}", v.shape, mybir.dt.from_np(v.dtype), kind="ExternalInput").ap()
    y = nc.dram_tensor("out_y", (1, T, D), F32, kind="ExternalOutput").ap()
    program(nc, aps, y)
    return run_bass_kernel_spmd(nc, [arrays], core_ids=[0]).results[0]["out_y"]
```

```python
from contextlib import ExitStack

import numpy as np

import concourse.bass as bass
from concourse import mybir

F32 = mybir.dt.float32
I32 = mybir.dt.int32
U32 = mybir.dt.uint32
R32 = mybir.dt.float32r
HIGH = -4096
ALU = mybir.AluOpType
ACT = mybir.ActivationFunctionType
AX = mybir.AxisListType

P = 128
T = 256
TT = T // P
D = 1024
KD = D // P
CH = 256
SLOTS = 12
EARLY = 6
LATE = [6, 7, 8, 9, 10, 11, 4, 5]
SLOT = 2048
ALPHA = 2.0 ** 0.25
LN_EPS = 1e-5
RMS_EPS = 1e-6

HEADS = 4
SUB = 8
CHUNK = 64
NSUB = CHUNK // SUB

E = 32
CAP = 64
ROUNDS = T // CAP
F = 1024
KF = F // P
LINKS = 8
PER = 12

NA = 4
NM = 8
KC = 16
GW = 64
F2 = 2816
KF2 = F2 // P
BIG = -1.0e30

ROWS, at = {}, 0
for name, n in (("lb", 8), ("hnorm", 4), ("convw", 6), ("convb", 2), ("onorm", 8), ("n1", 8), ("n2", 8),
                ("bada", 48), ("cqg", 3), ("ckvg", 2), ("naq", 1), ("nak", 1), ("c", 8), ("q96", 1), ("k96", 1)):
    ROWS[name] = at
    at += n
NROWS = at
ADA_COL = 0
SHIFT1, SCALE1, GATE1, SHIFT2, SCALE2, GATE2 = range(0, 48, 8)


class Kit:

    def __init__(self):
        self.chains = {}


class Factors:

    def __init__(self, A, B, C, q):
        self.A, self.B, self.C, self.q = A, B, C, q


def act_copy(nc, out, x):
    return nc.scalar.activation(out, x, ACT.Copy)


def chain(k, eng, name):
    if name not in k.chains:
        k.chains[name] = [k.sem(f"chain_{name}"), 0]
    c = k.chains[name]

    def link(ins):
        c[1] += 1
        ins.then_inc(c[0], 1)
        eng.wait_ge(c[0], c[1])
    return link


def loop_chain(eng, sem, base, per):
    c = [0]

    def link(ins):
        c[0] += 1
        assert c[0] <= per
        ins.then_inc(sem, 1)
        eng.wait_ge(sem, base + c[0])

    def end():
        assert c[0] == per, c[0]
    return link, end


def bc(ap, axis, n):
    v = ap.unsqueeze(axis)
    s = list(v.shape)
    s[axis] = n
    return v.to_broadcast(s)


IN_ORDER = [8, 9, 6, 7, 0, 1, 2, 3, 4, 5, 10, 11, 12, 13] + list(range(14, 22))
N_IN = len(IN_ORDER)
N_ADA = 12
ADA_AFTER = {9: 1, 11: 1, 13: 1, 15: 1, 19: 1, 21: N_ADA - 5}
ADA_EARLY = 5


def first_order():
    out, pair = [], 0
    for i in range(N_IN):
        out.append(("in", i))
        for _ in range(ADA_AFTER.get(i, 0)):
            out += [("ada", 2 * pair), ("ada", 2 * pair + 1)]
            pair += 1
    assert pair == N_ADA
    return out + [("branch", c) for c in range(4)] + [("out", c) for c in range(4)]


FIRST = first_order()
N_FIRST = len(FIRST)
assert N_FIRST % EARLY == 0
PE_BRANCH = N_IN
PE_OUT = N_IN + 4
N_PE = N_IN + 8


def first_chunks(a):
    tiled = {n: a[n][0].rearrange("(k p) n -> p k n", p=P) for n in (
        "w_in", "w_ada_2", "w_branch_sb", "w_branch_hgrn", "w_out")}
    out = []
    for kind, c in FIRST:
        if kind == "branch":
            w = tiled[("w_branch_sb", "w_branch_hgrn")[c // 2]]
            out.append((w[:, :, (c % 2) * 512:(c % 2 + 1) * 512], 4, 512))
        else:
            w = tiled[{"in": "w_in", "ada": "w_ada_2", "out": "w_out"}[kind]]
            c = IN_ORDER[c] if kind == "in" else c
            out.append((w[:, :, c * CH:(c + 1) * CH], 8, CH))
    return out


def last_chunks(a):
    out = []
    w = a["w_in_2"][0].rearrange("(k p) n -> p k n", p=P)
    for c0, n in [(c * CH, CH) for c in range(5)] + [(1280, 160)] + [(1440 + c * CH, CH) for c in range(3)]:
        out.append((w[:, :, c0:c0 + n], 8, n))
    w = a["mla_w_uq_2"][0].rearrange("(k p) n -> p k n", p=P)
    for c in range(2):
        out.append((w[:, :, c * 384:(c + 1) * 384], 3, 384))
    out.append((a["mla_w_ukv_2"][0].rearrange("(k p) n -> p k n", p=P), 2, 1024))
    w = a["w_out_2"][0].rearrange("(k p) n -> p k n", p=P)
    for c in range(4):
        out.append((w[:, :, c * CH:(c + 1) * CH], 8, CH))
    w = a["w_gu_2"][0].rearrange("(k p) n -> p k n", p=P)
    for c in range(F2 // CH):
        for half in (0, F2):
            out.append((w[:, :, half + c * CH:half + (c + 1) * CH], 8, CH))
    w = a["w_down_2"][0].rearrange("(j k p) n -> j p k n", p=P, k=2)
    for c in range(KF2 // 2):
        out.append((w[c], 2, 1024))
    return out


L_UQ = 9
L_UKV = 11
L_OUT = 12
L_GU = 16
L_DOWN = 38
N_LAST = 49


def slot_first(k, i, kt, n):
    return k.ring[:, i % EARLY, 0:kt * n].rearrange("p (k n) -> p k n", k=kt)


def slot_last(k, i, kt, n):
    return k.ring[:, LATE[i % len(LATE)], 0:kt * n].rearrange("p (k n) -> p k n", k=kt)


def load_first(k, sp, lo, hi):
    for i in range(lo, min(hi, N_FIRST)):
        src, kt, n = k.first[i]
        if i >= EARLY:
            kind, c = FIRST[i - EARLY]
            if kind == "ada":
                sp.wait_ge(k.ada_step, c // 2 + 1)
            else:
                sp.wait_ge(k.first_used, {"in": 0, "branch": PE_BRANCH, "out": PE_OUT}[kind] + c + 1)
        sp.dma_start(slot_first(k, i, kt, n), src).then_inc(k.first_in[i % EARLY], 16)


def first_arrived(k, eng, kind, c):
    i = FIRST.index((kind, c))
    eng.wait_ge(k.first_in[i % EARLY], 16 * (i // EARLY + 1))
    _, kt, n = k.first[i]
    return slot_first(k, i, kt, n)


def ada_rows(nc, k, pe, pair, bank):
    slot = FIRST.index(("ada", 2 * pair)) % EARLY
    for c in range(2):
        first_arrived(k, pe, "ada", 2 * pair + c)
    if pair:
        pe.wait_ge(k.ada_copied, pair)
    w = k.ring[:, slot:slot + 2, :].rearrange("p s (k n) -> p s k n", k=KD)
    for q in range(KD):
        g = 32 * (q % 4)
        last = nc.tensor.matmul(k.ps[g:g + 32, bank, :].rearrange("p (s n) -> p s n", s=2), k.crep[:, q, :],
                                w[:, :, q, :], start=(q < 4), stop=(q >= 4), skip_group_check=True)
    last.then_inc(k.ada_step, 1)


def ada_copy(k, eng, copy, pair, bank):
    eng.wait_ge(k.ada_step, pair + 1)
    if pair >= 2:
        eng.wait_ge(k.ada_summed, pair - 1)
    copy(k.ada_acc[:, pair % 2, :], k.ps[:, bank, :]).then_inc(k.ada_copied, 1)


def ada_sums(nc, k, pe, pair):
    pe.wait_ge(k.ada_copied, pair + 1)
    for m in range(4):
        last = nc.tensor.matmul(k.ps[:, 6, ADA_COL + 4 * pair + m:ADA_COL + 4 * pair + m + 1],
                                k.ada_acc[:, pair % 2, m * P:(m + 1) * P], k.pick[:, 0:1], start=True, stop=True)
    last.then_inc(k.ada_summed, 1)


def load_last(k, sp, lo, hi):
    for i in range(lo, min(hi, N_LAST)):
        src, kt, n = k.last[i]
        if i >= len(LATE):
            sp.wait_ge(k.last_used, i - len(LATE) + 1)
        sp.dma_start(slot_last(k, i, kt, n), src).then_inc(k.last_in[i % len(LATE)], 16)


def last_arrived(k, pe, i):
    pe.wait_ge(k.last_in[i % len(LATE)], 16 * (i // len(LATE) + 1))
    _, kt, n = k.last[i]
    return slot_last(k, i, kt, n)


def feature_major(nc, out, w, xT, kt, m):
    for j in range(m):
        for q in range(kt):
            last = nc.tensor.matmul(out[:, j * T:(j + 1) * T], w[:, q, j * P:(j + 1) * P], xT[:, q, :],
                                    start=(q == 0), stop=(q == kt - 1))
    return last


def token_major(nc, out, w, xT, kt, n):
    for t in range(TT):
        for q in range(kt):
            last = nc.tensor.matmul(out[:, t * n:(t + 1) * n], xT[:, q, t * P:(t + 1) * P], w[:, q, :],
                                    start=(q == 0), stop=(q == kt - 1))
    return last


def transpose_tokens(nc, k, out, x, first, n, wait=None):
    for t in range(TT):
        if wait is not None:
            wait(t)
        for j in range(n):
            last = nc.tensor.transpose(out[:, j * T + t * P:j * T + (t + 1) * P],
                                       x[:, t, (first + j) * P:(first + j + 1) * P], k.ident[:, :])
    return last


def projections(nc, k, a):
    sem = k.sem
    rows_in, x_in, rows_one = sem("rows_in"), sem("x_in"), sem("rows_one")
    consts = sem("consts")
    xT_done, xT_ready = sem("xT_done"), sem("xT_ready")
    col_done, cols_ready = sem("col_done"), sem("cols_ready")
    evac = k.evac
    lbd, lb_ready, f_ready, lf_ready = sem("lbd"), sem("lb_ready"), sem("f_ready"), sem("lf_ready")
    diff, expd, fac, zeroed, score = (sem(n) for n in ("hg_diff", "hg_exp", "hg_factors", "hg_zeroed", "hg_score"))
    bias_done = sem("bias_done")
    k.fbuf, k.kk, k.hq, k.sgq = (k.tmp(n, [P, HEADS, T]) for n in ("fbuf", "kk", "hq", "sgq"))
    k.bb = k.tmp("bb", [P, HEADS, T + 1])
    k.lb = k.tmp("lb", [P, 3 * HEADS])
    lb, om = k.lb[:, 0:4], k.lb[:, 4:8]
    arena = k.ring[:, EARLY:SLOTS, :].rearrange("p s n -> p (s n)")
    k.arena = arena
    k.st = arena[:, 0:HEADS * 384].rearrange("p (h n) -> p h n", h=HEADS)
    size = 2048 + 1792 + 576 + 2 * T
    bufs = []
    for b in range(2):
        o = HEADS * 384 + b * size
        bufs.append(Factors(
            A=arena[:, o:o + 2048].rearrange("p (b s t) -> p b s t", s=SUB, t=SUB),
            B=arena[:, o + 2048:o + 3840].rearrange("p (c i s) -> p c i s", c=4, i=NSUB - 1),
            C=arena[:, o + 3840:o + 4416].rearrange("p (c s) -> p c s", c=3),
            q=arena[:, o + 4416:o + 4416 + 2 * T].rearrange("p (l t) -> p l t", l=2)))
    tmpA = k.tmp("hg_tmpA", [P, 2, P])
    bank = k.ps[:, 7, :]
    jobs = {6: ("E", 0), 8: ("E", 1), 11: ("E", 2), 14: ("E", 3)}
    pe_jobs = {10: 0, 13: 1, 16: 2, 19: 3}
    ada_at = [i for i in sorted(ADA_AFTER) for _ in range(ADA_AFTER[i])][:ADA_EARLY]

    block = k.ctx_block("projections")
    with block as blk:
        @blk.sync
        def _(sp):
            for t in range(TT):
                sp.dma_start(k.x[:, t, :], a["x"][0, t * P:(t + 1) * P, :]).then_inc(x_in, 16)
            load_first(k, sp, 0, FIRST.index(("ada", 2 * ADA_EARLY)) + EARLY)
            for dst, src in k.broadcasts:
                sp.dma_start(dst, src).then_inc(k.bcast_in, 16)

        @blk.gpsimd
        def _(pool):
            link = chain(k, pool, "pool")
            link(nc.gpsimd.memset(k.ones[:, :], 1.0))
            link(nc.gpsimd.memset(k.ident[:, :], 0.0))
            link(nc.gpsimd.affine_select(out=k.ident[:, :], in_=k.ident[:, :], compare_op=ALU.not_equal, fill=1.0,
                                         base=0, pattern=[[-1, P]], channel_multiplier=1))
            nc.gpsimd.affine_select(out=k.strict[:, :], in_=k.ones[:, :], compare_op=ALU.is_ge, fill=0.0,
                                    base=-1, pattern=[[1, P]], channel_multiplier=-1)
            nc.gpsimd.affine_select(out=k.tri[:, :], in_=k.ones[:, :], compare_op=ALU.is_ge, fill=0.0,
                                    base=0, pattern=[[-1, P]], channel_multiplier=1)
            nc.gpsimd.affine_select(out=k.later[:, :], in_=k.ones[:, :], compare_op=ALU.is_ge, fill=0.0,
                                    base=-1, pattern=[[SUB, P // SUB], [0, SUB]], channel_multiplier=-1)
            link(nc.gpsimd.affine_select(out=k.same[:, :], in_=k.ones[:, :], compare_op=ALU.is_ge, fill=0.0,
                                         base=0, pattern=[[1, P]], channel_multiplier=-1))
            link(nc.gpsimd.affine_select(out=k.same[:, :], in_=k.same[:, :], compare_op=ALU.is_ge, fill=0.0,
                                         base=0, pattern=[[-SUB, P // SUB], [0, SUB]], channel_multiplier=1))
            for i in range(3):
                nc.gpsimd.tensor_copy(k.keep[:, i * P:(i + 1) * P], (k.ones if i == 1 else k.strict)[:, :])
            link(nc.gpsimd.iota(k.iota_i[:, :], pattern=[[1, CAP]], base=0, channel_multiplier=0))
            nc.gpsimd.tensor_copy(k.iota[:, :], k.iota_i[:, :]).then_inc(consts, 1)

        @blk.tensor
        def _(pe):
            pe.wait_ge(consts, 1)
            pe.wait_ge(x_in, 32)
            transpose_tokens(nc, k, k.flat[:, 0:2048], k.x, 0, KD).then_inc(xT_done, 1)
            pe.wait_ge(xT_ready, 2)

            def head_scores(h):
                b = bufs[h % 2]
                pe.wait_ge(fac, h + 1)
                pe.wait_ge(zeroed, h + 1)
                for tile in range(2):
                    for t in range(SUB):
                        v = b.A[:, tile * 16:(tile + 1) * 16, :, t].rearrange("p b s -> p (b s)")
                        for row in (0, CHUNK):
                            nc.tensor.matmul(bank[row:row + CHUNK, 384 + tile * SUB + t:385 + tile * SUB + t],
                                             v[:, row:row + CHUNK], k.ones[:, 0:1], start=True, stop=True)
                for pair in (0, 2):
                    for i in range(1, NSUB):
                        for c in (pair, pair + 1):
                            row, col = (c % 2) * CHUNK, (0 if c < 2 else 128) + c * CHUNK
                            nc.tensor.matmul(bank[row:row + CHUNK, col + i * SUB:col + (i + 1) * SUB],
                                             b.B[:, c, i - 1, :],
                                             b.q[:, 0, c * CHUNK + i * SUB:c * CHUNK + (i + 1) * SUB],
                                             start=True, stop=True)
                for c in range(1, 4):
                    n = min(c * CHUNK, P)
                    nc.tensor.matmul(bank[0:n, c * CHUNK:(c + 1) * CHUNK], b.C[:, c - 1, 0:n],
                                     b.q[:, 1, c * CHUNK:(c + 1) * CHUNK], start=True, stop=True)
                nc.tensor.matmul(bank[0:CHUNK, 320:384], b.C[:, 2, P:P + CHUNK], b.q[:, 1, 3 * CHUNK:4 * CHUNK],
                                 start=True, stop=True).then_inc(score, 1)

            for i in range(N_IN):
                w = first_arrived(k, pe, "in", i)
                if i >= 5:
                    pe.wait_ge(evac, i - 4)
                out = k.ps[:, i % 5, :]
                form = token_major if IN_ORDER[i] in (4, 5, 10, 11) else None
                last = token_major(nc, out, w, k.xT, KD, CH) if form else feature_major(nc, out, w, k.xT, KD, 2)
                last.then_inc(k.first_used, 1)
                if i == 1:
                    pe.wait_ge(rows_in, 16 * k.n_rows)
                    nc.tensor.transpose(bank[:, 0:NROWS], k.rows[:, :], k.ident[0:NROWS, 0:NROWS]).then_inc(col_done, 1)
                if i in pe_jobs:
                    head_scores(pe_jobs[i])
                if i - 1 in ada_at:
                    ada_sums(nc, k, pe, ada_at.index(i - 1))
                if i in ada_at:
                    if i == ada_at[0]:
                        pe.wait_ge(f_ready, 1)
                    ada_rows(nc, k, pe, ada_at.index(i), 5)
            pe.wait_ge(evac, N_IN)
            pe.wait_ge(k.bias_in, 16)
            for par in range(2):
                for m in range(KF):
                    last = nc.tensor.transpose(k.ps[:, 0, (par * 8 + m) * E:(par * 8 + m + 1) * E],
                                               k.b_up[:, m * 256 + par:(m + 1) * 256:2], k.ident[0:E, 0:E])
            last.then_inc(bias_done, 1)

        @blk.scalar
        def _(act):
            act.wait_ge(rows_one, 1)
            for dst, src in k.row_loads:
                act.dma_start(dst, src).then_inc(rows_in, 16)
            act.dma_start(k.b_up[:, :], a["expert_b_up"][0]).then_inc(k.bias_in, 16)
            link = chain(k, act, "act")
            act.wait_ge(lbd, 1)
            nc.scalar.activation(k.cact[:, :], k.cols[:, ROWS["c"]:ROWS["c"] + KD], ACT.Sigmoid)
            nc.scalar.activation(lb, k.lb[:, 8:12], ACT.Sigmoid).then_inc(lb_ready, 1)

            def exps(h):
                b = bufs[h % 2]
                act.wait_ge(diff, h + 1)
                for v in (b.A, b.B, b.C):
                    v = v.rearrange("p b s t -> p (b s t)") if len(v.shape) == 4 else v.rearrange("p b s -> p (b s)")
                    nc.scalar.activation(v, v, ACT.Exp)
                nc.scalar.activation(b.q, b.q, ACT.Exp).then_inc(expd, 1)

            for i, c in enumerate(IN_ORDER):
                act.wait_ge(k.first_used, i + 1)
                src = k.ps[:, i % 5, :]
                two = src.rearrange("p (m t) -> p m t", m=2)
                j = 2 * (c % 2)
                if c in (8, 9):
                    ins = nc.scalar.activation(k.fbuf[:, j:j + 2, :], two, ACT.Sigmoid)
                elif c in (6, 7):
                    act_copy(nc, k.hq[:, j:j + 2, :], two)
                    ins = nc.scalar.activation(k.sgq[:, j:j + 2, :], two, ACT.Sigmoid)
                elif c in (0, 1):
                    ins = nc.scalar.mul(k.sbq[:, j:j + 2, :], two, 0.125)
                elif c in (2, 3):
                    ins = act_copy(nc, k.sbk[:, j:j + 2, :], two)
                elif c in (4, 5):
                    ins = act_copy(nc, k.sbv[:, :, (c - 4) * CH:(c - 3) * CH], two)
                elif c in (10, 11):
                    ins = act_copy(nc, k.hgv[:, :, (c - 10) * CH:(c - 9) * CH], two)
                elif c in (12, 13):
                    ins = nc.scalar.activation(k.hgs[:, j:j + 2, :], two, ACT.Sigmoid)
                else:
                    ins = nc.scalar.activation(k.gates[:, 2 * (c - 14):2 * (c - 14) + 2, :], two, ACT.Sigmoid)
                ins.then_inc(evac, 1)
                if i in ada_at:
                    ada_copy(k, act, lambda out, x: act_copy(nc, out, x), ada_at.index(i), 5)
                if i == 4:
                    act.wait_ge(f_ready, 1)
                    nc.scalar.activation(k.sgq[:, :, :], k.fbuf[:, :, :], ACT.Ln).then_inc(lf_ready, 1)
                if i in jobs:
                    exps(jobs[i][1])
            act.wait_ge(bias_done, 1)
            link(act_copy(nc, k.bupT[:, :], k.ps[:, 0, :]))

        @blk.vector
        def _(dve):
            link = chain(k, dve, "dve")
            nc.vector.memset(k.rows[:, :], 1.0).then_inc(rows_one, 1)
            nc.vector.memset(k.bb[:, :, 0:1], 0.0)
            dve.wait_ge(consts, 1)
            nc.vector.tensor_scalar(k.nkeep[:, :], k.keep[:, :], -1.0, None, ALU.mult)
            nc.vector.memset(k.eps[:, 0:1], LN_EPS)
            link(nc.vector.memset(k.eps[:, 1:2], RMS_EPS))
            dve.wait_ge(xT_done, 1)
            nc.vector.tensor_copy(k.xT[:, 0:4, :].rearrange("p k t -> p (k t)"), k.flat[:, 0:1024]).then_inc(xT_ready, 1)
            nc.vector.tensor_copy(k.xT[:, 4:8, :].rearrange("p k t -> p (k t)"), k.flat[:, 1024:2048]).then_inc(xT_ready, 1)
            dve.wait_ge(col_done, 1)
            nc.vector.tensor_copy(k.cols[:, :], bank[:, 0:NROWS]).then_inc(cols_ready, 1)
            dve.wait_ge(cols_ready, 1)
            nc.vector.tensor_tensor(k.lb[:, 8:12], k.cols[:, 0:4], k.cols[:, 4:8], ALU.subtract).then_inc(lbd, 1)
            dve.wait_ge(lb_ready, 1)
            nc.vector.tensor_tensor(k.cact[:, :], k.cact[:, :], k.cols[:, ROWS["c"]:ROWS["c"] + KD], ALU.mult)
            nc.vector.tensor_reduce(k.pick[:, :], k.ident[:, :].rearrange("p (g e) -> p e g", e=E), AX.X, ALU.add)
            link(nc.vector.tensor_scalar(om, lb, -1.0, 1.0, ALU.mult, ALU.add))
            nc.vector.tensor_copy(k.crep[:, :, :], bc(k.cact[:, :], 2, 32))
            dve.wait_ge(evac, 4)
            for h in range(HEADS):
                ins = nc.vector.tensor_scalar(k.fbuf[:, h, :], k.fbuf[:, h, :], om[:, h:h + 1], lb[:, h:h + 1],
                                              ALU.mult, ALU.add)
            link(ins)
            link(nc.vector.tensor_tensor(k.hq[:, :, :], k.hq[:, :, :], k.sgq[:, :, :], ALU.mult))
            nc.vector.tensor_scalar(k.kk[:, :, :], k.fbuf[:, :, :], -1.0, 1.0, ALU.mult, ALU.add).then_inc(f_ready, 1)
            dve.wait_ge(lf_ready, 1)
            dve.wait_ge(f_ready, 1)
            one = k.ones[:, 0:1].to_broadcast([P, T])
            for h in range(HEADS):
                ins = nc.vector.tensor_tensor_scan(k.bb[:, h, 1:T + 1], one, k.sgq[:, h, :], 0.0, ALU.mult, ALU.add)
            link(ins)

            def diffs(h):
                b = bufs[h % 2]
                after = k.bb[:, h, 1:T + 1]
                before = k.bb[:, h, 0:T]
                small = after.rearrange("p (b s) -> p b s", s=SUB)
                nc.vector.tensor_tensor(b.A, bc(small, 2, SUB), bc(small, 3, SUB), ALU.subtract)
                for c in range(4):
                    keys = after[:, c * CHUNK:(c + 1) * CHUNK]
                    starts = before[:, c * CHUNK + SUB:(c + 1) * CHUNK:SUB]
                    nc.vector.tensor_tensor(b.B[:, c], bc(starts, 2, CHUNK), bc(keys, 1, NSUB - 1), ALU.subtract)
                starts = before[:, CHUNK:T:CHUNK]
                nc.vector.tensor_tensor(b.C, bc(starts, 2, 192), bc(after[:, 0:192], 1, 3), ALU.subtract)
                nc.vector.tensor_tensor(b.q[:, 0, :].rearrange("p (b s) -> p b s", s=SUB), small,
                                        bc(before[:, 0:T:SUB], 2, SUB), ALU.subtract)
                link(nc.vector.tensor_tensor(b.q[:, 1, :].rearrange("p (b s) -> p b s", s=CHUNK),
                                             after.rearrange("p (b s) -> p b s", s=CHUNK),
                                             bc(before[:, 0:T:CHUNK], 2, CHUNK), ALU.subtract))
                whole = arena[:, HEADS * 384 + (h % 2) * size:HEADS * 384 + (h % 2) * size + size]
                nc.vector.tensor_scalar(whole, whole, 0.0, None, ALU.min).then_inc(diff, 1)

            def factors(h):
                b = bufs[h % 2]
                key, query = k.kk[:, h, :], k.hq[:, h, :]
                dve.wait_ge(expd, h + 1)
                nc.vector.tensor_tensor(b.C, b.C, bc(key[:, 0:192], 1, 3), ALU.mult)
                for c in range(4):
                    nc.vector.tensor_tensor(b.B[:, c], b.B[:, c], bc(key[:, c * CHUNK:(c + 1) * CHUNK], 1, NSUB - 1),
                                            ALU.mult)
                link(nc.vector.tensor_tensor(b.A, b.A, bc(key.rearrange("p (b s) -> p b s", s=SUB), 3, SUB), ALU.mult))
                nc.vector.tensor_tensor(b.q, b.q, bc(query, 1, 2), ALU.mult)
                nc.vector.tensor_tensor(b.A, b.A, bc(query.rearrange("p (b s) -> p b s", s=SUB), 2, SUB),
                                        ALU.mult).then_inc(fac, 1)

            def zero():
                nc.vector.memset(bank[:, 0:384], 0.0).then_inc(zeroed, 1)

            def weights(h):
                dve.wait_ge(score, h + 1)
                for tile in range(2):
                    g = bank[:, 384 + tile * SUB:384 + (tile + 1) * SUB]
                    nc.vector.tensor_tensor(tmpA[:, tile, :].rearrange("p (b s) -> p b s", s=SUB),
                                            k.same[:, :].rearrange("p (b s) -> p b s", s=SUB), bc(g, 1, P // SUB),
                                            ALU.mult)
                    nc.vector.tensor_tensor(k.st[:, h, tile * 256:tile * 256 + P], bank[:, tile * 256:tile * 256 + P],
                                            k.later[:, :], ALU.mult)
                link(nc.vector.tensor_copy(k.st[:, h, P:2 * P], bank[:, P:2 * P]))
                for tile in range(2):
                    ins = nc.vector.tensor_tensor(k.st[:, h, tile * 256:tile * 256 + P],
                                                  k.st[:, h, tile * 256:tile * 256 + P], tmpA[:, tile, :], ALU.add)
                link(ins)

            zero()
            diffs(0)
            diffs(1)
            factors(0)
            for h in range(HEADS):
                weights(h)
                if h + 1 < HEADS:
                    zero()
                if h + 2 < HEADS:
                    diffs(h + 2)
                if h + 1 < HEADS:
                    factors(h + 1)


def mixers(nc, k, a):
    sem = k.sem
    z_done, l_ready, lk_ready, r_done, arg_ready, e_ready, w_ready, pv_done, o_evac = (sem(n) for n in (
        "sb_z", "sb_log", "sb_keep", "sb_sum", "sb_arg", "sb_exp", "sb_weights", "sb_out", "sb_evac"))
    o_done, sq_ready, on_ready = (sem(n) for n in ("hg_out", "hg_squares", "hg_normed"))
    el, lk, wt = (k.arena[:, HEADS * 384 * (1 + n):HEADS * 384 * (2 + n)].rearrange("p (h n) -> p h n", h=4)
                  for n in range(3))
    o = 4 * HEADS * 384
    sq = k.arena[:, o:o + 1024].rearrange("p (a n) -> p a n", n=512)
    on = k.arena[:, o + 1024:o + 2048].rearrange("p (a n) -> p a n", n=512)
    small = k.small
    ss, root, rs = small[:, 0:8], small[:, 8:16], small[:, 16:24]

    with k.ctx_block("mixers") as blk:
        @blk.sync
        def _(sp):
            load_first(k, sp, FIRST.index(("ada", 2 * ADA_EARLY)) + EARLY, FIRST.index(("branch", 0)) + EARLY)

        @blk.tensor
        def _(pe):
            def z(g):
                if g:
                    pe.wait_ge(o_evac, g)
                for b in range(4):
                    h = 4 * g + b
                    r = 64 * (h % 2)
                    q, key = k.sbq[r:r + 64, h // 2, :], k.sbk[r:r + 64, h // 2, :]
                    nc.tensor.matmul(k.ps[:, b, 0:T], key[:, 0:P], q, start=True, stop=False, skip_group_check=True)
                    last = nc.tensor.matmul(k.ps[:, b, T:T + P], key[:, P:T], q[:, P:T], start=False, stop=False,
                                            skip_group_check=True)
                last.then_inc(z_done, 1)

            def sums(g):
                pe.wait_ge(lk_ready, g + 1)
                for b in range(4):
                    nc.tensor.matmul(k.ps[:, b, 0:T], k.tri[:, :], lk[:, b, 0:T], start=False, stop=False,
                                     skip_group_check=True)
                    nc.tensor.matmul(k.ps[:, b, P:T], k.ones[:, :], lk[:, b, T:T + P], start=False, stop=False,
                                     skip_group_check=True)
                    last = nc.tensor.matmul(k.ps[:, b, T:T + P], k.tri[:, :], lk[:, b, T:T + P], start=False, stop=True,
                                            skip_group_check=True)
                last.then_inc(r_done, 1)

            def values(g):
                pe.wait_ge(w_ready, g + 1)
                for b in range(4):
                    h = 4 * g + b
                    r = 64 * (h % 2)
                    nc.tensor.matmul(k.ps[r:r + 64, b, 0:T], k.sbv[:, 0, h * 64:(h + 1) * 64], wt[:, b, 0:T],
                                     start=True, stop=False, skip_group_check=True)
                    last = nc.tensor.matmul(k.ps[r:r + 64, b, P:T], k.sbv[:, 1, h * 64:(h + 1) * 64], wt[:, b, T:T + P],
                                            start=False, stop=True, skip_group_check=True)
                last.then_inc(pv_done, 1)

            z(0)
            ada_rows(nc, k, pe, 5, 7)
            for h in range(HEADS):
                v = [k.hgv[:, t, h * P:(h + 1) * P] for t in range(TT)]
                nc.tensor.matmul(k.ps[:, 4, h * P:(h + 1) * P], k.st[:, h, 0:P], v[0], start=True, stop=True)
                nc.tensor.matmul(k.ps[:, 5, h * P:(h + 1) * P], k.st[:, h, P:2 * P], v[0], start=True, stop=False)
                last = nc.tensor.matmul(k.ps[:, 5, h * P:(h + 1) * P], k.st[:, h, 2 * P:3 * P], v[1],
                                        start=False, stop=True)
            last.then_inc(o_done, 1)
            ada_sums(nc, k, pe, 5)
            ada_rows(nc, k, pe, 6, 7)
            ada_sums(nc, k, pe, 6)
            ada_rows(nc, k, pe, 7, 7)
            sums(0)
            ada_sums(nc, k, pe, 7)
            ada_rows(nc, k, pe, 8, 7)
            values(0)
            z(1)
            ada_sums(nc, k, pe, 8)
            ada_rows(nc, k, pe, 9, 7)
            pe.wait_ge(on_ready, 1)
            transpose_tokens(nc, k, k.flat[:, 2048:3072], on, 0, HEADS).then_inc(k.hg_turned, 1)
            ada_sums(nc, k, pe, 9)
            ada_rows(nc, k, pe, 10, 7)
            ada_sums(nc, k, pe, 10)
            ada_rows(nc, k, pe, 11, 7)
            sums(1)
            ada_sums(nc, k, pe, 11)
            values(1)

        @blk.scalar
        def _(act):
            link = chain(k, act, "act")

            def logs(g):
                act.wait_ge(z_done, g + 1)
                if g:
                    act.wait_ge(lk_ready, g)
                link(nc.scalar.activation(el, k.ps[:, 0:4, 0:384], ACT.Abs))
                link(nc.scalar.activation(el, el, ACT.Exp, scale=-1.0))
                nc.scalar.activation(el, el, ACT.Ln, bias=1.0).then_inc(l_ready, 1)

            def exps(g):
                act.wait_ge(arg_ready, g + 1)
                nc.scalar.activation(wt, wt, ACT.Exp).then_inc(e_ready, 1)

            logs(0)
            act.wait_ge(o_done, 1)
            nc.scalar.activation(sq, k.ps[:, 4:6, :], ACT.Square).then_inc(sq_ready, 1)
            act.wait_ge(k.sums, 1)
            nc.scalar.activation(root, ss, ACT.Sqrt, bias=k.eps[:, 1:2], scale=1.0 / P).then_inc(k.roots, 1)
            exps(0)
            logs(1)
            exps(1)

        @blk.vector
        def _(dve):
            link = chain(k, dve, "dve")

            def copy(pair):
                ada_copy(k, dve, nc.vector.tensor_copy, pair, 7)

            def keeps(g):
                dve.wait_ge(l_ready, g + 1)
                if g:
                    dve.wait_ge(r_done, g)
                link(nc.vector.scalar_tensor_tensor(out=lk, in0=k.ps[:, 0:4, 0:384], scalar=0.0, in1=el,
                                                    op0=ALU.max, op1=ALU.add))
                nc.vector.tensor_tensor(lk, lk, bc(k.nkeep[:, :], 1, 4), ALU.mult).then_inc(lk_ready, 1)

            def args(g):
                dve.wait_ge(r_done, g + 1)
                if g:
                    dve.wait_ge(pv_done, g)
                nc.vector.tensor_scalar(wt, k.ps[:, 0:4, 0:384], 0.0, None, ALU.min).then_inc(arg_ready, 1)

            def weights(g):
                dve.wait_ge(e_ready, g + 1)
                nc.vector.tensor_tensor(wt, wt, bc(k.keep[:, :], 1, 4), ALU.mult).then_inc(w_ready, 1)

            def out(g):
                dve.wait_ge(pv_done, g + 1)
                for odd in range(2):
                    r = slice(64 * odd, 64 * odd + 64)
                    ins = nc.vector.tensor_copy(k.osbT[r, 2 * g:2 * g + 2, :], k.ps[r, odd:4:2, 0:T])
                ins.then_inc(o_evac, 1)

            copy(5)
            copy(6)
            keeps(0)
            copy(7)
            dve.wait_ge(sq_ready, 1)
            nc.vector.tensor_reduce(ss, sq.rearrange("p a (h n) -> p (a h) n", n=P), AX.X, ALU.add)\
                .then_inc(k.sums, 1)
            args(0)
            dve.wait_ge(k.roots, 1)
            link(nc.vector.reciprocal(rs, root))
            nc.vector.tensor_tensor(on.rearrange("p a (h n) -> p (a h) n", n=P),
                                    k.ps[:, 4:6, :].rearrange("p a (h n) -> p (a h) n", n=P), bc(rs, 2, P),
                                    ALU.mult).then_inc(on_ready, 1)
            weights(0)
            copy(8)
            out(0)
            copy(9)
            copy(10)
            keeps(1)
            copy(11)
            args(1)
            weights(1)
            out(1)
            dve.wait_ge(k.ada_summed, N_ADA)
            link(nc.vector.tensor_tensor(k.mod[:, :], k.ps[:, 6, ADA_COL:ADA_COL + 48],
                                         k.cols[:, ROWS["bada"]:ROWS["bada"] + 48], ALU.add))


def norm_stats(nc, k, link, x, var_ready):
    for t in range(TT):
        for half in range(2):
            nc.vector.bn_stats(k.stats[:, t, half, :], x[:, t, half * 512:(half + 1) * 512])
    link(nc.vector.memset(k.mv[:, :, :], 0.0))
    for t in range(TT):
        ins = nc.vector.bn_aggr(k.mv[:, t, :], k.stats[:, t, :, :])
    ins.then_inc(var_ready, 1)


def norm_apply(nc, k, dve, link, x, var_ready, n_var, root_ready, n, g, b, tile_ready):
    dve.wait_ge(var_ready, n_var)
    dve.wait_ge(root_ready, n)
    link(nc.vector.reciprocal(k.rstd[:, :], k.root[:, :]))
    for t in range(TT):
        ins = nc.vector.scalar_tensor_tensor(out=x[:, t, :], in0=x[:, t, :], scalar=k.mv[:, t, 0:1], in1=g,
                                             op0=ALU.subtract, op1=ALU.mult)
    link(ins)
    for t in range(TT):
        nc.vector.scalar_tensor_tensor(out=x[:, t, :], in0=x[:, t, :], scalar=k.rstd[:, t:t + 1], in1=b,
                                       op0=ALU.mult, op1=ALU.add).then_inc(tile_ready, 1)


def branches(nc, k, a):
    sem = k.sem
    hgT, merged, h_ready = (sem(n) for n in ("hgT_ready", "merged", "h_ready"))
    var, root, hT_done, hT_ready = k.ln_var, k.ln_root, k.turned, k.hT_ready
    log_done, negmax, expd, m_ready, pos_done = (sem(n) for n in (
        "logits_done", "top_negmax", "top_exp", "chosen", "pos_done"))
    ln_in, part_done, part_ready = sem("ln1_in"), sem("logit_parts"), sem("logit_parts_out")
    part = k.ada_acc[:, 0, 0:T]
    gates, m = k.gates, k.xT
    hT = k.gates[:, 0:8, :]
    lg, m8, ix, ixf, gv, tmp = k.lg, k.m8, k.ix, k.ixf, k.gv, k.rtmp

    with k.ctx_block("branches") as blk:
        @blk.sync
        def _(sp):
            load_first(k, sp, FIRST.index(("branch", 0)) + EARLY, N_FIRST)
            for q in range(PER):
                if q >= EARLY:
                    sp.wait_ge(k.first_used, N_PE - EARLY + (q - EARLY) + 1)
                load_expert(k, sp, a, 0, q)

        @blk.tensor
        def _(pe):
            for c in range(2):
                w = first_arrived(k, pe, "branch", c)
                feature_major(nc, k.flat[:, c * 1024:(c + 1) * 1024], w, k.osbT, 4, 4).then_inc(k.first_used, 1)
            pe.wait_ge(hgT, HEADS)
            for c in range(2):
                w = first_arrived(k, pe, "branch", 2 + c)
                feature_major(nc, k.flat[:, 2048 + c * 1024:2048 + (c + 1) * 1024], w, k.hgT, 4, 4)\
                    .then_inc(k.first_used, 1)
            pe.wait_ge(merged, 2)
            for c in range(4):
                w = first_arrived(k, pe, "out", c)
                token_major(nc, k.ps[:, c, :], w, m, KD, CH).then_inc(k.first_used, 1)
            transpose_tokens(nc, k, k.flat[:, 2048:4096], k.h, 0, KD, lambda t: pe.wait_ge(h_ready, t + 1))\
                .then_inc(hT_done, 1)
            pe.wait_ge(hT_ready, 2)
            pe.wait_ge(k.bcast_in, 16 * len(k.broadcasts))
            for q in range(KD):
                g = 32 * (q % 4)
                last = nc.tensor.matmul(k.ps[g:g + 32, 2, 0:T], k.rw[:, q, :], hT[:, q, :], start=(q < 4), stop=(q >= 4),
                                        skip_group_check=True)
            last.then_inc(part_done, 1)
            pe.wait_ge(part_ready, 1)
            for t in range(TT):
                last = nc.tensor.matmul(k.ps[:, 0, t * E:(t + 1) * E], part[:, t * P:(t + 1) * P], k.pick[:, :],
                                        start=True, stop=True)
            last.then_inc(log_done, 1)
            pe.wait_ge(m_ready, 1)
            mm = k.chosen
            nc.tensor.matmul(k.ps[:, 1, 0:E], k.strict[:, :], mm[:, 0, :], start=True, stop=True)
            nc.tensor.matmul(k.ps[:, 1, E:2 * E], k.ones[:, :], mm[:, 0, :], start=True, stop=False)
            nc.tensor.matmul(k.ps[:, 1, E:2 * E], k.strict[:, :], mm[:, 1, :], start=False, stop=True)
            nc.tensor.matmul(k.ps[:, 1, 2 * E:3 * E], k.ones[:, :], mm[:, 0, :], start=True, stop=False)
            nc.tensor.matmul(k.ps[:, 1, 2 * E:3 * E], k.ones[:, :], mm[:, 1, :], start=False, stop=True)\
                .then_inc(pos_done, 1)

        @blk.scalar
        def _(act):
            act.dma_start(k.g1, a["ln1_g"][0:1, :].to_broadcast([P, D])).then_inc(ln_in, 16)
            act.dma_start(k.b1, a["ln1_b"][0:1, :].to_broadcast([P, D])).then_inc(ln_in, 16)
            act.wait_ge(var, 1)
            nc.scalar.activation(k.root[:, :], k.mv[:, :, 1], ACT.Sqrt, bias=k.eps[:, 0:1]).then_inc(root, 1)
            act.wait_ge(hT_done, 1)
            act_copy(nc, hT[:, 4:8, :].rearrange("p k t -> p (k t)"), k.flat[:, 3072:4096]).then_inc(hT_ready, 1)
            act.wait_ge(negmax, 1)
            for t in range(TT):
                ins = nc.scalar.activation(gv[:, t, :], m8[:, t, 0:4], ACT.Exp, bias=k.small[:, t:t + 1])
            ins.then_inc(expd, 1)

        @blk.vector
        def _(dve):
            link = chain(k, dve, "dve")
            dve.wait_ge(k.hg_turned, 1)
            for h in range(HEADS):
                nc.vector.scalar_tensor_tensor(out=k.hgT[:, h, :], in0=k.flat[:, 2048 + h * T:2048 + (h + 1) * T],
                                               scalar=k.cols[:, ROWS["hnorm"] + h:ROWS["hnorm"] + h + 1],
                                               in1=k.hgs[:, h, :], op0=ALU.mult, op1=ALU.mult).then_inc(hgT, 1)
            for c in range(2):
                f = k.flat[:, c * 1024:(c + 1) * 1024].rearrange("p (m t) -> p m t", t=T)
                g = gates[:, 4 * c:4 * c + 4, :]
                dve.wait_ge(k.first_used, PE_BRANCH + c + 1)
                link(nc.vector.tensor_tensor(g, g, f, ALU.mult))
            for c in range(2):
                f = k.flat[:, 2048 + c * 1024:2048 + (c + 1) * 1024].rearrange("p (m t) -> p m t", t=T)
                g = gates[:, 8 + 4 * c:12 + 4 * c, :]
                dve.wait_ge(k.first_used, PE_BRANCH + 2 + c + 1)
                link(nc.vector.tensor_tensor(g, g, f, ALU.mult))
                nc.vector.tensor_tensor(m[:, 4 * c:4 * c + 4, :], gates[:, 4 * c:4 * c + 4, :], g, ALU.add)\
                    .then_inc(merged, 1)
            for c in range(4):
                dve.wait_ge(k.first_used, PE_OUT + c + 1)
                s = slice(c * CH, (c + 1) * CH)
                ins = nc.vector.scalar_tensor_tensor(out=k.h[:, :, s], in0=k.x[:, :, s], scalar=ALPHA,
                                                     in1=k.ps[:, c, :].rearrange("p (t n) -> p t n", t=TT),
                                                     op0=ALU.mult, op1=ALU.add)
            link(ins)
            dve.wait_ge(k.bcast_in, 16 * len(k.broadcasts))
            dve.wait_ge(ln_in, 32)
            norm_stats(nc, k, link, k.h, var)
            norm_apply(nc, k, dve, link, k.h, var, 1, root, 1, k.g1, k.b1, h_ready)
            dve.wait_ge(hT_done, 1)
            nc.vector.tensor_copy(hT[:, 0:4, :].rearrange("p k t -> p (k t)"), k.flat[:, 2048:3072])\
                .then_inc(hT_ready, 1)
            dve.wait_ge(part_done, 1)
            nc.vector.tensor_copy(part, k.ps[:, 2, 0:T]).then_inc(part_ready, 1)
            dve.wait_ge(log_done, 1)
            link(nc.vector.tensor_tensor(lg[:, :, :], k.ps[:, 0, 0:TT * E].rearrange("p (t e) -> p t e", t=TT),
                                         bc(k.rb[:, :], 1, TT), ALU.add))
            for t in range(TT):
                ins = nc.vector.max(m8[:, t, :], lg[:, t, :])
            link(ins)
            nc.vector.tensor_scalar(k.small[:, 0:TT], m8[:, :, 0], -1.0, None, ALU.mult).then_inc(negmax, 1)
            for t in range(TT):
                ins = nc.vector.max_index(ix[:, t, :], m8[:, t, :], lg[:, t, :])
            link(ins)
            link(nc.vector.tensor_copy(ixf[:, :, :], ix[:, :, :]))
            dve.wait_ge(expd, 1)
            link(nc.vector.tensor_reduce(k.small[:, 2:4], gv[:, :, :], AX.X, ALU.add))
            link(nc.vector.reciprocal(k.small[:, 4:6], k.small[:, 2:4]))
            link(nc.vector.tensor_tensor(gv[:, :, :], gv[:, :, :], bc(k.small[:, 4:6], 2, 4), ALU.mult))
            for j in range(4):
                for t in range(TT):
                    nc.vector.tensor_scalar(tmp[:, 0, t, :], k.iota[:, 0:E], ixf[:, t, j:j + 1], None, ALU.is_equal)
                    ins = nc.vector.tensor_scalar(tmp[:, 1, t, :], k.iota[:, 0:E], ixf[:, t, j:j + 1],
                                                  gv[:, t, j:j + 1], ALU.is_equal, ALU.mult)
                link(ins)
                for n, dst in ((0, k.chosen), (1, k.gate)):
                    if j == 0:
                        ins = nc.vector.tensor_copy(dst[:, :, :], tmp[:, n])
                    else:
                        ins = nc.vector.tensor_tensor(dst[:, :, :], dst[:, :, :], tmp[:, n], ALU.add)
                if j < 3:
                    link(ins)
                else:
                    ins.then_inc(m_ready, 1)
            dve.wait_ge(pos_done, 1)
            dve.wait_ge(m_ready, 1)
            pl = k.place[:, :, 0:E]
            link(nc.vector.tensor_scalar(pl, k.ps[:, 1, 0:2 * E].rearrange("p (t e) -> p t e", t=TT), 1.0, None, ALU.add))
            link(nc.vector.tensor_tensor(pl, pl, k.chosen[:, :, :], ALU.mult))
            link(nc.vector.tensor_scalar(pl, pl, -1.0, None, ALU.add))
            nc.vector.tensor_scalar(k.place[:, :, E:E + 2], k.place[:, :, 0:2], float(-CAP), None, ALU.add)
            link(nc.vector.tensor_reduce(k.small[:, 0:1], k.ps[:, 1, 2 * E:3 * E], AX.X, ALU.max))
            for j in range(1, ROUNDS):
                ins = nc.vector.tensor_scalar(k.small[:, j:j + 1], k.small[:, 0:1], float(j * CAP), None, ALU.is_gt)
            link(ins)
            link(nc.vector.tensor_reduce(k.small[:, 4:5], k.small[:, 1:ROUNDS], AX.X, ALU.add))
            link(nc.vector.tensor_copy(k.rounds[:, :], k.small[:, 4:5]))


def load_expert(k, sp, a, e, q):
    slot = (EARLY + q) % SLOTS
    if q < 8:
        src = a["expert_w_up"][0, bass.ds(e, 1), q * P:(q + 1) * P, :].rearrange("e p n -> p (e n)")
        dst = k.ring[:, slot, :]
    else:
        j = q - 8
        src = a["expert_w_down"][0, bass.ds(e, 1), j * 256:(j + 1) * 256, :].rearrange("e (k p) n -> p (e k) n", p=P)
        dst = k.ring[:, slot, :].rearrange("p (k n) -> p k n", k=2)
    sp.dma_start(dst, src).then_inc(k.expert_in[q], 16)


def experts(nc, k, a):
    sem = k.sem
    hot_ready, gated_ready, g_done, row_ready, xt_done, xg_ready, selps_done, selT_ready = (sem(n) for n in (
        "hot_ready", "gated_ready", "gathered", "xrow_ready", "x_turned", "xg_ready", "sel_turned", "selT_ready"))
    hrow_ready, hT_done, glu_ready, sig_ready, act_ready, y_ready, sc_done, acc_done = (sem(n) for n in (
        "hrow_ready", "up_turned", "glu_ready", "sig_ready", "act_ready", "y_ready", "scattered", "acc_done"))
    gT_done, gT_ready, base_done = sem("gate_turned"), sem("gateT_ready"), sem("bias_sum_done")
    used = k.expert_used
    dchain = sem("moe_dve")
    pairs = E // 2
    up, down, turned, rows, seT = k.ps[:, 0:2, :], k.ps[:, 2, :], k.ps[:, 3:5, :], k.ps[:, 5:7, :], k.ps[:, 7, 0:T]
    scat = (up, rows)

    def extra_rounds(eng):
        return eng.value_load(k.rounds[0:1, 0:1], min_val=0, max_val=ROUNDS - 1)

    def flat(ap):
        return ap.rearrange("p a n -> p (a n)")

    with k.ctx_block("experts") as blk:
        @blk.sync
        def _(sp):
            for dst, src in k.late_loads:
                sp.dma_start(dst, src).then_inc(k.late_in, 16)
            extra = extra_rounds(sp)

            def refill(e, done):
                for q in range(PER):
                    sp.wait_ge(used, done + q + 1)
                    load_expert(k, sp, a, e, q)

            with sp.Fori(0, E - 1) as e:
                refill(e + 1, e * PER)
            with sp.If(extra > 0):
                with sp.Fori(0, extra) as r:
                    refill(0, r * (E * PER) + (E - 1) * PER)
                    with sp.Fori(0, E - 1) as e:
                        refill(e + 1, r * (E * PER) + e * PER + E * PER)
            done = extra * (E * PER)
            for i, slot in enumerate(LATE):
                src, kt, cols = k.last[i]
                q = (slot - EARLY) % SLOTS
                sp.wait_ge(used, done + (E * PER + q + 1 - PER))
                sp.dma_start(slot_last(k, i, kt, cols), src).then_inc(k.last_in[i], 16)

        @blk.tensor
        def _(pe):
            extra = extra_rounds(pe)

            def gather():
                for half in range(2):
                    for t in range(TT):
                        last = nc.tensor.matmul(rows[:, half, :], k.sel[:, 0, t, :],
                                                k.h[:, t, half * 512:(half + 1) * 512], start=(t == 0), stop=(t == TT - 1))
                last.then_inc(g_done, 1)

            def turn_rows():
                for q in range(KD):
                    last = nc.tensor.transpose(flat(rows)[:, q * P:(q + 1) * P], k.xrow[:, q * P:(q + 1) * P],
                                               k.ident[:, :])
                last.then_inc(xt_done, 1)

            def scatter():
                for t, out in enumerate(scat):
                    for half in range(2):
                        last = nc.tensor.matmul(out[:, half, :], k.selT[:, t * P:(t + 1) * P],
                                                k.y[:, half * 512:(half + 1) * 512], start=True, stop=True)
                    last.then_inc(sc_done, 1)

            def arrivals(q, h):
                return 16 * (h + 1) + (0 if q < SLOTS - EARLY else 16 * (N_FIRST // EARLY))

            for t in range(TT):
                last = nc.tensor.transpose(k.ps[0:E, 7, t * P:(t + 1) * P], k.gate[:, t, :], k.ident[:, :])
            last.then_inc(gT_done, 1)
            pe.wait_ge(hot_ready, 1)
            gather()
            pe.wait_ge(gT_ready, 1)
            pe.wait_ge(k.bias_in, 32)
            for t, out in enumerate((up, turned)):
                for half in range(2):
                    last = nc.tensor.matmul(out[:, half, :], k.gateT[0:E, t * P:(t + 1) * P],
                                            k.b_dn[:, half * 512:(half + 1) * 512], start=True, stop=True)
                last.then_inc(base_done, 1)
                if t == 0:
                    pe.wait_ge(row_ready, 1)
                    turn_rows()
            pe.wait_ge(acc_done, 1)
            with pe.Fori(0, extra + 1) as r, pe.Fori(0, pairs) as p:
                n = r * pairs + p
                pe.wait_ge(xg_ready, n + 1)
                for h in range(2):
                    if h == 1:
                        pe.wait_ge(acc_done, n * 2 + 3)
                    for q in range(KD):
                        pe.wait_ge(k.expert_in[q], n * 32 + arrivals(q, h))
                        w = k.ring[:, (EARLY + q) % SLOTS, :]
                        for u in range(2):
                            for a2 in range(2):
                                c = a2 * 1024 + u * 512
                                last = nc.tensor.matmul(up[a2 * CAP:(a2 + 1) * CAP, u, :], k.xg[:, q, h * CAP:(h + 1) * CAP],
                                                        w[:, c:c + 512], start=(q == 0), stop=(q == KD - 1),
                                                        skip_group_check=True)
                        last.then_inc(used, 1)
                    pe.wait_ge(hrow_ready, n * 2 + h + 1)
                    pe.wait_ge(acc_done, n * 2 + 2)
                    for par in range(2):
                        for j in range(4):
                            last = nc.tensor.transpose(turned[:, par, j * P:(j + 1) * P],
                                                       k.hrow[:, j * 256 + par:(j + 1) * 256:2], k.ident[:, :])
                    last.then_inc(hT_done, 1)
                    if h == 0:
                        pe.wait_ge(selT_ready, n + 1)
                        pe.wait_ge(y_ready, n * 2 + 1)
                        scatter()
                    else:
                        pe.wait_ge(gated_ready, n + 1)
                        for t in range(TT):
                            last = nc.tensor.transpose(seT[:, t * P:(t + 1) * P], k.sel[:, 1, t, :], k.ident[:, :])
                        last.then_inc(selps_done, 1)
                        pe.wait_ge(hot_ready, n + 2)
                        pe.wait_ge(acc_done, n * 2 + 4)
                        gather()
                        pe.wait_ge(row_ready, n + 2)
                        turn_rows()
                    pe.wait_ge(act_ready, n * 2 + h + 1)
                    pe.wait_ge(y_ready, n * 2 + h + 1)
                    for j in range(4):
                        pe.wait_ge(k.expert_in[8 + j], n * 32 + arrivals(8 + j, h))
                        w = k.ring[:, (EARLY + 8 + j) % SLOTS, :]
                        for kk in range(2):
                            m = 2 * j + kk
                            for a2 in range(2):
                                c = kk * D + a2 * 512
                                last = nc.tensor.matmul(down[a2 * CAP:(a2 + 1) * CAP, :], k.act[:, m % 4, m // 4, :],
                                                        w[:, c:c + 512], start=(m == 0), stop=(m == KF - 1),
                                                        skip_group_check=True)
                        last.then_inc(used, 1)
            pe.wait_ge(selT_ready, extra * pairs + pairs + 1)
            pe.wait_ge(y_ready, extra * (2 * pairs) + 2 * pairs + 1)
            scatter()

        @blk.scalar
        def _(act):
            act.dma_start(k.b_dn[:, :], a["expert_b_down"][0]).then_inc(k.bias_in, 16)
            extra = extra_rounds(act)
            act.wait_ge(gT_done, 1)
            act_copy(nc, k.gateT[0:E, :], k.ps[0:E, 7, 0:T]).then_inc(gT_ready, 1)
            act.wait_ge(g_done, 1)
            act_copy(nc, k.xrow[:, :], flat(rows)).then_inc(row_ready, 1)
            act.wait_ge(xt_done, 1)
            act_copy(nc, k.xg[:, :, :].rearrange("p k n -> p (k n)"), flat(rows)).then_inc(xg_ready, 1)
            with act.Fori(0, extra + 1) as r, act.Fori(0, pairs) as p:
                n = r * pairs + p
                for h in range(2):
                    act.wait_ge(used, n * 24 + h * 12 + 8)
                    act_copy(nc, k.hrow[:, :], flat(up)).then_inc(hrow_ready, 1)
                    act.wait_ge(glu_ready, n * 2 + h + 1)
                    nc.scalar.activation(k.sig[:, :, :, :], k.glu[:, :, :, :], ACT.Sigmoid, scale=1.702)\
                        .then_inc(sig_ready, 1)
                    if h == 1:
                        act.wait_ge(selps_done, n + 1)
                        act_copy(nc, k.selT[:, :], seT).then_inc(selT_ready, 1)
                        act.wait_ge(g_done, n + 2)
                        act_copy(nc, k.xrow[:, :], flat(rows)).then_inc(row_ready, 1)
                        act.wait_ge(xt_done, n + 2)
                        act_copy(nc, k.xg[:, :, :].rearrange("p k n -> p (k n)"), flat(rows)).then_inc(xg_ready, 1)
                    act.wait_ge(used, n * 24 + h * 12 + 12)
                    for a2 in range(2):
                        ins = act_copy(nc, k.y[h * CAP:(h + 1) * CAP, a2 * 512:(a2 + 1) * 512],
                                             down[a2 * CAP:(a2 + 1) * CAP, :])
                    ins.then_inc(y_ready, 1)

        @blk.vector
        def _(dve):
            extra = extra_rounds(dve)

            def choose(p, gated):
                for h in range(2):
                    for t in range(TT):
                        place = k.place[:, t, bass.ds(p * 2 + h, 1)]
                        g = (k.gate[:, t, bass.ds(p * 2 + h, 1)], ALU.mult) if gated else (None, ALU.bypass)
                        last = nc.vector.tensor_scalar(k.sel[:, int(gated), t, h * CAP:(h + 1) * CAP], k.slots[:, :],
                                                       place, g[0], ALU.is_equal, g[1])
                return last

            def collect(t):
                nc.vector.tensor_tensor(k.acc[:, t, :], k.acc[:, t, :], flat(scat[t]), ALU.add).then_inc(acc_done, 1)

            choose(0, False).then_inc(hot_ready, 1)
            nc.vector.memset(k.selT[:, :], 0.0).then_inc(selT_ready, 1)
            nc.vector.memset(k.y[:, :], 0.0).then_inc(y_ready, 1)
            for t, src in enumerate((up, turned)):
                dve.wait_ge(base_done, t + 1)
                nc.vector.tensor_copy(k.acc[:, t, :], flat(src)).then_inc(acc_done, 1)
            with dve.Fori(0, extra + 1) as r:
                with dve.Fori(0, pairs) as p:
                    n = r * pairs + p
                    link, end = loop_chain(dve, dchain, n * LINKS + r, LINKS)
                    for h in range(2):
                        e = p * 2 + h
                        b = k.bupT[:, :].rearrange("p (x a j e) -> p x j a e", x=2, a=2, e=E)[:, :, :, :, bass.ds(e, 1)]
                        wide = [P, 4, 2, CAP]
                        g, l = (turned[:, par, :].rearrange("p (j a s) -> p j a s", a=2, s=CAP) for par in range(2))
                        dve.wait_ge(hT_done, n * 2 + h + 1)
                        link(nc.vector.tensor_tensor(k.glu[:, :, :, :], g, b[:, 0].to_broadcast(wide), ALU.add))
                        nc.vector.tensor_scalar(k.glu[:, :, :, :], k.glu[:, :, :, :], 7.0, None, ALU.min)\
                            .then_inc(glu_ready, 1)
                        link(nc.vector.tensor_tensor(k.lin[:, :, :, :], l, b[:, 1].to_broadcast(wide), ALU.add))
                        link(nc.vector.tensor_scalar(k.lin[:, :, :, :], k.lin[:, :, :, :], 7.0, -7.0, ALU.min, ALU.max))
                        dve.wait_ge(glu_ready, n * 2 + h + 1)
                        link(nc.vector.scalar_tensor_tensor(out=k.lin[:, :, :, :], in0=k.lin[:, :, :, :], scalar=1.0,
                                                            in1=k.glu[:, :, :, :], op0=ALU.add, op1=ALU.mult))
                        dve.wait_ge(sig_ready, n * 2 + h + 1)
                        nc.vector.tensor_tensor(k.act[:, :, :, :], k.lin[:, :, :, :], k.sig[:, :, :, :], ALU.mult)\
                            .then_inc(act_ready, 1)
                        if h == 0:
                            for t in range(TT):
                                dve.wait_ge(sc_done, n * 2 + t + 1)
                                dve.wait_ge(acc_done, n * 2 + t + 1)
                                collect(t)
                            choose(p, True).then_inc(gated_ready, 1)
                            choose(p + 1, False).then_inc(hot_ready, 1)
                    end()
                nc.vector.tensor_scalar(k.slots[:, :], k.slots[:, :], float(CAP), None, ALU.add).then_inc(dchain, 1)
                dve.wait_ge(dchain, (r + 1) * (pairs * LINKS + 1))
            for t in range(TT):
                dve.wait_ge(sc_done, extra * (2 * pairs) + (2 * pairs + t + 1))
                dve.wait_ge(acc_done, extra * (2 * pairs) + (2 * pairs + t + 1))
                collect(t)


def second_in(nc, k, a):
    sem = k.sem
    x_ready = sem("x2_ready")
    var, root, rroot, xn_ready, xnT_done, hT_ready, evac = (
        k.ln_var, k.ln_root, k.rms_root, k.normed, k.turned, k.hT_ready, k.evac)
    gd, gb_done = sem("gate_diag"), sem("gate_rows")
    gb_out, flip_ready, bm_done, bm_out = (sem(n) for n in ("gate_rows_out", "flip_ready", "bias_turned", "bias_out"))
    x2, xn, hT = k.h, k.xn, k.hT2
    rs = k.small[:, 0:2]
    nav = k.proj[:, :, 0:512].rearrange("p t (g n) -> p t g n", n=64)
    kr = k.proj[:, :, 1408:1440]
    with k.ctx_block("second_in") as blk:
        @blk.sync
        def _(sp):
            load_last(k, sp, len(LATE), L_UQ + len(LATE))

        @blk.tensor
        def _(pe):
            for n in range(2):
                pe.wait_ge(gd, n + 1)
                for m in range(KD):
                    last = nc.tensor.matmul(k.flat[:, n * D + m * P:n * D + (m + 1) * P], k.ones[:, :],
                                            k.diag[:, n, m * P:(m + 1) * P], start=True, stop=True)
                last.then_inc(gb_done, 1)
            pe.wait_ge(gb_out, 1)
            pe.wait_ge(flip_ready, 1)
            pe.wait_ge(k.late_in, 16 * len(k.late_loads))
            bias = k.bm[:, :, :, :].rearrange("p t h n -> p (t h n)")
            for b in range(4):
                last = nc.tensor.matmul(k.ps[:, b, :], k.flip[:, :], bias[:, b * 512:(b + 1) * 512], start=True, stop=True)
            last.then_inc(bm_done, 1)
            transpose_tokens(nc, k, k.flat[:, 2048:4096], xn, 0, KD, lambda t: pe.wait_ge(xn_ready, t + 1))\
                .then_inc(xnT_done, 1)
            pe.wait_ge(bm_out, 1)
            pe.wait_ge(hT_ready, 4)
            for i in range(L_UQ):
                w = last_arrived(k, pe, i)
                if i >= 8:
                    pe.wait_ge(evac, N_IN + i - 7)
                n = k.last[i][2]
                out = k.ps[:, i % 8, :]
                last = token_major(nc, out, w, hT, KD, n) if i < 6 else feature_major(nc, out, w, hT, KD, 2)
                last.then_inc(k.last_used, 1)

        @blk.scalar
        def _(act):
            link = chain(k, act, "act")
            act.wait_ge(var, 2)
            nc.scalar.activation(k.root[:, :], k.mv[:, :, 1], ACT.Sqrt, bias=k.eps[:, 0:1]).then_inc(root, 1)
            act.wait_ge(gb_done, 2)
            act_copy(nc, k.gB[:, :, :].rearrange("p n d -> p (n d)"), k.flat[:, 0:2048]).then_inc(gb_out, 1)
            for t in range(TT):
                act.wait_ge(x_ready, t + 1)
                ins = nc.scalar.activation(xn[:, t, :], x2[:, t, :], ACT.Square, accum_out=k.small[:, 2 + t:3 + t])
            link(ins)
            nc.scalar.activation(k.root[:, :], k.small[:, 2:4], ACT.Sqrt, bias=k.eps[:, 1:2], scale=1.0 / D)\
                .then_inc(rroot, 1)
            act.wait_ge(bm_done, 1)
            act_copy(nc, k.bm[:, :, :, :].rearrange("p t h n -> p (t h n)"), k.flat[:, 0:2048]).then_inc(bm_out, 1)
            act.wait_ge(xnT_done, 2)
            for m in range(4, KD):
                ins = nc.scalar.activation(hT[:, m, :], k.flat[:, 2048 + m * T:2048 + (m + 1) * T], ACT.Identity,
                                           bias=k.mod[:, SHIFT1 + m:SHIFT1 + m + 1], scale=k.ada[:, m:m + 1])
            ins.then_inc(hT_ready, 1)
            for i in range(L_UQ):
                act.wait_ge(k.last_used, i + 1)
                n = k.last[i][2]
                src = k.ps[:, i % 8, :]
                if i < 6:
                    ins = act_copy(nc, k.proj[:, :, i * CH:i * CH + n],
                                         src[:, 0:TT * n].rearrange("p (t n) -> p t n", t=TT))
                else:
                    ins = act_copy(nc, k.conv[:, 2 * (i - 6):2 * (i - 5), :], src.rearrange("p (m t) -> p m t", m=2))
                ins.then_inc(evac, 1)
                if i == 2:
                    act.wait_ge(k.ang_ready, 1)
                    nc.scalar.activation(k.trig[:, :, :], k.ang[:, :, :], ACT.Sin).then_inc(k.trig_ready, 1)
                if i == 6:
                    act.wait_ge(k.sums, 2)
                    for lo, hi, width in ((0, 16, 64), (16, 18, 384), (18, 20, 256), (20, 22, 32)):
                        ins = nc.scalar.activation(k.sroot[:, lo:hi], k.ss[:, lo:hi], ACT.Sqrt, bias=k.eps[:, 1:2],
                                                   scale=1.0 / width)
                    ins.then_inc(k.roots, 1)

        @blk.gpsimd
        def _(pool):
            link = chain(k, pool, "pool")
            link(nc.gpsimd.memset(k.flip[:, :], 0.0))
            for half in range(2):
                v = k.flip[half * GW:(half + 1) * GW, half * GW:(half + 1) * GW]
                ins = nc.gpsimd.affine_select(out=v, in_=v, compare_op=ALU.not_equal, fill=1.0, base=-(GW - 1),
                                              pattern=[[1, GW]], channel_multiplier=1)
            ins.then_inc(flip_ready, 1)
            pool.wait_ge(bm_out, 1)
            for half in range(2):
                v = k.bm[half * GW:(half + 1) * GW, :, :, :].rearrange("p t h (j w) -> p (t h j) w", w=GW)
                left, right = v[:, :, 0:GW - KC], v[:, :, KC:GW]
                link(nc.gpsimd.affine_select(out=left, in_=left, compare_op=ALU.is_ge, fill=BIG, base=KC // 2,
                                             pattern=[[0, TT * NA * 4], [1, GW - KC]], channel_multiplier=-1))
                link(nc.gpsimd.affine_select(out=right, in_=right, compare_op=ALU.is_ge, fill=BIG,
                                             base=KC // 2 - 1 - KC, pattern=[[0, TT * NA * 4], [-1, GW - KC]],
                                             channel_multiplier=1))

        @blk.vector
        def _(dve):
            link = chain(k, dve, "dve")
            for n, (row, gain) in enumerate(((SCALE1, "n1"), (SCALE2, "n2"))):
                nc.vector.scalar_tensor_tensor(out=k.ada[:, n * KD:(n + 1) * KD], in0=k.mod[:, row:row + KD], scalar=1.0,
                                               in1=k.cols[:, ROWS[gain]:ROWS[gain] + KD], op0=ALU.add, op1=ALU.mult)
            link(nc.vector.scalar_tensor_tensor(out=x2[:, :, :], in0=k.h[:, :, :], scalar=ALPHA, in1=k.acc[:, :, :],
                                                op0=ALU.mult, op1=ALU.add))
            dve.wait_ge(k.late_in, 16 * len(k.late_loads))
            norm_stats(nc, k, link, x2, var)
            for n, row in enumerate((GATE1, GATE2)):
                for m in range(KD):
                    ins = nc.vector.tensor_scalar(k.diag[:, n, m * P:(m + 1) * P], k.ident[:, :],
                                                  k.mod[:, row + m:row + m + 1], None, ALU.mult)
                ins.then_inc(gd, 1)
            norm_apply(nc, k, dve, link, x2, var, 2, root, 2, k.g2[:, :], k.b2[:, :], x_ready)
            dve.wait_ge(rroot, 1)
            link(nc.vector.reciprocal(rs, k.root[:, :]))
            for t in range(TT):
                nc.vector.tensor_scalar(xn[:, t, :], x2[:, t, :], rs[:, t:t + 1], None, ALU.mult).then_inc(xn_ready, 1)
            dve.wait_ge(xnT_done, 2)
            for m in range(4):
                ins = nc.vector.tensor_scalar(hT[:, m, :], k.flat[:, 2048 + m * T:2048 + (m + 1) * T],
                                              k.ada[:, m:m + 1], k.mod[:, SHIFT1 + m:SHIFT1 + m + 1], ALU.mult, ALU.add)
            ins.then_inc(hT_ready, 1)
            link(nc.vector.tensor_copy(k.posf[:, :], k.pos[:, :]))
            for i, f in enumerate(k.inv):
                ins = nc.vector.tensor_scalar(k.ang[:, :, i], k.posf[:, :], float(f), None, ALU.mult)
            link(ins)
            sn, cs, turn = k.ang[:, :, 0:16], k.ang[:, :, 16:32], k.turn[:, :, :]
            magic, c1 = 1.5 * 2.0 ** 23, 6.28125
            c2 = float(np.float32(2 * np.pi - c1))
            link(nc.vector.tensor_scalar(turn, sn, float(1 / (2 * np.pi)), magic, ALU.mult, ALU.add))
            link(nc.vector.tensor_scalar(turn, turn, magic, None, ALU.subtract))
            link(nc.vector.scalar_tensor_tensor(out=sn, in0=turn, scalar=-c1, in1=sn, op0=ALU.mult, op1=ALU.add))
            link(nc.vector.scalar_tensor_tensor(out=sn, in0=turn, scalar=-c2, in1=sn, op0=ALU.mult, op1=ALU.add))
            link(nc.vector.tensor_scalar(turn, sn, float(np.pi / 2), float(-2 * np.pi), ALU.is_gt, ALU.mult))
            link(nc.vector.scalar_tensor_tensor(out=cs, in0=sn, scalar=float(np.pi / 2), in1=turn, op0=ALU.add,
                                                op1=ALU.add))
            lim = float(np.nextafter(np.float32(np.pi), np.float32(0)))
            nc.vector.tensor_scalar(k.ang[:, :, :], k.ang[:, :, :], lim, -lim, ALU.min, ALU.max).then_inc(k.ang_ready, 1)
            dve.wait_ge(evac, N_IN + 6)
            link(nc.vector.tensor_tensor(k.sq[:, :, 0:1440], k.proj[:, :, :], k.proj[:, :, :], ALU.mult))
            for t in range(TT):
                nc.vector.tensor_reduce(k.ss[:, t * 8:(t + 1) * 8], k.sq[:, t, 0:512].rearrange("p (g n) -> p g n", n=64),
                                        AX.X, ALU.add)
            nc.vector.tensor_reduce(k.ss[:, 16:18], k.sq[:, :, 768:1152], AX.X, ALU.add)
            nc.vector.tensor_reduce(k.ss[:, 18:20], k.sq[:, :, 1152:1408], AX.X, ALU.add)
            nc.vector.tensor_reduce(k.ss[:, 20:22], k.sq[:, :, 1408:1440], AX.X, ALU.add).then_inc(k.sums, 1)
            dve.wait_ge(k.roots, 2)
            link(nc.vector.reciprocal(k.srs[:, 0:22], k.sroot[:, 0:22]))
            for t in range(TT):
                ins = nc.vector.tensor_tensor(nav[:, t], nav[:, t], bc(k.srs[:, t * 8:(t + 1) * 8], 2, 64), ALU.mult)
            ins.then_inc(k.na_n, 1)
            nc.vector.tensor_tensor(k.proj[:, :, 768:1152], k.proj[:, :, 768:1152], bc(k.srs[:, 16:18], 2, 384), ALU.mult)
            nc.vector.tensor_tensor(k.proj[:, :, 1152:1408], k.proj[:, :, 1152:1408], bc(k.srs[:, 18:20], 2, 256), ALU.mult)\
                .then_inc(k.ck_n, 1)
            link(nc.vector.tensor_tensor(kr, kr, bc(k.srs[:, 20:22], 2, 32), ALU.mult))


def group_norm(nc, link, x, sq, ss, n):
    link(nc.vector.tensor_tensor(sq, x, x, ALU.mult))
    return nc.vector.tensor_reduce(ss, sq, AX.X, ALU.add)


def heads_in(nc, k, a):
    sem = k.sem
    na_t, ck_t, ck_ready = (sem(n) for n in ("na_turned", "lat_turned", "latT_ready"))
    q_evac, q_ready, k_ready, qt_done, cv_out, kt_done = (sem(n) for n in (
        "mla_evac", "q96_ready", "k96_ready", "q96_turned", "conv_out",
        "k96_turned"))
    cv, cv_t = sem("conv_ready"), sem("conv_turned")
    proj = k.proj
    ss, root, rs = k.ss, k.sroot, k.srs
    sq = k.sq
    qm, kv = k.qm, k.kv
    kr = proj[:, :, 1408:1440]
    with k.ctx_block("heads_in") as blk:
        @blk.sync
        def _(sp):
            load_last(k, sp, L_UQ + len(LATE), L_OUT + len(LATE))

        @blk.tensor
        def _(pe):
            pe.wait_ge(k.na_n, 1)
            transpose_tokens(nc, k, k.flat[:, 0:1024], proj[:, :, 0:512], 0, 4).then_inc(na_t, 1)
            pe.wait_ge(k.ck_n, 1)
            transpose_tokens(nc, k, k.flat[:, 1024:2304], proj[:, :, 768:1408], 0, 5).then_inc(ck_t, 1)
            pe.wait_ge(ck_ready, 1)
            pe.wait_ge(k.naT_ready, 1)
            for c in range(2):
                w = last_arrived(k, pe, L_UQ + c)
                for t in range(TT):
                    b = (5 + 2 * c + t) % 8
                    for q in range(3):
                        last = nc.tensor.matmul(k.ps[:, b, 0:384], k.ckT[:, q, t * P:(t + 1) * P], w[:, q, :],
                                                start=(q == 0), stop=(q == 2))
                last.then_inc(k.last_used, 1)
            w = last_arrived(k, pe, L_UKV)
            for t in range(TT):
                for half in range(2):
                    for q in range(2):
                        last = nc.tensor.matmul(k.ps[:, 1 + 2 * t + half, :], k.ckT[:, 3 + q, t * P:(t + 1) * P],
                                                w[:, q, half * 512:(half + 1) * 512], start=(q == 0), stop=(q == 1))
            last.then_inc(k.last_used, 1)
            pe.wait_ge(cv, 1)
            pe.wait_ge(q_evac, 3)
            for m in range(2):
                for t in range(TT):
                    last = nc.tensor.transpose(k.ps[:, 7, t * 256 + m * P:t * 256 + (m + 1) * P],
                                               k.cy[:, m, t * P:(t + 1) * P], k.ident[:, :])
            last.then_inc(cv_t, 1)
            pe.wait_ge(k_ready, 1)
            for h in range(NM):
                for t in range(TT):
                    last = nc.tensor.transpose(k.flat[0:96, h * T + t * P:h * T + (t + 1) * P],
                                               k.k96[:, t, h * 96:(h + 1) * 96], k.ident[:, :])
            last.then_inc(kt_done, 1)
            pe.wait_ge(q_ready, 1)
            pe.wait_ge(cv_out, 1)
            for h in range(NM):
                for t in range(TT):
                    last = nc.tensor.transpose(k.flat[0:96, 2048 + h * T + t * P:2048 + h * T + (t + 1) * P],
                                               qm[:, t, h * 96:(h + 1) * 96], k.ident[:, :])
            last.then_inc(qt_done, 1)

        @blk.scalar
        def _(act):
            for c in range(2):
                act.wait_ge(k.last_used, L_UQ + c + 1)
                for t in range(TT):
                    ins = act_copy(nc, qm[:, t, c * 384:(c + 1) * 384], k.ps[:, (5 + 2 * c + t) % 8, 0:384])
                ins.then_inc(q_evac, 1)
            act.wait_ge(k.last_used, L_OUT)
            act_copy(nc, kv[:, :, :].rearrange("p t n -> p (t n)"), k.flat[:, 512:512 + 2048]).then_inc(q_evac, 1)
            act.wait_ge(k.sums, 3)
            nc.scalar.activation(root[:, 0:16], ss[:, 0:16], ACT.Sqrt, bias=k.eps[:, 1:2], scale=1.0 / 64)
            nc.scalar.activation(root[:, 16:32], ss[:, 16:32], ACT.Sqrt, bias=k.eps[:, 1:2], scale=1.0 / 32)
            nc.scalar.activation(root[:, 32:48], ss[:, 32:48], ACT.Sqrt, bias=k.eps[:, 1:2], scale=1.0 / 64)\
                .then_inc(k.roots, 1)
            act.wait_ge(cv_t, 1)
            act_copy(nc, k.mixed[:, :, 768:1024], k.ps[:, 7, :].rearrange("p (t n) -> p t n", t=TT)).then_inc(cv_out, 1)
            act.wait_ge(kt_done, 1)
            nc.scalar.activation(k.k96T[0:96, :, :].rearrange("p h t -> p (h t)"), k.flat[0:96, 0:2048], ACT.Copy,
                                 scale=k.cols[0:96, ROWS["k96"]:ROWS["k96"] + 1])
            act.wait_ge(qt_done, 1)
            link = chain(k, act, "act")
            link(nc.scalar.activation(k.q96T[0:96, :, :].rearrange("p h t -> p (h t)"), k.flat[0:96, 2048:4096], ACT.Copy,
                                      scale=k.cols[0:96, ROWS["q96"]:ROWS["q96"] + 1]))

        @blk.gpsimd
        def _(pool):
            link = chain(k, pool, "pool")
            u, y = k.cu, k.cy
            nc.gpsimd.memset(u[:, :, 0:1], 0.0)
            nc.gpsimd.memset(u[:, :, T + 1:T + 2], 0.0)
            link(nc.gpsimd.tensor_tensor(u[:, :, 1:T + 1], k.conv[:, 4:6, :], k.conv[:, 0:2, :], ALU.mult))
            r = ROWS["convw"]
            for m in range(2):
                ins = nc.gpsimd.tensor_scalar(y[:, m, :], u[:, m, 1:T + 1], k.cols[:, r + 2 + m:r + 3 + m],
                                              k.cols[:, ROWS["convb"] + m:ROWS["convb"] + m + 1], ALU.mult, ALU.add)
            link(ins)
            for tap in (0, 2):
                for m in range(2):
                    ins = nc.gpsimd.tensor_scalar(k.ctmp[:, m, :], u[:, m, tap:tap + T],
                                                  k.cols[:, r + 2 * tap + m:r + 2 * tap + m + 1], None, ALU.mult)
                link(ins)
                link(nc.gpsimd.tensor_tensor(y[:, :, :], y[:, :, :], k.ctmp[:, :, :], ALU.add))
            nc.gpsimd.tensor_tensor(y[:, :, :], y[:, :, :], k.conv[:, 2:4, :], ALU.mult).then_inc(cv, 1)

        @blk.vector
        def _(dve):
            link = chain(k, dve, "dve")
            dve.wait_ge(ck_t, 1)
            for m in range(5):
                ins = nc.vector.tensor_scalar(k.ckT[:, m, :], k.flat[:, 1024 + m * T:1024 + (m + 1) * T],
                                              k.cols[:, ROWS["cqg"] + m:ROWS["cqg"] + m + 1], None, ALU.mult)
            ins.then_inc(ck_ready, 1)
            nc.vector.tensor_scalar(k.naT[:, 0:2, :], k.flat[:, 0:512].rearrange("p (m t) -> p m t", t=T),
                                    k.cols[:, ROWS["naq"]:ROWS["naq"] + 1], 0.125, ALU.mult, ALU.mult)
            nc.vector.tensor_scalar(k.naT[:, 2:4, :], k.flat[:, 512:1024].rearrange("p (m t) -> p m t", t=T),
                                    k.cols[:, ROWS["nak"]:ROWS["nak"] + 1], None, ALU.mult).then_inc(k.naT_ready, 1)
            dve.wait_ge(k.trig_ready, 1)
            sin, cos = k.trig[:, :, 0:16], k.trig[:, :, 16:32]
            ro, rt = k.rope, k.rope_t
            link(nc.vector.tensor_tensor(kr, kr, bc(k.krg[:, :], 1, TT), ALU.mult))
            nc.vector.tensor_tensor(ro[:, :, 0:16], kr[:, :, 0:16], cos, ALU.mult)
            nc.vector.tensor_tensor(rt[:, :, 0:16], kr[:, :, 16:32], sin, ALU.mult)
            nc.vector.tensor_tensor(ro[:, :, 16:32], kr[:, :, 16:32], cos, ALU.mult)
            link(nc.vector.tensor_tensor(rt[:, :, 16:32], kr[:, :, 0:16], sin, ALU.mult))
            nc.vector.tensor_tensor(ro[:, :, 0:16], ro[:, :, 0:16], rt[:, :, 0:16], ALU.subtract)
            link(nc.vector.tensor_tensor(ro[:, :, 16:32], ro[:, :, 16:32], rt[:, :, 16:32], ALU.add))
            dve.wait_ge(q_evac, 2)
            link(nc.vector.tensor_tensor(sq[:, :, 0:768], qm[:, :, :], qm[:, :, :], ALU.mult))
            for t in range(TT):
                v = sq[:, t, 0:768].rearrange("p (h n) -> p h n", n=96)
                nc.vector.tensor_reduce(ss[:, t * 8:(t + 1) * 8], v[:, :, 0:64], AX.X, ALU.add)
                ins = nc.vector.tensor_reduce(ss[:, 16 + t * 8:16 + (t + 1) * 8], v[:, :, 64:96], AX.X, ALU.add)
            dve.wait_ge(q_evac, 3)
            keys = [kv[:, t, :].rearrange("p (h n) -> p h n", n=128) for t in range(TT)]
            for t in range(TT):
                ins = nc.vector.tensor_tensor(sq[:, t, 768:1280].rearrange("p (h n) -> p h n", n=64),
                                              keys[t][:, :, 0:64], keys[t][:, :, 0:64], ALU.mult)
            link(ins)
            for t in range(TT):
                ins = nc.vector.tensor_reduce(ss[:, 32 + t * 8:32 + (t + 1) * 8],
                                              sq[:, t, 768:1280].rearrange("p (h n) -> p h n", n=64), AX.X, ALU.add)
            ins.then_inc(k.sums, 1)
            dve.wait_ge(k.roots, 3)
            link(nc.vector.reciprocal(rs[:, 0:48], root[:, 0:48]))
            for t in range(TT):
                v = qm[:, t, :].rearrange("p (h n) -> p h n", n=96)
                nc.vector.tensor_tensor(v[:, :, 0:64], v[:, :, 0:64], bc(rs[:, t * 8:(t + 1) * 8], 2, 64), ALU.mult)
                nc.vector.tensor_tensor(v[:, :, 64:96], v[:, :, 64:96], bc(rs[:, 16 + t * 8:24 + t * 8], 2, 32), ALU.mult)
                kd = k.k96[:, t, :].rearrange("p (h n) -> p h n", n=96)
                nc.vector.tensor_tensor(kd[:, :, 0:64], keys[t][:, :, 0:64], bc(rs[:, 32 + t * 8:40 + t * 8], 2, 64),
                                        ALU.mult)
                ins = nc.vector.tensor_copy(kd[:, :, 64:96], bc(ro[:, t, :], 1, NM))
            ins.then_inc(k_ready, 1)
            dve.wait_ge(k_ready, 1)
            vs = [qm[:, t, :].rearrange("p (h n) -> p h n", n=96)[:, :, 64:96] for t in range(TT)]
            for t in range(TT):
                ins = nc.vector.tensor_tensor(vs[t], vs[t], bc(k.qrg[:, :], 1, NM), ALU.mult)
            link(ins)
            for t in range(TT):
                c, s = bc(cos[:, t, :], 1, NM), bc(sin[:, t, :], 1, NM)
                x1, x2 = vs[t][:, :, 0:16], vs[t][:, :, 16:32]
                r1, r2 = (sq[:, t, n:n + 128].rearrange("p (h n) -> p h n", n=16) for n in (0, 128))
                nc.vector.tensor_tensor(r1, x2, s, ALU.mult)
                link(nc.vector.tensor_tensor(r2, x1, s, ALU.mult))
                nc.vector.tensor_tensor(x1, x1, c, ALU.mult)
                link(nc.vector.tensor_tensor(x2, x2, c, ALU.mult))
                nc.vector.tensor_tensor(x1, x1, r1, ALU.subtract)
                ins = nc.vector.tensor_tensor(x2, x2, r2, ALU.add)
                if t == 0:
                    link(ins)
            ins.then_inc(q_ready, 1)


def attention(nc, k, a):
    sem = k.sem
    s_done, m_ready, e_ready, pt_done, pt_ready, o_done, o_out = (sem(n) for n in (
        "att_scores", "att_max", "att_exp", "att_turned", "att_weights", "att_values", "att_out"))
    heads = NA + NM
    mscale = float(MLA_SCALE)
    with k.ctx_block("attention") as blk:
        @blk.tensor
        def _(pe):
            def scores(i):
                if i >= 3:
                    pe.wait_ge(e_ready, i - 2)
                for t in range(TT):
                    if i < NA:
                        r = 64 * (i % 2)
                        q, key = k.naT[r:r + 64, i // 2, :], k.naT[r:r + 64, 2 + i // 2, :]
                    else:
                        q, key = k.q96T[0:96, i - NA, :], k.k96T[0:96, i - NA, :]
                    last = nc.tensor.matmul(k.ps[:, i % 3, t * T:(t + 1) * T], q[:, t * P:(t + 1) * P], key,
                                            start=True, stop=True)
                last.then_inc(s_done, 1)

            def turn(i):
                pe.wait_ge(e_ready, i + 1)
                if i >= 2:
                    pe.wait_ge(pt_ready, i - 1)
                for s in range(TT):
                    for t in range(TT):
                        last = nc.tensor.transpose(k.ps[:, 3 + i % 2, s * T + t * P:s * T + (t + 1) * P],
                                                   k.e[:, i % 2, t, s * P:(s + 1) * P], k.ident[:, :])
                last.then_inc(pt_done, 1)

            def values(i):
                pe.wait_ge(pt_ready, i + 1)
                if i >= 2:
                    pe.wait_ge(o_out, i - 1)
                for t in range(TT):
                    for s in range(TT):
                        v = k.proj[:, s, 512 + 64 * i:576 + 64 * i] if i < NA else \
                            k.kv[:, s, (i - NA) * 128 + 64:(i - NA) * 128 + 128]
                        last = nc.tensor.matmul(k.ps[:, 5 + i % 2, t * 64:(t + 1) * 64], k.pt[:, i % 2, s, t * P:(t + 1) * P],
                                                v, start=(s == 0), stop=(s == 1))
                last.then_inc(o_done, 1)

            scores(0)
            scores(1)
            for i in range(heads):
                if i + 2 < heads:
                    scores(i + 2)
                turn(i)
                if i >= 1:
                    values(i - 1)
            values(heads - 1)

        @blk.scalar
        def _(act):
            def exps(i):
                act.wait_ge(m_ready, i + 1)
                if i >= 2:
                    act.wait_ge(pt_done, i - 1)
                for t in range(TT):
                    src = k.sB[:, i % 2, t, :] if i < NA else k.ps[:, i % 3, t * T:(t + 1) * T]
                    ins = nc.scalar.activation(k.e[:, i % 2, t, :], src, ACT.Exp, bias=k.nmax[:, i, t:t + 1],
                                               scale=1.0 if i < NA else mscale, accum_out=k.den[:, i, t:t + 1])
                ins.then_inc(e_ready, 1)

            def copy(i):
                act.wait_ge(pt_done, i + 1)
                if i >= 2:
                    act.wait_ge(o_done, i - 1)
                act_copy(nc, k.pt[:, i % 2, :, :].rearrange("p s t -> p (s t)"), k.ps[:, 3 + i % 2, :])\
                    .then_inc(pt_ready, 1)

            for i in range(heads):
                exps(i)
                if i >= 1:
                    copy(i - 1)
            copy(heads - 1)

        @blk.vector
        def _(dve):
            link = chain(k, dve, "dve")

            def maxima(i):
                dve.wait_ge(s_done, i + 1)
                src = k.ps[:, i % 3, :].rearrange("p (t n) -> p t n", t=TT)
                if i < NA:
                    if i >= 2:
                        dve.wait_ge(e_ready, i - 1)
                    link(nc.vector.tensor_tensor(k.sB[:, i % 2, :, :], src, k.bm[:, :, i, :], ALU.add))
                    src = k.sB[:, i % 2, :, :]
                link(nc.vector.tensor_reduce(k.small[:, 0:TT], src, AX.X, ALU.max))
                nc.vector.tensor_scalar(k.nmax[:, i, :], k.small[:, 0:TT], -1.0 if i < NA else -mscale, None, ALU.mult)\
                    .then_inc(m_ready, 1)

            def out(i):
                dve.wait_ge(o_done, i + 1)
                link(nc.vector.reciprocal(k.rden[:, i, :], k.den[:, i, :]))
                nc.vector.tensor_tensor(k.mixed[:, :, i * 64:(i + 1) * 64],
                                        k.ps[:, 5 + i % 2, 0:TT * 64].rearrange("p (t n) -> p t n", t=TT),
                                        bc(k.rden[:, i, :], 2, 64), ALU.mult).then_inc(o_out, 1)

            maxima(0)
            for i in range(heads):
                if i + 1 < heads:
                    maxima(i + 1)
                if i >= 1:
                    out(i - 1)
                if i == 9:
                    dve.wait_ge(o_out, 8)
                    mix_sums(nc, k, link, 12, 16)
                    mix_sums(nc, k, link, 0, 8)
            out(heads - 1)


MLA_SCALE = 96 ** -0.5


def split_matmul(nc, out, stationary, moving, start, stop):
    for n, (i, j) in enumerate(((0, 0), (0, 1), (1, 0))):
        last = nc.tensor.matmul(out, stationary[i], moving[j], start=start and n == 0, stop=stop and n == 2)
    return last


def mix_sums(nc, k, link, lo, hi):
    v, sq = (x[:, :, :].rearrange("p t (g n) -> p t g n", n=64)[:, :, lo:hi] for x in (k.mixed, k.mixsq))
    link(nc.vector.tensor_tensor(sq, v, v, ALU.mult))
    for t in range(TT):
        last = nc.vector.tensor_reduce(k.ss[:, t * 16 + lo:t * 16 + hi], sq[:, t], AX.X, ALU.add)
    return last


def output(nc, k, a, y):
    sem = k.sem
    mn, mt, mT_ready, xs = (sem(n) for n in ("mix_normed", "mix_turned", "mixT_ready", "x3_added"))
    rroot, xn_ready, xt = k.rms_root, k.normed, k.turned
    w_mask, w_high, w_low, h_mask, h_high, h_low, m_mask, m_high, m_low = (sem(n) for n in (
        "w_mask", "w_high", "w_low", "h_mask", "h_high", "h_low", "mlp_mask", "mlp_high", "mlp_low"))
    x3_sq, x3_sum, mlp_done = sem("x3_squares"), sem("x3_sum"), sem("mlp_done")
    sig, a_ready, stored, y_ready = sem("gate_sigmoid"), sem("mlp_ready"), sem("stored"), sem("y_out")
    x, xn, mixed, hT = k.h, k.xn, k.mixed, k.hraw
    g = mixed[:, :, :].rearrange("p t (g n) -> p (t g) n", n=64)
    with k.ctx_block("output") as blk:
        @blk.sync
        def _(sp):
            load_last(k, sp, L_OUT + len(LATE), N_LAST)
            for half in range(2):
                for t in range(TT):
                    sp.wait_ge(y_ready, half * 2 + t + 1)
                    sp.dma_start(y[0, t * P:(t + 1) * P, half * 512:(half + 1) * 512],
                                 xn[:, t, half * 512:(half + 1) * 512]).then_inc(stored, 16)
            sp.wait_ge(stored, 64)

        @blk.tensor
        def _(pe):
            def chunk(i):
                pe.wait_ge(w_high, i - L_OUT + 1)
                pe.wait_ge(w_low, i - L_OUT + 1)
                _, kt, n = k.last[i]
                return [v[:, 0:kt * n].rearrange("p (k n) -> p k n", k=kt) for v in (k.whi[i % 2], k.wlo[i % 2])]

            transpose_tokens(nc, k, k.flat[:, 0:2048], mixed, 0, KD, lambda t: pe.wait_ge(mn, t + 1)).then_inc(mt, 1)
            pe.wait_ge(h_high, 2)
            pe.wait_ge(h_low, 2)
            for c in range(4):
                w = chunk(L_OUT + c)
                for t in range(TT):
                    for q in range(KD):
                        last = split_matmul(nc, k.ps[:, 4 + c, t * CH:(t + 1) * CH],
                                            [v[:, q, t * P:(t + 1) * P] for v in (k.hhi, k.hlo)], [v[:, q, :] for v in w],
                                            q == 0, q == KD - 1)
                last.then_inc(k.last_used, 1)
            transpose_tokens(nc, k, k.flat[:, 0:2048], xn, 0, KD, lambda t: pe.wait_ge(xn_ready, TT + t + 1))\
                .then_inc(xt, 1)
            pe.wait_ge(h_high, 4)
            pe.wait_ge(h_low, 4)
            for c in range(F2 // CH):
                for half in range(2):
                    w = chunk(L_GU + 2 * c + half)
                    if half == 0 and c >= 2:
                        pe.wait_ge(a_ready, c - 1)
                    for j in range(2):
                        for q in range(KD):
                            last = split_matmul(nc, k.ps[:, 2 * (c % 2) + half, j * T:(j + 1) * T],
                                                [v[:, q, j * P:(j + 1) * P] for v in w], [v[:, q, :] for v in (k.hhi, k.hlo)],
                                                q == 0, q == KD - 1)
                    last.then_inc(k.last_used, 1)
            for c in range(KF2 // 2):
                w = chunk(L_DOWN + c)
                pe.wait_ge(m_high, c + 1)
                pe.wait_ge(m_low, c + 1)
                final = c == KF2 // 2 - 1
                groups = [(half, t, kk) for half in range(2) for t in range(TT) for kk in range(2)]
                if not final:
                    groups.sort(key=lambda x: x[2])
                for half, t, kk in groups:
                    last = split_matmul(nc, k.ps[:, 4 + 2 * half + t, :],
                                        [v[:, c % 2, kk, t * P:(t + 1) * P] for v in (k.mhi, k.mlo)],
                                        [v[:, kk, half * 512:(half + 1) * 512] for v in w],
                                        c == 0 and kk == 0, final and kk == 1)
                    if final and kk == 1:
                        last.then_inc(mlp_done, 1)
                if not final:
                    last.then_inc(k.last_used, 1)

        @blk.scalar
        def _(act):
            def high_w(i):
                act.wait_ge(w_mask, i - L_OUT + 1)
                act_copy(nc, k.whi[i % 2][:, :], k.wmask[:, :]).then_inc(w_high, 1)

            def high_m(c):
                act.wait_ge(m_mask, c + 1)
                act_copy(nc, k.mhi[:, c % 2], k.mmask[:, c % 2]).then_inc(m_high, 1)

            def high_h(n):
                for half in range(2):
                    s = slice(4 * half, 4 * half + 4)
                    act.wait_ge(h_mask, 2 * n + half + 1)
                    act_copy(nc, k.hhi[:, s, :], k.hmask[:, s, :]).then_inc(h_high, 1)

            act.wait_ge(k.sums, 4)
            nc.scalar.activation(k.sroot[:, 0:32], k.ss[:, 0:32], ACT.Sqrt, bias=k.eps[:, 1:2], scale=1.0 / 64)\
                .then_inc(k.roots, 1)
            high_w(L_OUT)
            act.wait_ge(mt, 1)
            for m in range(4, KD):
                ins = nc.scalar.activation(hT[:, m, :], k.flat[:, m * T:(m + 1) * T], ACT.Copy,
                                           scale=k.cols[:, ROWS["onorm"] + m:ROWS["onorm"] + m + 1])
            ins.then_inc(mT_ready, 1)
            high_h(0)
            high_w(L_OUT + 1)
            for c in range(4):
                act.wait_ge(xs, c + 1)
                s = slice(c * CH, (c + 1) * CH)
                for t in range(TT):
                    ins = nc.scalar.activation(xn[:, t, s], x[:, t, s], ACT.Square,
                                               accum_out=k.small[:, 8 + 2 * c + t:9 + 2 * c + t])
                if c < 3:
                    high_w(L_OUT + 2 + c)
            ins.then_inc(x3_sq, 1)
            act.wait_ge(x3_sum, 1)
            nc.scalar.activation(k.root[:, :], k.small[:, 2:4], ACT.Sqrt, bias=k.eps[:, 1:2], scale=1.0 / D)\
                .then_inc(rroot, 1)
            high_w(L_GU + 1)
            act.wait_ge(xt, 3)
            for m in range(4, KD):
                ins = nc.scalar.activation(hT[:, m, :], k.flat[:, m * T:(m + 1) * T], ACT.Identity,
                                           bias=k.mod[:, SHIFT2 + m:SHIFT2 + m + 1], scale=k.ada[:, KD + m:KD + m + 1])
            ins.then_inc(mT_ready, 1)
            high_h(1)
            for c in range(F2 // CH):
                high_w(L_GU + 2 * c + 2)
                act.wait_ge(k.last_used, L_GU + 2 * c + 1)
                if c >= 2:
                    act.wait_ge(a_ready, c - 1)
                nc.scalar.activation(k.sB[:, c % 2, :, :].rearrange("p t n -> p (t n)"), k.ps[:, 2 * (c % 2), :],
                                     ACT.Sigmoid).then_inc(sig, 1)
                high_w(L_GU + 2 * c + 3)
                if c in (3, 4):
                    high_m(c - 3)
            for c in range(2, KF2 // 2):
                high_w(L_DOWN + c)
                high_m(c)

        @blk.vector
        def _(dve):
            link = chain(k, dve, "dve")

            def low_w(i):
                last_arrived(k, dve, i)
                n = i - L_OUT
                if n >= 2:
                    dve.wait_ge(k.last_used, i - 1)
                if n >= 1:
                    dve.wait_ge(w_high, n)
                    dve.wait_ge(w_low, n)
                w = k.ring[:, LATE[i % len(LATE)], :]
                nc.vector.tensor_scalar(k.wmask[:, :].bitcast(I32), w.bitcast(I32), HIGH, None, ALU.bitwise_and)\
                    .then_inc(w_mask, 1)
                dve.wait_ge(w_mask, n + 1)
                nc.vector.tensor_tensor(k.wlo[i % 2][:, :], w, k.wmask[:, :], ALU.subtract).then_inc(w_low, 1)

            def low_m(c):
                dve.wait_ge(a_ready, c + 1)
                if c >= 2:
                    dve.wait_ge(k.last_used, L_DOWN + c - 1)
                    dve.wait_ge(m_high, c - 1)
                    dve.wait_ge(m_low, c - 1)
                m = k.mlp[:, 2 * c:2 * c + 2, :]
                nc.vector.tensor_scalar(k.mmask[:, c % 2].bitcast(I32), m.bitcast(I32), HIGH, None, ALU.bitwise_and)\
                    .then_inc(m_mask, 1)
                dve.wait_ge(m_mask, c + 1)
                nc.vector.tensor_tensor(k.mlo[:, c % 2], m, k.mmask[:, c % 2], ALU.subtract).then_inc(m_low, 1)

            def low_h(n, own):
                link(own)
                if n:
                    dve.wait_ge(h_high, 2 * n)
                    dve.wait_ge(h_low, 2 * n)
                for half in range(2):
                    s = slice(4 * half, 4 * half + 4)
                    if half == 1:
                        dve.wait_ge(mT_ready, n + 1)
                    nc.vector.tensor_scalar(k.hmask[:, s, :].bitcast(I32), hT[:, s, :].bitcast(I32), HIGH, None,
                                            ALU.bitwise_and).then_inc(h_mask, 1)
                    dve.wait_ge(h_mask, 2 * n + half + 1)
                    nc.vector.tensor_tensor(k.hlo[:, s, :], hT[:, s, :], k.hmask[:, s, :], ALU.subtract)\
                        .then_inc(h_low, 1)

            mix_sums(nc, k, link, 8, 12).then_inc(k.sums, 1)
            dve.wait_ge(k.roots, 4)
            link(nc.vector.reciprocal(k.srs[:, 0:32], k.sroot[:, 0:32]))
            for t in range(TT):
                v = g[:, t * 16:(t + 1) * 16, :]
                nc.vector.tensor_tensor(v, v, bc(k.srs[:, t * 16:(t + 1) * 16], 2, 64), ALU.mult).then_inc(mn, 1)
            low_w(L_OUT)
            dve.wait_ge(mt, 1)
            for m in range(4):
                ins = nc.vector.tensor_scalar(hT[:, m, :], k.flat[:, m * T:(m + 1) * T],
                                              k.cols[:, ROWS["onorm"] + m:ROWS["onorm"] + m + 1], None, ALU.mult)
            low_h(0, ins)
            low_w(L_OUT + 1)
            for c in range(4):
                dve.wait_ge(k.last_used, L_OUT + c + 1)
                s = slice(c * CH, (c + 1) * CH)
                link(nc.vector.tensor_tensor(xn[:, :, s], k.ps[:, 4 + c, :].rearrange("p (t n) -> p t n", t=TT),
                                             bc(k.gB[:, 0, s], 1, TT), ALU.mult))
                nc.vector.tensor_tensor(x[:, :, s], x[:, :, s], xn[:, :, s], ALU.add).then_inc(xs, 1)
                if c < 3:
                    low_w(L_OUT + 2 + c)
            dve.wait_ge(x3_sq, 1)
            nc.vector.tensor_reduce(k.small[:, 2:4], k.small[:, 8:16].rearrange("p (c t) -> p t c", t=TT), AX.X, ALU.add)\
                .then_inc(x3_sum, 1)
            dve.wait_ge(rroot, 2)
            link(nc.vector.reciprocal(k.small[:, 0:2], k.root[:, :]))
            for t in range(TT):
                nc.vector.tensor_scalar(xn[:, t, :], x[:, t, :], k.small[:, t:t + 1], None, ALU.mult).then_inc(xn_ready, 1)
            low_w(L_GU + 1)
            dve.wait_ge(xt, 3)
            for m in range(4):
                ins = nc.vector.tensor_scalar(hT[:, m, :], k.flat[:, m * T:(m + 1) * T], k.ada[:, KD + m:KD + m + 1],
                                              k.mod[:, SHIFT2 + m:SHIFT2 + m + 1], ALU.mult, ALU.add)
            low_h(1, ins)
            for c in range(F2 // CH):
                low_w(L_GU + 2 * c + 2)
                low_w(L_GU + 2 * c + 3)
                s = k.sB[:, c % 2, :, :].rearrange("p t n -> p (t n)")
                dve.wait_ge(sig, c + 1)
                link(nc.vector.tensor_tensor(s, s, k.ps[:, 2 * (c % 2), :], ALU.mult))
                dve.wait_ge(k.last_used, L_GU + 2 * c + 2)
                nc.vector.tensor_tensor(k.mlp[:, 2 * c:2 * c + 2, :].rearrange("p k t -> p (k t)"), s,
                                        k.ps[:, 2 * (c % 2) + 1, :], ALU.mult).then_inc(a_ready, 1)
                if c in (3, 4):
                    low_m(c - 3)
            for c in range(2, KF2 // 2):
                low_w(L_DOWN + c)
                low_m(c)
            for half in range(2):
                s = slice(half * 512, (half + 1) * 512)
                for t in range(TT):
                    dve.wait_ge(mlp_done, 2 * half + t + 1)
                    link(nc.vector.tensor_tensor(xn[:, t, s], k.ps[:, 4 + 2 * half + t, :], k.gB[:, 1, s], ALU.mult))
                    nc.vector.tensor_tensor(xn[:, t, s], xn[:, t, s], x[:, t, s], ALU.add).then_inc(y_ready, 1)


def program(nc, a, y):
    with ExitStack() as whole:
        k = Kit()
        k.sem = lambda name: whole.enter_context(nc.semaphore(name))
        k.ctx_block = lambda name: nc.Block(name=name)

        def sb(name, shape, dt=F32):
            return whole.enter_context(nc.sbuf_tensor(name, shape, dt))

        k.ps = whole.enter_context(nc.psum_tensor("ps", [P, 8, 512], F32))
        k.flat = k.ps[:, :, :].rearrange("p b n -> p (b n)")
        k.ring = sb("ring", [P, SLOTS, SLOT])
        k.ident, k.ones, k.strict, k.tri, k.later, k.same = (sb(n, [P, P]) for n in (
            "ident", "ones", "strict", "tri", "later", "same"))
        k.keep, k.nkeep = sb("keep", [P, 3 * P]), sb("nkeep", [P, 3 * P])
        k.iota_i, k.iota = sb("iota_i", [P, CAP], I32), sb("iota", [P, CAP])
        k.eps = sb("eps", [P, 2])
        k.cols = sb("cols", [P, NROWS])
        k.bupT = sb("bupT", [P, 2 * KF * E])
        k.mod, k.cact = sb("mod", [P, 48]), sb("cact", [P, KD])
        k.small = sb("small", [P, 64])
        k.h = sb("h", [P, TT, D])
        k.krg, k.qrg = sb("krg", [P, 32]), sb("qrg", [P, 32])
        k.pos = sb("pos", [P, TT], I32)
        k.stats, k.mv = sb("stats", [P, TT, 2, 6]), sb("mv", [P, TT, 2])
        k.root, k.rstd = sb("root", [P, TT]), sb("rstd", [P, TT])
        k.chosen, k.gate = (sb(n, [P, TT, E]) for n in ("chosen", "gate"))
        k.place = sb("place", [P, TT, E + 2])
        k.rounds = sb("rounds", [P, 1], I32)
        k.slots = k.iota

        k.first_in = [k.sem(f"first_in{i}") for i in range(EARLY)]
        k.first_used, k.ada_step, k.ada_copied, k.ada_summed = (k.sem(n) for n in (
            "first_used", "ada_step", "ada_copied", "ada_summed"))
        k.last_in = [k.sem(f"last_in{i}") for i in range(len(LATE))]
        k.last_used = k.sem("last_used")
        k.expert_in = [k.sem(f"expert_in{i}") for i in range(SLOTS - EARLY)] + k.first_in
        k.expert_used = k.sem("expert_used")
        k.bcast_in, k.late_in, k.bias_in, k.hg_turned, k.naT_ready = (k.sem(n) for n in (
            "bcast_in", "late_in", "bias_in", "hg_turned", "naT_ready"))
        k.evac, k.ln_var, k.ln_root, k.rms_root, k.normed, k.turned, k.hT_ready, k.sums, k.roots = (k.sem(n) for n in (
            "in_evac", "ln_var", "ln_root", "rms_root", "rms_normed", "h_turned", "hT_ready", "sums", "roots"))
        k.na_n, k.ck_n, k.ang_ready, k.trig_ready = (k.sem(n) for n in (
            "na_normed", "lat_normed", "angles", "trig"))
        k.inv = [np.float32(10000.0) ** np.float32(-i / 32) for i in range(0, 32, 2)]
        k.first, k.last = first_chunks(a), last_chunks(a)

        with ExitStack() as early:
            k.tmp = lambda name, shape, dt=F32: early.enter_context(nc.sbuf_tensor(name, shape, dt))
            k.x = k.tmp("x", [P, TT, D])
            k.xT = k.tmp("xT", [P, KD, T])
            k.rows = k.tmp("rows", [NROWS, P])
            k.sbq, k.sbk, k.osbT, k.hgs = (k.tmp(n, [P, 4, T]) for n in ("sbq", "sbk", "osbT", "hgs"))
            k.sbv, k.hgv = (k.tmp(n, [P, TT, 512]) for n in ("sbv", "hgv"))
            k.gates = k.tmp("gates", [P, 16, T])
            k.rw, k.rb = k.tmp("rw", [P, KD, E]), k.tmp("rb", [P, E])
            k.lg = k.tmp("lg", [P, TT, E])
            k.m8, k.ixf = k.tmp("m8", [P, TT, 8]), k.tmp("ixf", [P, TT, 8])
            k.ix = k.tmp("ix", [P, TT, 8], U32)
            k.gv = k.tmp("gv", [P, TT, 4])
            k.ada_acc, k.crep, k.pick = k.tmp("ada_acc", [P, 2, 2 * CH]), k.tmp("crep", [P, KD, 32]), k.tmp("pick", [P, E])
            k.rtmp = k.tmp("rtmp", [P, 2, TT, E])
            k.b_up = k.h[0:E, :, :].rearrange("p t n -> p (t n)")

            def rows_of(name, ap, extra=0):
                r = ROWS[name] + extra
                return (k.rows[r:r + ap.shape[0], 0:ap.shape[1]], ap)

            def as_rows(ap):
                return ap.rearrange("(r p) -> r p", p=P)

            k.row_loads = [
                rows_of("lb", as_rows(a["hgrn_lb_logits"][0])), rows_of("lb", as_rows(a["hgrn_lb_logits"][1]), 4),
                rows_of("hnorm", as_rows(a["hgrn_norm_g"][0])),
                rows_of("convw", a["conv_w_2"][0].rearrange("k (c p) -> (k c) p", p=P)),
                rows_of("convb", as_rows(a["conv_b_2"][0])), rows_of("onorm", as_rows(a["out_norm_g_2"][0])),
                rows_of("n1", as_rows(a["norm1_g_2"][0])), rows_of("n2", as_rows(a["norm2_g_2"][0])),
                rows_of("bada", as_rows(a["b_ada_2"][0])), rows_of("cqg", as_rows(a["mla_q_a_g_2"][0])),
                rows_of("ckvg", as_rows(a["mla_kv_a_g_2"][0])), rows_of("c", as_rows(a["c_2"][0])),
                rows_of("q96", a["mla_qn_g_2"]), rows_of("k96", a["mla_kn_g_2"]),
            ]
            for name, src in (("naq", a["na_q_g_2"]), ("nak", a["na_k_g_2"])):
                r = ROWS[name]
                k.row_loads += [(k.rows[r:r + 1, 0:64], src), (k.rows[r:r + 1, 64:128], src)]
            k.n_rows = len(k.row_loads)
            k.broadcasts = [(k.rw[:, :, :], a["router_w"][0].rearrange("(k p) e -> p k e", p=P)),
                            (k.rb[:, :], a["router_b"][0:1, :].to_broadcast([P, E])),
                            (k.krg[:, :], a["mla_kr_g_2"][0:1, :].to_broadcast([P, 32])),
                            (k.qrg[:, :], a["mla_qr_g_2"][0:1, :].to_broadcast([P, 32])),
                            ] + [(k.pos[:, t:t + 1], a["positions_2"][0, t * P:(t + 1) * P].rearrange("(p o) -> p o", o=1))
                                 for t in range(TT)]
            projections(nc, k, a)
            k.hgT = k.fbuf
            k.g1, k.b1 = (v[:, :, :].rearrange("p h t -> p (h t)") for v in (k.kk, k.hq))
            mixers(nc, k, a)
            branches(nc, k, a)
        with ExitStack() as late:
            def lt(name, shape, dt=F32):
                return late.enter_context(nc.sbuf_tensor(name, shape, dt))

            k.gB, k.ada, k.xn = lt("gB", [P, 2, D]), lt("ada", [P, 2 * KD]), lt("xn", [P, TT, D])
            k.ss, k.sroot, k.srs = (lt(n, [P, 48]) for n in ("ss", "sroot", "srs"))
            for_heads = late.enter_context(ExitStack())

            def ht(name, shape, dt=F32):
                return for_heads.enter_context(nc.sbuf_tensor(name, shape, dt))

            k.acc = ht("acc", [P, TT, D])
            k.g2, k.b2, k.bm = ht("g2", [P, D]), ht("b2", [P, D]), ht("bm", [P, TT, NA, T])
            k.late_loads = [(k.g2[:, :], a["ln2_g"][0:1, :].to_broadcast([P, D])),
                            (k.b2[:, :], a["ln2_b"][0:1, :].to_broadcast([P, D]))]
            rpb = a["na_rpb_2"]
            for t in range(TT):
                for half in range(2):
                    for h in range(NA):
                        r = 2 * t + half
                        off = (h * 15 + 7 - r) * 31 + 15 - (GW - 1)
                        src = bass.AP(rpb.tensor, off, [[1, GW], [31, 4], [1, GW]])
                        k.late_loads.append((k.bm[half * GW:(half + 1) * GW, t, h, :].rearrange("p (j w) -> p j w", j=4), src))
            with ExitStack() as middle:
                def md(name, shape):
                    return middle.enter_context(nc.sbuf_tensor(name, shape, F32))

                k.sel, k.selT = md("sel", [P, 2, TT, 2 * CAP]), md("selT", [P, T])
                k.xg, k.y = md("xg", [P, KD, 2 * CAP]), md("y", [P, D])
                k.xrow, k.hrow = md("xrow", [P, D]), md("hrow", [P, D])
                k.gateT, k.b_dn = md("gateT", [E, T]), md("b_dn", [E, D])
                k.glu, k.lin, k.sig, k.act = (md(n, [P, 4, 2, CAP]) for n in ("glu", "lin", "sigm", "act"))
                experts(nc, k, a)
            k.hT2, k.proj, k.conv = ht("hT2", [P, KD, T]), ht("proj", [P, TT, 1440]), ht("conv", [P, 6, T])
            k.flip = ht("flip", [P, P])
            k.naT, k.k96T = ht("naT", [P, 4, T]), ht("k96T", [P, NM, T])
            k.cu, k.cy, k.ctmp = ht("cu", [P, 2, T + 2]), ht("cy", [P, 2, T]), ht("ctmp", [P, 2, T])
            k.posf, k.ang, k.trig, k.turn = (ht(n, [P, TT] + s) for n, s in (
                ("posf", []), ("ang", [32]), ("trig", [32]), ("turn", [16])))
            k.rope, k.rope_t = ht("rope", [P, TT, 32]), ht("rope_t", [P, TT, 32])
            k.nmax, k.den, k.rden = (ht(n, [P, NA + NM, TT]) for n in ("nmax", "den", "rden"))
            free = k.ring[:, 0:4, :].rearrange("p s n -> p (s n)")

            def view(at, n, t=None):
                v = free[:, at:at + n]
                return v if t is None else v.rearrange("p (t n) -> p t n", t=t)

            k.diag, k.sq = view(0, 2 * D, 2), view(4352, 2880, TT)
            second_in(nc, k, a)
            k.kv, k.mixed, k.q96T = k.acc, k.xn, k.hT2
            k.ckT, k.qm, k.k96 = view(0, 1280, 5), view(1280, 1536, TT), view(2816, 1536, TT)
            heads_in(nc, k, a)
            k.sB, k.e, k.pt = (view(n * 1024, 1024).rearrange("p (b t n) -> p b t n", b=2, t=TT) for n in range(3))
            k.mixsq = view(4096, 2 * D, TT)
            attention(nc, k, a)
            for_heads.close()
            k.mlp = view(1024, KF2 * T, KF2)
            k.hraw, k.hmask = view(1024, KD * T, KD), view(1024 + KD * T, KD * T, KD)
            k.whi, k.wlo = ([lt(f"{n}{b}", [P, SLOT], R32) for b in range(2)] for n in ("w_hi", "w_lo"))
            k.hhi, k.hlo = (lt(n, [P, KD, T], R32) for n in ("h_hi", "h_lo"))
            k.mhi, k.mlo = (lt(n, [P, 2, 2, T], R32) for n in ("mlp_hi", "mlp_lo"))
            k.wmask, k.mmask = lt("w_masked", [P, SLOT]), lt("mlp_masked", [P, 2, 2, T])
            output(nc, k, a, y)


def kernel(**inputs):
    import concourse.bacc as bacc
    from concourse.bass_utils import run_bass_kernel_spmd

    nc = bacc.Bacc("TRN2", target_bir_lowering=False, num_devices=1)
    arrays, aps = {}, {}
    for name, value in inputs.items():
        v = np.ascontiguousarray(value)
        arrays[f"in_{name}"] = v
        aps[name] = nc.dram_tensor(f"in_{name}", v.shape, mybir.dt.from_np(v.dtype), kind="ExternalInput").ap()
    y = nc.dram_tensor("out_y", (1, T, D), F32, kind="ExternalOutput").ap()
    program(nc, aps, y)
    return run_bass_kernel_spmd(nc, [arrays], core_ids=[0]).results[0]["out_y"]
```
